# Optimizing a Trainium2 kernel written in Bass

```python
import math
import jax, jax.numpy as jnp
from jax import lax
import numpy as np

D_MODEL = 1024
BATCH = 1
SEQ = 1024
DEPTH = 1

ROPE_THETA = 10000.0
NORM_EPS = 1e-6
Q_BLOCK = 128

DIFF_HEADS = 4
DIFF_HEAD_DIM = 64
DIFF_V_DIM = 2 * DIFF_HEAD_DIM
DIFF_WIDTH = DIFF_HEADS * DIFF_V_DIM
DIFF_QK_COLS = DIFF_HEADS * 2 * DIFF_HEAD_DIM

MLA_HEADS = 4
MLA_NOPE = 128
MLA_ROPE = 64
MLA_V = 128
MLA_Q_RANK = 384
MLA_KV_RANK = 256
MLA_WIDTH = MLA_HEADS * MLA_V

SPLIT_SIZES = (DIFF_QK_COLS, DIFF_QK_COLS, DIFF_WIDTH, DIFF_WIDTH,
               MLA_Q_RANK, MLA_KV_RANK, MLA_ROPE, MLA_WIDTH,
               D_MODEL, D_MODEL)
IN_COLS = sum(SPLIT_SIZES)


def rms_norm(x, gain):
    xf = x.astype(jnp.float32)
    y = xf * lax.rsqrt(jnp.mean(xf * xf, axis=-1, keepdims=True) + NORM_EPS)
    return (y * gain.astype(jnp.float32)).astype(x.dtype)

def rope_tables(positions, dim):
    inv_freq = ROPE_THETA ** (-jnp.arange(0, dim, 2, dtype=jnp.float32) / dim)
    ang = positions.astype(jnp.float32)[..., None] * inv_freq
    return jnp.cos(ang), jnp.sin(ang)

def apply_rope(x, cos, sin):
    b, s, half = cos.shape
    shape = (b,) + (1,) * (x.ndim - 3) + (s, half)
    c = cos.reshape(shape).astype(x.dtype)
    sn = sin.reshape(shape).astype(x.dtype)
    x1, x2 = x[..., :half], x[..., half:]
    return jnp.concatenate([x1 * c - x2 * sn, x2 * c + x1 * sn], axis=-1)

def causal_multimap_attention(q, k, v, map_weights, scale):
    b, h, m, s, dk = q.shape
    dv = v.shape[-1]
    nb = s // Q_BLOCK
    qb = jnp.moveaxis(q.reshape(b, h, m, nb, Q_BLOCK, dk), 3, 0)
    kpos = jnp.arange(s)
    w = map_weights.astype(jnp.float32)

    def one_block(args):
        q_blk, i = args
        qpos = i * Q_BLOCK + jnp.arange(Q_BLOCK)
        sc = jnp.einsum('bhmqd,bhmkd->bhmqk', q_blk, k).astype(jnp.float32) * scale
        sc = jnp.where(kpos[None, :] <= qpos[:, None], sc, -jnp.inf)
        p = jax.nn.softmax(sc, axis=-1)
        p = jnp.einsum('m,bhmqk->bhqk', w, p)
        return jnp.einsum('bhqk,bhkd->bhqd', p.astype(v.dtype), v)

    out = lax.map(one_block, (qb, jnp.arange(nb)))
    return jnp.moveaxis(out, 0, 2).reshape(b, h, s, dv)

def first_inputs(seed: int = 0) -> dict:
    key = jax.random.key(seed)
    ks = jax.random.split(key, 20)
    L = DEPTH
    nrm = lambda k, shape, fan: jax.random.normal(k, shape, jnp.float32) * fan ** -0.5
    gain = lambda k, n: 1.0 + 0.05 * jax.random.normal(k, (L, n), jnp.float32)
    x = jax.random.normal(ks[0], (BATCH, SEQ, D_MODEL), jnp.float32)
    positions = jnp.broadcast_to(jnp.arange(SEQ, dtype=jnp.int32), (BATCH, SEQ))
    return {
        "x": x,
        "positions": positions,
        "norm_in": gain(ks[1], D_MODEL),
        "w_in": nrm(ks[2], (L, D_MODEL, IN_COLS), D_MODEL),
        "diff_lambda_q1": 0.1 * jax.random.normal(ks[3], (L, DIFF_HEAD_DIM), jnp.float32),
        "diff_lambda_k1": 0.1 * jax.random.normal(ks[4], (L, DIFF_HEAD_DIM), jnp.float32),
        "diff_lambda_q2": 0.1 * jax.random.normal(ks[5], (L, DIFF_HEAD_DIM), jnp.float32),
        "diff_lambda_k2": 0.1 * jax.random.normal(ks[6], (L, DIFF_HEAD_DIM), jnp.float32),
        "diff_subln": gain(ks[7], DIFF_V_DIM),
        "mla_q_norm": gain(ks[8], MLA_Q_RANK),
        "w_uq": nrm(ks[9], (L, MLA_Q_RANK, MLA_HEADS * (MLA_NOPE + MLA_ROPE)), MLA_Q_RANK),
        "mla_kv_norm": gain(ks[10], MLA_KV_RANK),
        "w_ukv": nrm(ks[11], (L, MLA_KV_RANK, MLA_HEADS * (MLA_NOPE + MLA_V)), MLA_KV_RANK),
        "w_proj_diff": nrm(ks[12], (L, DIFF_WIDTH, D_MODEL), DIFF_WIDTH),
        "w_proj_mla": nrm(ks[13], (L, MLA_WIDTH, D_MODEL), MLA_WIDTH),
        "w_out": nrm(ks[14], (L, D_MODEL, D_MODEL), D_MODEL),
        "norm_final": 1.0 + 0.05 * jax.random.normal(ks[15], (D_MODEL,), jnp.float32),
    }

def first_block(x, positions, norm_in, w_in, diff_lambda_q1, diff_lambda_k1,
              diff_lambda_q2, diff_lambda_k2, diff_subln, mla_q_norm, w_uq,
              mla_kv_norm, w_ukv, w_proj_diff, w_proj_mla, w_out, norm_final):
    b, s, _ = x.shape
    cos_d, sin_d = rope_tables(positions, DIFF_HEAD_DIM)
    cos_m, sin_m = rope_tables(positions, MLA_ROPE)
    split_idx = list(np.cumsum(SPLIT_SIZES)[:-1])

    for layer in range(DEPTH):
        lambda_init = 0.8 - 0.6 * math.exp(-0.3 * layer)
        h = rms_norm(x, norm_in[layer])
        proj = h @ w_in[layer]
        (dq, dk, dv, dgate, cq, ckv, kr, mgate, g_diff, g_mla) = jnp.split(proj, split_idx, axis=-1)

        dq = dq.reshape(b, s, DIFF_HEADS, 2, DIFF_HEAD_DIM).transpose(0, 2, 3, 1, 4)
        dk = dk.reshape(b, s, DIFF_HEADS, 2, DIFF_HEAD_DIM).transpose(0, 2, 3, 1, 4)
        dv = dv.reshape(b, s, DIFF_HEADS, DIFF_V_DIM).transpose(0, 2, 1, 3)
        dq = apply_rope(dq, cos_d, sin_d)
        dk = apply_rope(dk, cos_d, sin_d)
        lam = (jnp.exp(jnp.sum(diff_lambda_q1[layer] * diff_lambda_k1[layer]))
               - jnp.exp(jnp.sum(diff_lambda_q2[layer] * diff_lambda_k2[layer]))
               + lambda_init)
        weights = jnp.stack([jnp.ones_like(lam), -lam])
        o_diff = causal_multimap_attention(dq, dk, dv, weights, DIFF_HEAD_DIM ** -0.5)
        o_diff = rms_norm(o_diff, diff_subln[layer]) * (1.0 - lambda_init)
        o_diff = o_diff.transpose(0, 2, 1, 3).reshape(b, s, DIFF_WIDTH)
        o_diff = o_diff * jax.nn.silu(dgate)

        cq = rms_norm(cq, mla_q_norm[layer])
        q = (cq @ w_uq[layer]).reshape(b, s, MLA_HEADS, MLA_NOPE + MLA_ROPE).transpose(0, 2, 1, 3)
        q_nope, q_rope = q[..., :MLA_NOPE], apply_rope(q[..., MLA_NOPE:], cos_m, sin_m)
        ckv = rms_norm(ckv, mla_kv_norm[layer])
        kv = (ckv @ w_ukv[layer]).reshape(b, s, MLA_HEADS, MLA_NOPE + MLA_V).transpose(0, 2, 1, 3)
        k_nope, mv = kv[..., :MLA_NOPE], kv[..., MLA_NOPE:]
        k_rope = apply_rope(kr[:, None], cos_m, sin_m)
        mq = jnp.concatenate([q_nope, q_rope], axis=-1)[:, :, None]
        mk = jnp.concatenate([k_nope, jnp.broadcast_to(k_rope, k_nope.shape[:-1] + (MLA_ROPE,))], axis=-1)[:, :, None]
        o_mla = causal_multimap_attention(mq, mk, mv, jnp.ones((1,), jnp.float32),
                                          (MLA_NOPE + MLA_ROPE) ** -0.5)
        o_mla = o_mla.transpose(0, 2, 1, 3).reshape(b, s, MLA_WIDTH)
        o_mla = o_mla * jax.nn.silu(mgate)

        merged = (jax.nn.sigmoid(g_diff) * (o_diff @ w_proj_diff[layer])
                  + jax.nn.sigmoid(g_mla) * (o_mla @ w_proj_mla[layer]))
        x = x + merged @ w_out[layer]

    return rms_norm(x, norm_final)


HEAD_DIM = 64
D_ATTN = D_MODEL // 2
D_RWKV = D_MODEL - D_ATTN
D_MIX = D_ATTN + D_RWKV
N_ATTN_HEADS = D_ATTN // HEAD_DIM
N_RWKV_HEADS = D_RWKV // HEAD_DIM
DILATED_BRANCHES = ((128, 1), (512, 4), (2048, 16))
LORA_DECAY = 32
LORA_AAA = 32
LORA_MV = 32
LORA_GATE = 96
D_FF = 4 * D_MODEL
GN_EPS = 64e-5
N_SHIFT = 3 * D_RWKV + LORA_DECAY + LORA_AAA + LORA_GATE
N_COLS_FIRST = 3 * D_ATTN + N_SHIFT
N_COLS_REST = N_COLS_FIRST + LORA_MV


def _rms_norm(x, g):
    xf = x.astype(jnp.float32)
    y = xf * lax.rsqrt(jnp.mean(xf * xf, axis=-1, keepdims=True) + NORM_EPS)
    return (y * g.astype(jnp.float32)).astype(x.dtype)

def _token_shift(z, mu):
    prev = jnp.pad(z, ((0, 0), (1, 0), (0, 0)))[:, :-1]
    return z + (prev - z) * mu

def _dilated_branch(q, k, v, window, dilation):
    B, S, H, Dh = q.shape
    L = S // dilation
    K = window // dilation
    qb = math.gcd(L, Q_BLOCK)
    nb = L // qb

    def phase(t):
        return t.reshape(B, L, dilation, H, Dh).transpose(0, 2, 3, 1, 4)

    qs, ks, vs = phase(q), phase(k), phase(v)
    pad = ((0, 0), (0, 0), (0, 0), (K, 0), (0, 0))
    kp, vp = jnp.pad(ks, pad), jnp.pad(vs, pad)
    idx = jnp.arange(nb)[:, None] * qb + jnp.arange(qb + K)[None, :]
    kb = kp[:, :, :, idx, :]
    vb = vp[:, :, :, idx, :]
    qblk = qs.reshape(B, dilation, H, nb, qb, Dh)
    s = jnp.einsum('bdhnqc,bdhnkc->bdhnqk', qblk, kb) * (1.0 / math.sqrt(Dh))
    j = jnp.arange(qb)[:, None]
    m_idx = jnp.arange(qb + K)[None, :]
    dist = j + K - m_idx
    blk = jnp.arange(nb)[:, None, None]
    valid = (dist >= 0) & (dist <= K) & (blk * qb + m_idx - K >= 0)
    s = jnp.where(valid, s, -jnp.inf)
    m = jnp.max(s, axis=-1)
    p = jnp.exp(s - m[..., None])
    l = jnp.sum(p, axis=-1)
    acc = jnp.einsum('bdhnqk,bdhnkc->bdhnqc', p, vb)
    acc = acc.reshape(B, dilation, H, L, Dh).transpose(0, 3, 1, 2, 4).reshape(B, S, H, Dh)
    m = m.reshape(B, dilation, H, L).transpose(0, 3, 1, 2).reshape(B, S, H)
    l = l.reshape(B, dilation, H, L).transpose(0, 3, 1, 2).reshape(B, S, H)
    return m, l, acc

def _dilated_attention(q, k, v):
    B, S, _ = q.shape
    heads = lambda t: t.astype(jnp.float32).reshape(B, S, N_ATTN_HEADS, HEAD_DIM)
    qh, kh, vh = heads(q), heads(k), heads(v)
    outs = [_dilated_branch(qh, kh, vh, w, d) for (w, d) in DILATED_BRANCHES]
    m_all = jnp.maximum(jnp.maximum(outs[0][0], outs[1][0]), outs[2][0])
    num = sum(jnp.exp(m - m_all)[..., None] * acc for (m, l, acc) in outs)
    den = sum(jnp.exp(m - m_all) * l for (m, l, acc) in outs)
    o = num / den[..., None]
    return o.reshape(B, S, D_ATTN).astype(q.dtype)

def _rwkv7_scan(r, w, k, v, kk, b):
    B, S, H, N = r.shape

    def step(state, inp):
        r_t, w_t, k_t, v_t, kk_t, b_t = inp
        sa = jnp.einsum('bhij,bhj->bhi', state, kk_t)
        state = (state * w_t[:, :, None, :]
                 - sa[..., None] * b_t[:, :, None, :]
                 + v_t[..., None] * k_t[:, :, None, :])
        y = jnp.einsum('bhij,bhj->bhi', state, r_t)
        return state, y

    xs = tuple(jnp.moveaxis(t, 1, 0) for t in (r, w, k, v, kk, b))
    state0 = jnp.zeros((B, H, N, N), jnp.float32)
    _, ys = lax.scan(step, state0, xs)
    return jnp.moveaxis(ys, 0, 1)

def _rwkv7(r, k, v, xw, xa, xg, w0, w_up, a0, a_up, g_up, k_k, k_a, r_k, gn_w, gn_b):
    B, S, _ = r.shape
    H, N = N_RWKV_HEADS, HEAD_DIM
    f32 = jnp.float32
    heads = lambda t: t.astype(f32).reshape(B, S, H, N)
    logw = -jax.nn.softplus(-(w0 + jnp.tanh(xw) @ w_up).astype(f32)) - 0.5
    decay = jnp.exp(-jnp.exp(logw))
    a = jax.nn.sigmoid((a0 + xa @ a_up).astype(f32))
    g = (jax.nn.sigmoid(xg) @ g_up).astype(f32)
    kk = heads(k * k_k)
    kk = kk / jnp.maximum(jnp.sqrt(jnp.sum(kk * kk, axis=-1, keepdims=True)), 1e-12)
    k_mod = k.astype(f32) * (1.0 + (a - 1.0) * k_a.astype(f32))
    rh, kh, vh, ah, wh = heads(r), heads(k_mod), heads(v), heads(a), heads(decay)
    y = _rwkv7_scan(rh, wh, kh, vh, kk, kk * ah)
    mean = jnp.mean(y, axis=-1, keepdims=True)
    var = jnp.mean(jnp.square(y - mean), axis=-1, keepdims=True)
    yn = ((y - mean) * lax.rsqrt(var + GN_EPS)).reshape(B, S, D_RWKV)
    yn = yn * gn_w.astype(f32) + gn_b.astype(f32)
    bonus = jnp.sum(rh * kh * r_k.astype(f32), axis=-1, keepdims=True) * vh
    out = (yn + bonus.reshape(B, S, D_RWKV)) * g
    return out.astype(r.dtype)

def second_inputs(seed: int = 0) -> dict:
    key = jax.random.key(seed)
    ks = iter(jax.random.split(key, 40))
    f32 = jnp.float32
    nrm = lambda shape, scale: jax.random.normal(next(ks), shape, f32) * scale
    gain = lambda shape: 1.0 + nrm(shape, 0.05)
    L1 = DEPTH - 1
    return {
        "x": nrm((BATCH, SEQ, D_MODEL), 1.0),
        "norm_mix_pre": gain((DEPTH, D_MODEL)),
        "norm_mix_post": gain((DEPTH, D_MODEL)),
        "norm_ffn_pre": gain((DEPTH, D_MODEL)),
        "norm_ffn_post": gain((DEPTH, D_MODEL)),
        "w_in_first": nrm((D_MODEL, N_COLS_FIRST), D_MODEL ** -0.5),
        "w_in_rest": nrm((L1, D_MODEL, N_COLS_REST), D_MODEL ** -0.5),
        "mu_shift": jax.random.uniform(next(ks), (DEPTH, N_SHIFT), f32),
        "mu_shift_mv": jax.random.uniform(next(ks), (L1, LORA_MV), f32),
        "attn_out_gain": gain((DEPTH, D_ATTN)),
        "decay_w0": jax.random.uniform(next(ks), (DEPTH, D_RWKV), f32, -5.0, 0.0),
        "decay_up": nrm((DEPTH, LORA_DECAY, D_RWKV), 0.5 * LORA_DECAY ** -0.5),
        "aaa_a0": nrm((DEPTH, D_RWKV), 0.1),
        "aaa_up": nrm((DEPTH, LORA_AAA, D_RWKV), 0.5 * LORA_AAA ** -0.5),
        "mv_v0": nrm((L1, D_RWKV), 0.5),
        "mv_up": nrm((L1, LORA_MV, D_RWKV), 0.5 * LORA_MV ** -0.5),
        "gate_up": nrm((DEPTH, LORA_GATE, D_RWKV), LORA_GATE ** -0.5),
        "k_k": 0.85 + nrm((DEPTH, D_RWKV), 0.1),
        "k_a": 1.0 + nrm((DEPTH, D_RWKV), 0.1),
        "r_k": nrm((DEPTH, N_RWKV_HEADS, HEAD_DIM), 0.1),
        "gn_w": gain((DEPTH, D_RWKV)),
        "gn_b": nrm((DEPTH, D_RWKV), 0.02),
        "w_out": nrm((DEPTH, D_MIX, D_MODEL), D_MIX ** -0.5),
        "w_ffn_up": nrm((DEPTH, D_MODEL, D_FF), D_MODEL ** -0.5),
        "w_ffn_down": nrm((DEPTH, D_FF, D_MODEL), D_FF ** -0.5),
    }

def second_block(x, norm_mix_pre, norm_mix_post, norm_ffn_pre, norm_ffn_post,
              w_in_first, w_in_rest, mu_shift, mu_shift_mv, attn_out_gain,
              decay_w0, decay_up, aaa_a0, aaa_up, mv_v0, mv_up, gate_up,
              k_k, k_a, r_k, gn_w, gn_b, w_out, w_ffn_up, w_ffn_down):
    v_first = None
    o0, o1, o2 = 3 * D_RWKV, 3 * D_RWKV + LORA_DECAY, 3 * D_RWKV + LORA_DECAY + LORA_AAA
    for i in range(DEPTH):
        h = _rms_norm(x, norm_mix_pre[i])
        z = h @ (w_in_first if i == 0 else w_in_rest[i - 1])
        q = z[..., 0:D_ATTN]
        k = z[..., D_ATTN:2 * D_ATTN]
        v = z[..., 2 * D_ATTN:3 * D_ATTN]
        zs = _token_shift(z[..., 3 * D_ATTN:3 * D_ATTN + N_SHIFT], mu_shift[i])
        r_r = zs[..., 0:D_RWKV]
        k_r = zs[..., D_RWKV:2 * D_RWKV]
        v_r = zs[..., 2 * D_RWKV:3 * D_RWKV]
        xw = zs[..., o0:o1]
        xa = zs[..., o1:o2]
        xg = zs[..., o2:N_SHIFT]
        if i == 0:
            v_first = v_r
        else:
            xmv = _token_shift(z[..., N_COLS_FIRST:], mu_shift_mv[i - 1])
            vgate = jax.nn.sigmoid(mv_v0[i - 1] + xmv @ mv_up[i - 1])
            v_r = v_r + (v_first - v_r) * vgate
        attn = _rms_norm(_dilated_attention(q, k, v), attn_out_gain[i])
        rw = _rwkv7(r_r, k_r, v_r, xw, xa, xg, decay_w0[i], decay_up[i], aaa_a0[i],
                    aaa_up[i], gate_up[i], k_k[i], k_a[i], r_k[i], gn_w[i], gn_b[i])
        mixed = jnp.concatenate([attn, rw], axis=-1) @ w_out[i]
        x = x + _rms_norm(mixed, norm_mix_post[i])
        h = _rms_norm(x, norm_ffn_pre[i])
        f = jnp.square(jax.nn.relu(h @ w_ffn_up[i])) @ w_ffn_down[i]
        x = x + _rms_norm(f, norm_ffn_post[i])
    return x


def setup_inputs(seed=0):
    out = dict(first_inputs(seed))
    for name, value in second_inputs(seed + 1).items():
        if name != "x":
            out[name + "_2"] = value
    return out


def reference(
    x, positions, norm_in, w_in, diff_lambda_q1, diff_lambda_k1, diff_lambda_q2, diff_lambda_k2,
    diff_subln, mla_q_norm, w_uq, mla_kv_norm, w_ukv, w_proj_diff, w_proj_mla, w_out,
    norm_final, norm_mix_pre_2, norm_mix_post_2, norm_ffn_pre_2, norm_ffn_post_2, w_in_first_2,
    w_in_rest_2, mu_shift_2, mu_shift_mv_2, attn_out_gain_2, decay_w0_2, decay_up_2, aaa_a0_2,
    aaa_up_2, mv_v0_2, mv_up_2, gate_up_2, k_k_2, k_a_2, r_k_2, gn_w_2, gn_b_2, w_out_2,
    w_ffn_up_2, w_ffn_down_2,
):
    x = first_block(
        x, positions, norm_in, w_in, diff_lambda_q1, diff_lambda_k1, diff_lambda_q2,
        diff_lambda_k2, diff_subln, mla_q_norm, w_uq, mla_kv_norm, w_ukv, w_proj_diff,
        w_proj_mla, w_out, norm_final,
    )
    return second_block(
        x, norm_mix_pre_2, norm_mix_post_2, norm_ffn_pre_2, norm_ffn_post_2, w_in_first_2,
        w_in_rest_2, mu_shift_2, mu_shift_mv_2, attn_out_gain_2, decay_w0_2, decay_up_2,
        aaa_a0_2, aaa_up_2, mv_v0_2, mv_up_2, gate_up_2, k_k_2, k_a_2, r_k_2, gn_w_2, gn_b_2,
        w_out_2, w_ffn_up_2, w_ffn_down_2,
    )


_drawn_inputs = setup_inputs


def setup_inputs(seed=0):
    import zlib

    import numpy as np

    out = dict(_drawn_inputs(seed))
    spreads = {}
    factors = {'diff_lambda_q1': 5.049,
     'diff_lambda_k1': 3.657,
     'diff_lambda_q2': 8.0,
     'mla_q_norm': 8.0,
     'mla_kv_norm': 8.0,
     'decay_up_2': 5.228,
     'aaa_a0_2': 3.783,
     'gn_w_2': 3.47,
     'gn_b_2': 8.0}
    for name, (base, spread) in spreads.items():
        noise = np.random.default_rng([zlib.crc32(name.encode()), seed]).standard_normal(out[name].shape)
        drawn = base * np.exp(spread * noise) if base else spread * noise
        out[name] = __import__('jax').numpy.asarray(drawn.astype(out[name].dtype))
    for name, factor in factors.items():
        out[name] = (out[name] * factor).astype(out[name].dtype)
    return out
```

```python
import concourse.bass as bass
from concourse import mybir
from concourse.alu_op_type import AluOpType as ALU
from contextlib import ExitStack
import math
import numpy as np

F32 = mybir.dt.float32
BF16 = mybir.dt.bfloat16
I32 = mybir.dt.int32
ACT = mybir.ActivationFunctionType
AX = mybir.AxisListType

NT = 8
S = 1024
D = 1024
NEG = -1.0e30
EPS = 1e-6
GN_EPS = 64e-5
LAMBDA_INIT = 0.2
TWO_PI = 2.0 * math.pi


class Queue:

    def __init__(self, sem):
        self.sem, self.n, self.ops, self.seen = sem, 0, [], {}

    def wait(self, *marks):
        for m in marks:
            if m is None:
                continue
            if isinstance(m, list):
                self.wait(*m)
                continue
            s, v = m
            if self.seen.get(s.name, 0) < v:
                self.seen[s.name] = v
                self.ops.append(lambda e, s=s, v=v: e.wait_ge(s, v))

    def put(self, make, wait=(), inc=True):
        self.wait(*wait)
        if not inc:
            self.ops.append(make)
            return None
        self.n += 1
        self.ops.append(lambda e: make(e).then_inc(self.sem, 1))
        return (self.sem, self.n)

    @property
    def last(self):
        return (self.sem, self.n)

    def emit(self, e):
        for op in self.ops:
            op(e)

    def tt(self, out, a, b, op, *wait):
        return self.put(lambda e: e.tensor_tensor(out, a, b, op), wait)

    def ts(self, out, a, s1, op0, s2, op1, *wait):
        if op1 is None:
            return self.put(lambda e: e.tensor_scalar(out, a, s1, None, op0), wait)
        return self.put(lambda e: e.tensor_scalar(out, a, s1, s2, op0, op1), wait)

    def stt(self, out, a, s, b, op0, op1, *wait):
        return self.put(lambda e: e.scalar_tensor_tensor(out, a, s, b, op0, op1), wait)

    def copy(self, out, a, *wait):
        return self.put(lambda e: e.tensor_copy(out, a), wait)

    def recip(self, out, a, *wait):
        return self.put(lambda e: e.reciprocal(out, a), wait)

    def red(self, out, a, op, *wait):
        return self.put(lambda e: e.tensor_reduce(out, a, AX.X, op), wait)

    def act(self, out, a, f, *wait, bias=0.0, scale=1.0, acc=None):
        if acc is None:
            return self.put(lambda e: e.activation(out, a, f, bias=bias, scale=scale), wait)
        return self.put(lambda e: e.activation(out, a, f, bias=bias, scale=scale, accum_out=acc), wait)

    def mm(self, out, l, r, start, stop, *wait, inc=False):
        return self.put(lambda e: e.matmul(out, l, r, start=start, stop=stop), wait, inc)

    def tr(self, out, a, ident, *wait, inc=False):
        return self.put(lambda e: e.transpose(out, a, ident), wait, inc)


class Dma:

    def __init__(self, q, lanes):
        self.q, self.lanes, self.k = q, lanes, [0] * len(lanes)
        self.at = 0

    def go(self, out, in_, *wait, lane=None):
        if lane is None:
            lane = self.at
            self.at = (self.at + 1) % len(self.lanes)
        s = self.lanes[lane]
        if self.k[lane]:
            self.q.wait((s, 16 * self.k[lane]))
        self.q.wait(*wait)
        self.k[lane] += 1
        self.q.ops.append(lambda e: e.dma_start(out, in_).then_inc(s, 16))
        return (s, 16 * self.k[lane])

    def all(self):
        return [(s, 16 * k) for s, k in zip(self.lanes, self.k) if k]


class Ring:

    def __init__(self, bufs):
        self.bufs, self.free, self.i = bufs, [None] * len(bufs), -1

    def next(self):
        self.i = (self.i + 1) % len(self.bufs)
        return self.i, self.bufs[self.i], self.free[self.i]


def constants():
    f = np.float32
    c = {}
    c["ident"] = np.eye(128, dtype=f)
    q = np.arange(128)
    caus = np.zeros((128, 1024), f)
    caus[:, 896:] = np.where(q[None, :] <= q[:, None], 0.0, NEG)
    c["caus"] = caus
    dist = (q[:, None] + 896) - np.arange(1024)[None, :]
    cnt = ((dist >= 0) & (dist <= 128)).astype(int)
    cnt += (dist >= 0) & (dist % 4 == 0) & (dist <= 512)
    cnt += (dist >= 0) & (dist % 16 == 0)
    c["dil"] = np.where(cnt > 0, 8.0 * np.log(np.maximum(cnt, 1)), NEG).astype(f)
    same = (q[:, None] // 64) == (q[None, :] // 64)
    lv = []
    for l in range(6):
        m = 1 << l
        t, s_ = q[:, None], q[None, :]
        lv.append(((t // (2 * m) == s_ // (2 * m)) & ((t // m) % 2 == 1) & ((s_ // m) % 2 == 0)))
    c["lvl"] = np.concatenate([x.astype(f) for x in lv], 1)
    c["lvl0t"] = lv[0].T.astype(f)
    c["slow"] = (same & (q[:, None] > q[None, :])).astype(f)
    c["supt"] = (same & (q[None, :] > q[:, None])).astype(f)
    c["incl"] = (same & (q[None, :] >= q[:, None])).astype(f)
    c["bones"] = same.astype(f)
    hs = np.zeros((128, 2), f)
    hs[:64, 0] = 1
    hs[64:, 1] = 1
    c["hsel"] = hs
    rs = np.ones((128, 1024), f)
    rs[:, ::64] = 0
    c["reset"] = rs
    inv = (10000.0 ** (-np.arange(0, 64, 2, dtype=np.float64) / 64)).astype(f)
    c["invf"] = np.broadcast_to(inv, (128, 32)).copy()
    return c


def program(nc, a, out):
    ctx = ExitStack()
    with ctx, nc.allow_non_contiguous_dma(reason="small vectors onto partitions"):
        M = ctx.enter_context(nc.sbuf_tensor("M", [128, 52096], F32))
        PS = ctx.enter_context(nc.psum_tensor("PS", [128, 4096], F32))
        Bk = [PS[:, 512 * b:512 * b + 512] for b in range(8)]

        def sem(n):
            return ctx.enter_context(nc.semaphore(n))

        pe, ve, ac, po, sp = (Queue(sem(n)) for n in ("s_pe", "s_ve", "s_act", "s_pool", "s_sp"))
        NW = 3
        wdma = Dma(sp, [sem(f"s_w{i}") for i in range(NW)])
        cdma = Dma(sp, [sem(f"s_c{i}") for i in range(6)])
        odma = Dma(po, [sem(f"s_o{i}") for i in range(8)])

        def fence():
            return [q.last for q in (pe, ve, ac, po) if q.n]

        top = [0]

        def take(n):
            top[0] += n
            return M[:, top[0] - n:top[0]]

        ident = take(128)
        MASK = take(1024)
        lvl = take(768)
        lvl0t, slow, supt, incl, bones = (take(128) for _ in range(5))
        hsel = take(2)
        invf = take(32)
        cosT, sinT = take(256), take(256)
        st = take(512)
        g_in, g_q, g_kv, g_sub, g_fin = take(8), take(3), take(2), take(1), None
        g_mix, g_ffn, g_att = take(8), take(8), take(4)
        posi, posf = take(8), take(8)
        lamv = take(8)
        mu_c, w0_c, a0_c, kk_c, ka_c, ka1_c, rk_c = take(14), take(4), take(4), take(4), take(4), take(4), take(4)
        WC = take(64)
        bon = take(64)
        assert top[0] < 4400
        top[0] = 4400
        Wb = [take(4096) for _ in range(NW)]
        HT = take(8192)
        R = take(52096 - top[0])
        ht3 = HT.rearrange("p (k s) -> p k s", k=8)
        W = Ring(Wb)

        def cload(dst, src, *wait):
            return cdma.go(dst, src, *wait)

        c_id = cload(ident, a["c_ident"])
        queues = dict(sp=sp, po=po, pe=pe, ve=ve, ac=ac, odma=odma, cdma=cdma, wdma=wdma)

        def slab(w, c0, n, k0=0, K=8):
            i, buf, free = W.next()
            v = buf[:, 0:K * n].rearrange("p (k n) -> p k n", k=K)
            src = w[k0 * 128:(k0 + K) * 128, c0:c0 + n].rearrange("(k p) n -> p k n", p=128)
            m = wdma.go(v, src, free, lane=i)
            return i, v, m

        class Banks:
            def __init__(self, ids):
                self.ids, self.i = ids, -1

            def next(self):
                self.i = (self.i + 1) % len(self.ids)
                b = self.ids[self.i]
                return b, bank_free[b]

        bank_free = [None] * 8
        allb = Banks(list(range(8)))

        def gemm(b, free, n, L, Rr, K, *wait, m=128):
            pe.wait(free, *wait)
            for k in range(K):
                mark = pe.mm(Bk[b][0:m, 0:n], L(k), Rr(k), k == 0, k == K - 1, inc=(k == K - 1))
            return mark

        stn = [0]

        def stat(n):
            if stn[0] + n > 512:
                stn[0] = 0
            stn[0] += n
            return st[:, stn[0] - n:stn[0]]

        def bc(ap, n):
            return ap.unsqueeze(2).to_broadcast([ap.shape[0], ap.shape[1], n])

        def transposed(src, n, dst3, t, ready, banks, gain=None, lo=0):
            marks = []
            for j0 in range(0, n, 4):
                m = min(4, n - j0)
                b, free = banks.next()
                pe.wait(free, ready, c_id)
                for j in range(m):
                    d = pe.tr(Bk[b][:, 128 * j:128 * j + 128], src[:, (j0 + j) * 128:(j0 + j + 1) * 128],
                              ident, inc=(j == m - 1))
                o = dst3[:, lo + j0:lo + j0 + m, t * 128:(t + 1) * 128]
                p = Bk[b][:, 0:128 * m].rearrange("p (j s) -> p j s", j=m)
                if gain is None:
                    e = ac.act(o, p, ACT.Copy, d)
                else:
                    e = ve.tt(o, p, bc(gain[:, j0:j0 + m], 128), ALU.mult, d)
                bank_free[b] = e
                marks.append(e)
            return marks, d

        def rstd(ss, n, inv_n, eps, *wait):
            m = ve.ts(ss, ss, inv_n, ALU.mult, eps, ALU.add, *wait)
            m = ac.act(ss, ss, ACT.Sqrt, m)
            return ve.recip(ss, ss, m)

        def all_wait():
            m = fence()
            for q in (pe, ve, ac, po):
                q.wait(*m)
            return m

        def attention(H, maps, score, v_of, dv, scale, finish, diff=None):
            PH = all_wait()
            pair = Ring([(0, 1), (2, 3)])
            slots = Ring([SB[:, 1024 * j:1024 * j + 1024] for j in range(4)])
            pts = Ring([SB[:, 4096:5120], SB[:, 5120:6144]])
            tb = Banks([4, 5])
            ob = Banks([6, 7])
            units = [(i, h) for i in range(8) for h in range(H)]
            state = {}

            def stage_a(u):
                i, h = u
                N = 128 * (i + 1)
                mx, nm, l, r = stat(maps), stat(maps), stat(maps), stat(maps)
                sl = []
                for m_ in range(maps):
                    pi, (b0, b1), pf = pair.next()
                    pe.wait(pf)
                    for n0 in range(0, N, 512):
                        n1 = min(N, n0 + 512)
                        parts = score(h, m_, i, n0, n1)
                        for k, (l_, r_) in enumerate(parts):
                            mk = pe.mm(PS[:, 512 * b0 + n0:512 * b0 + n1], l_, r_, k == 0, k == len(parts) - 1,
                                       inc=(k == len(parts) - 1 and n1 == N))
                    si, buf, sf = slots.next()
                    mt = ve.put(lambda e, buf=buf, b0=b0, m_=m_: e.tensor_tensor_reduce(
                        out=buf[:, 0:N], in0=PS[:, 512 * b0:512 * b0 + N], in1=MASK[:, 1024 - N:1024], scale=1.0,
                        scalar=-3.0e38, op0=ALU.add, op1=ALU.max, accum_out=mx[:, m_:m_ + 1]), [mk, sf])
                    pair.free[pi] = mt
                    sl.append((si, buf))
                mn = ve.ts(nm, mx, -scale, ALU.mult, None, None, mt)
                for m_ in range(maps):
                    buf = sl[m_][1]
                    me = ac.act(buf[:, 0:N], buf[:, 0:N], ACT.Exp, mn, bias=nm[:, m_:m_ + 1], scale=scale,
                                acc=l[:, m_:m_ + 1])
                if diff:
                    mr = ve.recip(r, l, me)
                    mr = ve.ts(r[:, 1:2], r[:, 1:2], lamv[:, 5:6], ALU.mult, None, None, mr, diff)
                    m2 = ve.ts(sl[1][1][:, 0:N], sl[1][1][:, 0:N], r[:, 1:2], ALU.mult, None, None, mr)
                    me = ve.stt(sl[0][1][:, 0:N], sl[0][1][:, 0:N], r[:, 0:1], sl[1][1][:, 0:N], ALU.mult, ALU.add, m2)
                    slots.free[sl[1][0]] = me
                    mr = None
                else:
                    mr = ve.recip(r, l, me)
                state[u] = (sl[0], me, r, mr)

            def stage_b(u):
                i, h = u
                (si, buf), me, r, mr = state[u]
                pi, pt, pf = pts.next()
                for j0 in range(0, i + 1, 4):
                    n = min(4, i + 1 - j0)
                    b, free = tb.next()
                    pe.wait(free, me)
                    for j in range(n):
                        d = pe.tr(Bk[b][:, 128 * j:128 * j + 128], buf[:, (j0 + j) * 128:(j0 + j + 1) * 128], ident,
                                  inc=(j == n - 1))
                    mc = ac.act(pt[:, 128 * j0:128 * (j0 + n)], Bk[b][:, 0:128 * n], ACT.Copy, d, pf)
                    bank_free[b] = mc
                slots.free[si] = d
                state[u] = (pi, pt, mc, r, mr)

            def stage_c(u):
                i, h = u
                pi, pt, mc, r, mr = state.pop(u)
                b, free = ob.next()
                pe.wait(free, mc)
                for j in range(i + 1):
                    d = pe.mm(Bk[b][:, 0:dv], pt[:, 128 * j:128 * j + 128], v_of(j, h), j == 0, j == i, inc=(j == i))
                pts.free[pi] = d
                bank_free[b] = finish(i, h, Bk[b][:, 0:dv], r, d)

            U = len(units)
            for s_ in range(U + 2):
                if s_ < U:
                    stage_a(units[s_])
                if 1 <= s_ <= U:
                    stage_b(units[s_ - 1])
                if s_ >= 2:
                    stage_c(units[s_ - 2])

        SB = R[:, 19456:19456 + 6144]
        R0, R1, R2, R3 = (R[:, 4096 * j:4096 * j + 4096] for j in range(4))
        xd = nc.dram_tensor("x1_kept", [128, 8192], F32, kind="Internal").ap()
        md = nc.dram_tensor("mix_kept", [128, 4096], F32, kind="Internal").ap()

        def block1():
            xsrc = a["x"].rearrange("b (t p) d -> p (b t) d", p=128)
            c_gin = cload(g_in, a["norm_in"].rearrange("l (k p) -> p (l k)", p=128))
            xr = R[:, 0:8192].rearrange("p (t d) -> p t d", t=8)
            cx = [cload(xr[:, 2 * j:2 * j + 2, :], xsrc[:, 2 * j:2 * j + 2, :]) for j in range(4)]
            small = [
                (MASK, a["c_caus"]), (posi.bitcast(I32), a["positions"].rearrange("b (t p) -> p (b t)", p=128)),
                (invf, a["c_invf"]), (g_q, a["mla_q_norm"].rearrange("l (k p) -> p (l k)", p=128)),
                (g_kv, a["mla_kv_norm"].rearrange("l (k p) -> p (l k)", p=128)),
                (g_sub, a["diff_subln"].rearrange("l (k p) -> p (l k)", p=128)),
            ]
            ss = stat(8)
            junk = [R[:, 8192:9216], R[:, 11264:12288]]
            jm = [None, None]
            for t in range(8):
                jm[t % 2] = m = ac.act(junk[t % 2], xr[:, t, :], ACT.Square, cx[t // 2], jm[t % 2], acc=ss[:, t:t + 1])
            m = rstd(ss, 8, 1.0 / D, EPS, m)
            xs = Ring([R[:, 9216:10240], R[:, 10240:11264]])
            h_done = []
            for t in range(8):
                i, buf, free = xs.next()
                m1 = ve.ts(buf, xr[:, t, :], ss[:, t:t + 1], ALU.mult, None, None, m, free)
                marks, d = transposed(buf, 8, ht3, t, m1, allb, gain=g_in)
                if t == 0:
                    ve.wait(c_gin)
                xs.free[i] = d
                h_done = marks
            for dst, src in small:
                m_small = cload(dst, src)
            c_small = cdma.all()

            m = ve.copy(posf, posi.bitcast(I32), c_small)
            tmpA, tmpB = R[:, 12288:12544], R[:, 12544:12800]
            pos3, inv3 = bc(posf, 32), invf.unsqueeze(1).to_broadcast([128, 8, 32])
            A3 = tmpA.rearrange("p (t f) -> p t f", t=8)
            m = ve.tt(A3, pos3, inv3, ALU.mult, m)
            MAGIC = 12582912.0
            m = ve.ts(tmpB, tmpA, 1.0 / TWO_PI, ALU.mult, MAGIC, ALU.add, m)
            m = ve.ts(tmpB, tmpB, MAGIC, ALU.subtract, None, None, m)
            c1 = 6.28125
            c2 = float(np.float32(np.floor((TWO_PI - c1) * 2 ** 21) / 2 ** 21))
            c3 = TWO_PI - c1 - c2
            for c_ in (c1, c2, c3):
                m = ve.stt(tmpA, tmpB, -c_, tmpA, ALU.mult, ALU.add, m)
            PI = 3.1415925
            m = ve.ts(tmpB, tmpA, math.pi / 2, ALU.add, None, None, m)
            m2 = ve.ts(cosT, tmpB, PI, ALU.is_gt, None, None, m)
            m2 = ve.stt(tmpB, cosT, -TWO_PI, tmpB, ALU.mult, ALU.add, m2)
            m2 = ve.ts(tmpB, tmpB, PI, ALU.min, -PI, ALU.max, m2)
            m = ve.ts(tmpA, tmpA, PI, ALU.min, -PI, ALU.max, m2)
            c_rope = [ac.act(cosT, tmpB, ACT.Sin, m), ac.act(sinT, tmpA, ACT.Sin, m)]
            cos3 = cosT.rearrange("p (t f) -> p t f", t=8)
            sin3 = sinT.rearrange("p (t f) -> p t f", t=8)

            lrow = R[:, 12800:13056]
            for j, n in enumerate(("diff_lambda_q1", "diff_lambda_k1", "diff_lambda_q2", "diff_lambda_k2")):
                cl = cload(lrow[:, 64 * j:64 * j + 64], bass_rows(a[n], 128))
            cl = cdma.all()
            m = ve.put(lambda e: e.tensor_tensor_reduce(out=lrow[:, 0:64], in0=lrow[:, 0:64], in1=lrow[:, 64:128], scale=1.0,
                       scalar=0.0, op0=ALU.mult, op1=ALU.add, accum_out=lamv[:, 0:1]), [cl])
            m = ve.put(lambda e: e.tensor_tensor_reduce(out=lrow[:, 128:192], in0=lrow[:, 128:192], in1=lrow[:, 192:256], scale=1.0,
                       scalar=0.0, op0=ALU.mult, op1=ALU.add, accum_out=lamv[:, 1:2]), [])
            m = ac.act(lamv[:, 2:4], lamv[:, 0:2], ACT.Exp, m)
            m = ve.tt(lamv[:, 4:5], lamv[:, 3:4], lamv[:, 2:3], ALU.subtract, m)
            c_lam = ve.ts(lamv[:, 5:6], lamv[:, 4:5], -LAMBDA_INIT, ALU.add, None, None, m)

            w_in = a["w_in"][0]
            PH = fence()
            R0, R1, R2, R3 = (R[:, 4096 * j:4096 * j + 4096] for j in range(4))
            R4, R5 = R[:, 16384:18432], R[:, 18432:19456]
            SB = R[:, 19456:19456 + 6144]
            XT = R[:, 25600:27216]
            rt = Ring([SB[:, 0:512], SB[:, 512:1024], SB[:, 1024:1536]])
            rt2 = Ring([SB[:, 1536:2048], SB[:, 2048:2560], SB[:, 2560:3072]])

            def rope(b, mark, t, groups, dst, c0=0):
                n = groups * 64
                x4 = Bk[b][:, c0:c0 + n].rearrange("p (g h f) -> p g h f", g=groups, h=2)
                i1, b1, f1 = rt.next()
                i2, b2, f2 = rt2.next()
                t1 = b1[:, 0:n].rearrange("p (g h f) -> p g h f", g=groups, h=2)
                t2 = b2[:, 0:n].rearrange("p (g h f) -> p g h f", g=groups, h=2)
                cb = cos3[:, t, :].unsqueeze(1).unsqueeze(1).to_broadcast([128, groups, 2, 32])
                sb_ = sin3[:, t, :].unsqueeze(1).unsqueeze(1).to_broadcast([128, groups, 2, 32])
                ve.tt(t1, x4, cb, ALU.mult, mark, c_rope, f1)
                m = ve.tt(t2, x4, sb_, ALU.mult, f2)
                free = m
                po.wait(m)
                m1 = po.tt(t1[:, :, 0, :], t1[:, :, 0, :], t2[:, :, 1, :], ALU.subtract)
                m2 = po.tt(t1[:, :, 1, :], t1[:, :, 1, :], t2[:, :, 0, :], ALU.add)
                rt2.free[i2] = m2
                return i1, b1, m2, free

            def proj(c0, n, each, w=w_in, K=8, lhs=None, tiles=8, banks=allb, first=()):
                i, v, m = slab(w, c0, n, K=K)
                L = lhs or ht3
                for t in range(tiles):
                    b, free = banks.next()
                    mk = gemm(b, free, n, lambda k: L[:, k, t * 128:(t + 1) * 128], lambda k: v[:, k, :], K, m, *first)
                    bank_free[b] = each(t, b, mk)
                W.free[i] = mk

            def rope_into(dst3, groups):
                def each(t, b, mk):
                    i1, buf, m, free = rope(b, mk, t, groups, None)
                    _, d = transposed(buf, groups // 2, dst3, t, m, allb)
                    rt.free[i1] = d
                    return free
                return each

            qT3 = R0.rearrange("p (c s) -> p c s", c=4)
            kT3 = R1.rearrange("p (c s) -> p c s", c=4)
            V3 = R2.rearrange("p (t d) -> p t d", t=8)
            all_wait()
            proj(0, 512, rope_into(qT3, 8), first=h_done)
            proj(512, 512, rope_into(kT3, 8))
            proj(1024, 512, lambda t, b, mk: ac.act(V3[:, t, :], Bk[b], ACT.Copy, mk))

            def diff_score(h, m_, i, n0, n1):
                return [(qT3[64 * m_:64 * m_ + 64, h, 128 * i:128 * i + 128], kT3[64 * m_:64 * m_ + 64, h, n0:n1])]

            def o_place(i, h, reg):
                return reg[:, h * 1024 + i * 128:h * 1024 + (i + 1) * 128]

            attention(4, 2, diff_score, lambda j, h: V3[:, j, 128 * h:128 * h + 128], 128, 0.125,
                      lambda i, h, p, r, d: ve.copy(o_place(i, h, R0), p, d), diff=c_lam)
            PH = all_wait()
            ssd = take_s = stat(32)
            od3 = R0.rearrange("p (h t d) -> p h t d", h=4, t=8)
            for h in range(4):
                m = po.tt(SB[:, 0:1024].rearrange("p (t d) -> p t d", t=8), od3[:, h], od3[:, h], ALU.mult, *(() if h == 0 else (m,)))
                m = ve.red(ssd[:, 8 * h:8 * h + 8], SB[:, 0:1024].rearrange("p (t d) -> p t d", t=8), ALU.add, m)
            m = rstd(ssd, 32, 1.0 / 128, EPS, m)
            m = ve.ts(ssd, ssd, 1.0 - LAMBDA_INIT, ALU.mult, None, None, m)
            for h in range(4):
                m = ve.tt(od3[:, h], od3[:, h], bc(ssd[:, 8 * h:8 * h + 8], 128), ALU.mult, m)
            PH = all_wait()
            cqr = R1[:, 0:3072].rearrange("p (t d) -> p t d", t=8)
            ckr = R2[:, 0:2048].rearrange("p (t d) -> p t d", t=8)
            krT = R5
            kr3 = R5.rearrange("p (c s) -> p c s", c=1)
            ssq, ssk = stat(8), stat(8)
            tr_ = Ring([XT[:, 0:384], XT[:, 384:768]])

            def cq_each(t, b, mk):
                ac.act(cqr[:, t, :], Bk[b][:, 0:384], ACT.Copy, mk)
                return ac.act(XT[:, 768:1152], Bk[b][:, 0:384], ACT.Square, ac.last, acc=ssq[:, t:t + 1])

            def ckv_each(t, b, mk):
                ac.act(ckr[:, t, :], Bk[b][:, 0:256], ACT.Copy, mk)
                m = ac.act(XT[:, 768:1024], Bk[b][:, 0:256], ACT.Square, ac.last, acc=ssk[:, t:t + 1])
                i1, b1, f1 = rt.next()
                i2, b2, f2 = rt2.next()
                x = Bk[b][:, 256:320].rearrange("p (h f) -> p h f", h=2)
                t1 = b1[:, 0:64].rearrange("p (h f) -> p h f", h=2)
                t2 = b2[:, 0:64].rearrange("p (h f) -> p h f", h=2)
                cb = cos3[:, t, :].unsqueeze(1).to_broadcast([128, 2, 32])
                sb_ = sin3[:, t, :].unsqueeze(1).to_broadcast([128, 2, 32])
                ve.tt(t1, x, cb, ALU.mult, m, f1)
                m = ve.tt(t2, x, sb_, ALU.mult, f2)
                free = m
                po.tt(t1[:, 0, :], t1[:, 0, :], t2[:, 1, :], ALU.subtract, m)
                m = po.tt(t1[:, 1, :], t1[:, 1, :], t2[:, 0, :], ALU.add)
                m = po.copy(b1[:, 64:128], b1[:, 0:64], m)
                rt2.free[i2] = m
                _, d = transposed(b1, 1, kr3, t, m, allb)
                rt.free[i1] = d
                return free

            proj(2048, 384, cq_each)
            proj(2432, 320, ckv_each)
            PH = all_wait()
            m = rstd(ssq, 8, 1.0 / 384, EPS)
            mk_ = rstd(ssk, 8, 1.0 / 256, EPS)
            cqT = SB[:, 3072:6144].rearrange("p (c s) -> p c s", c=3)
            ckT = HTx = R3[:, 0:2048].rearrange("p (c s) -> p c s", c=2)
            for t in range(8):
                i, buf, free = tr_.next()
                m1 = ve.ts(buf, cqr[:, t, :], ssq[:, t:t + 1], ALU.mult, None, None, m, free)
                _, tr_.free[i] = transposed(buf, 3, cqT, t, m1, allb, gain=g_q)
                i, buf, free = tr_.next()
                m1 = ve.ts(buf[:, 0:256], ckr[:, t, :], ssk[:, t:t + 1], ALU.mult, None, None, mk_, free)
                _, tr_.free[i] = transposed(buf, 2, ckT, t, m1, allb, gain=g_kv)
            PH = all_wait()
            qn3 = R1.rearrange("p (c s) -> p c s", c=4)
            kn3 = R2.rearrange("p (c s) -> p c s", c=4)
            qr3 = R4.rearrange("p (c s) -> p c s", c=2)
            i, v, m = slab(a["w_uq"][0], 0, 768, K=3)
            for h in range(4):
                for s_ in range(2):
                    b, free = allb.next()
                    mk = gemm(b, free, 512, lambda k: v[:, k, 192 * h:192 * h + 128], lambda k: cqT[:, k, 512 * s_:512 * s_ + 512], 3, m)
                    bank_free[b] = ac.act(qn3[:, h, 512 * s_:512 * s_ + 512], Bk[b], ACT.Copy, mk)
            vr = v.rearrange("p k (h c) -> p k h c", h=4)
            for t in range(8):
                b, free = allb.next()
                pe.wait(free)
                for h in range(4):
                    for k in range(3):
                        mk = pe.mm(Bk[b][:, 64 * h:64 * h + 64], cqT[:, k, 128 * t:128 * t + 128], vr[:, k, h, 128:192],
                                   k == 0, k == 2, inc=(k == 2 and h == 3))
                i1, buf, m1, free = rope(b, mk, t, 4, None)
                bank_free[b] = free
                _, d = transposed(buf, 2, qr3, t, m1, allb)
                rt.free[i1] = d
            W.free[i] = mk
            i, v, m = slab(a["w_ukv"][0], 0, 1024, K=2)
            for h in range(4):
                for s_ in range(2):
                    b, free = allb.next()
                    mk = gemm(b, free, 512, lambda k: v[:, k, 256 * h:256 * h + 128], lambda k: ckT[:, k, 512 * s_:512 * s_ + 512], 2, m)
                    bank_free[b] = ac.act(kn3[:, h, 512 * s_:512 * s_ + 512], Bk[b], ACT.Copy, mk)
            vr2 = v.rearrange("p k (h c) -> p k h c", h=4)
            V4 = R[:, 19456:19456 + 3072]
            mvA = [None] * 8
            for t in range(8):
                b, free = allb.next()
                pe.wait(free)
                for h in range(4):
                    for k in range(2):
                        mk = pe.mm(Bk[b][:, 128 * h:128 * h + 128], ckT[:, k, 128 * t:128 * t + 128], vr2[:, k, h, 128:256],
                                   k == 0, k == 1, inc=(k == 1 and h == 3))
                mvA[t] = (b, mk)
            W.free[i] = mk
            for t in range(8):
                b, _ = mvA[t]
                bank_free[b] = ac.act(R3[:, 512 * t:512 * t + 512], Bk[b], ACT.Copy, mk)
            mV3 = R3.rearrange("p (t d) -> p t d", t=8)

            def mla_score(h, m_, i, n0, n1):
                c, o = h // 2, 64 * (h % 2)
                return [(qn3[:, h, 128 * i:128 * i + 128], kn3[:, h, n0:n1]),
                        (qr3[o:o + 64, c, 128 * i:128 * i + 128], R5[o:o + 64, n0:n1])]

            attention(4, 1, mla_score, lambda j, h: mV3[:, j, 128 * h:128 * h + 128], 128, 192.0 ** -0.5,
                      lambda i, h, p, r, d: ve.ts(o_place(i, h, R1), p, r[:, 0:1], ALU.mult, None, None, d))

            PH = all_wait()
            oT = [R2.rearrange("p (c s) -> p c s", c=4), R3.rearrange("p (c s) -> p c s", c=4)]
            gb = Ring([SB[:, 512 * j:512 * j + 512] for j in range(3)])
            gsub = g_sub.to_broadcast([128, 4])

            def gate_each(reg, dst, gain):
                r4 = reg.rearrange("p (h t d) -> p h t d", h=4, t=8)

                def each(t, b, mk):
                    gi, buf, gf = gb.next()
                    m = ac.act(buf, Bk[b], ACT.Silu, mk, gf)
                    b4 = buf.rearrange("p (h d) -> p h d", h=4)
                    m2 = po.tt(b4, b4, r4[:, :, t, :], ALU.mult, m)
                    _, d = transposed(buf, 4, dst, t, m2, allb, gain=gain)
                    gb.free[gi] = d
                    return m
                return each

            proj(1536, 512, gate_each(R0, oT[0], gsub))
            proj(2752, 512, gate_each(R1, oT[1], None))
            PH = all_wait()
            MG = R[:, 0:8192].rearrange("p (t d) -> p t d", t=8)
            g1 = Ring([SB[:, 0:512], SB[:, 512:1024]])
            for c in range(2):
                for kind, (wg, wp, o_) in enumerate(((3264, "w_proj_diff", oT[0]), (4288, "w_proj_mla", oT[1]))):
                    ig, vg, mg = slab(w_in, wg + 512 * c, 512)
                    ip, vp, mp = slab(a[wp][0], 512 * c, 512, K=4)
                    for t in range(8):
                        b, free = allb.next()
                        mk = gemm(b, free, 512, lambda k: ht3[:, k, 128 * t:128 * t + 128], lambda k: vg[:, k, :], 8, mg)
                        gi, buf, gf = g1.next()
                        m = ac.act(buf, Bk[b], ACT.Sigmoid, mk, gf)
                        bank_free[b] = m
                        b, free = allb.next()
                        mk = gemm(b, free, 512, lambda k: o_[:, k, 128 * t:128 * t + 128], lambda k: vp[:, k, :], 4, mp)
                        dst = MG[:, t, 512 * c:512 * c + 512]
                        if kind == 0:
                            m = ve.tt(dst, Bk[b], buf, ALU.mult, m, mk)
                            bank_free[b] = m
                            g1.free[gi] = m
                        else:
                            m = ve.tt(buf, Bk[b], buf, ALU.mult, m, mk)
                            bank_free[b] = m
                            g1.free[gi] = po.tt(dst, dst, buf, ALU.add, m)
                    W.free[ig] = W.free[ip] = mk
            PH = all_wait()
            for t in range(8):
                transposed(MG[:, t, :], 8, ht3, t, None, allb)
            mT = fence()
            X1 = R[:, 8192:16384].rearrange("p (t d) -> p t d", t=8)
            cx = [cdma.go(X1[:, 2 * j:2 * j + 2, :], xsrc[:, 2 * j:2 * j + 2, :], PH) for j in range(4)]
            gfin = SB[:, 0:1024]
            c_gf = cdma.go(gfin, bass_rows(a["norm_final"].rearrange("(a n) -> a n", a=1), 128), PH)
            for c in range(2):
                i, v, m = slab(a["w_out"][0], 512 * c, 512)
                for t in range(8):
                    b, free = allb.next()
                    mk = gemm(b, free, 512, lambda k: ht3[:, k, 128 * t:128 * t + 128], lambda k: v[:, k, :], 8, m, mT)
                    dst = X1[:, t, 512 * c:512 * c + 512]
                    bank_free[b] = ve.tt(dst, Bk[b], dst, ALU.add, mk, cx)
                W.free[i] = mk
            ssf = stat(8)
            for t in range(8):
                m = ac.act(SB[:, 1024:2048], X1[:, t, :], ACT.Square, ve.last, ac.last, acc=ssf[:, t:t + 1])
            m = rstd(ssf, 8, 1.0 / D, EPS, m)
            for t in range(8):
                mx1 = ve.stt(X1[:, t, :], X1[:, t, :], ssf[:, t:t + 1], gfin, ALU.mult, ALU.mult, m, c_gf)

        def gemm_feat(v, m, lhs3, col, cols, K, evac, banks=allb):
            for s_ in range(2):
                b, free = banks.next()
                mk = gemm(b, free, 512, lambda k: v[:, k, col:col + cols], lambda k: lhs3[:, k, 512 * s_:512 * s_ + 512],
                          K, m, m=cols)
                bank_free[b] = evac(s_, b, mk)
            return mk

        def norm_T(X, gain, scratch, reads=()):
            ss = stat(8)
            jm = None
            for t in range(8):
                jm = ac.act(scratch[2], X[:, t, :], ACT.Square, jm, *reads, acc=ss[:, t:t + 1])
            m = rstd(ss, 8, 1.0 / D, EPS, jm)
            xs = Ring(scratch[0:2])
            for t in range(8):
                i, buf, free = xs.next()
                m1 = ve.ts(buf, X[:, t, :], ss[:, t:t + 1], ALU.mult, None, None, m, free)
                _, xs.free[i] = transposed(buf, 8, ht3, t, m1, allb, gain=gain)

        def vec_cols(name, c0, n):
            return a[name].rearrange("l n -> (l n)")[c0:c0 + n].rearrange("(k p) -> p k", p=128 if n >= 128 else n)

        def block2():
            X1 = R[:, 8192:16384].rearrange("p (t d) -> p t d", t=8)
            PH = all_wait()
            m_x1 = odma.go(xd, R[:, 8192:16384], *PH)
            for dst, name, c0, n in (
                    (g_mix, "norm_mix_pre_2", 0, 1024), (g_ffn, "norm_ffn_pre_2", 0, 1024), (g_att, "attn_out_gain_2", 0, 512),
                    (mu_c[:, 0:12], "mu_shift_2", 0, 1536), (mu_c[0:64, 12:13], "mu_shift_2", 1536, 64),
                    (mu_c[0:96, 13:14], "mu_shift_2", 1600, 96), (w0_c, "decay_w0_2", 0, 512), (a0_c, "aaa_a0_2", 0, 512),
                    (kk_c, "k_k_2", 0, 512), (ka_c, "k_a_2", 0, 512)):
                cload(dst, vec_cols(name, c0, n))
            cload(rk_c, a["r_k_2"].rearrange("l (k h) c -> (h c) (l k)", h=2))
            for dst, name in ((lvl, "lvl"), (lvl0t, "lvl0t"), (slow, "slow"), (supt, "supt"), (incl, "incl"),
                              (bones, "bones"), (hsel, "hsel")):
                cload(dst, a["c_" + name])
            cload(MASK, a["c_dil"], *PH)
            C2 = cdma.all()
            w1 = a["w_in_first_2"]

            ve.wait(C2)
            norm_T(X1, g_mix, [R[:, 0:1024], R[:, 1024:2048], R[:, 2048:3072]])
            PH = all_wait()
            qT3 = R0.rearrange("p (c s) -> p c s", c=4)
            kT3 = R1.rearrange("p (c s) -> p c s", c=4)
            V3 = R2.rearrange("p (t d) -> p t d", t=8)
            for c0, dst in ((0, qT3), (512, kT3)):
                i, v, m = slab(w1, c0, 512)
                for c in range(4):
                    W.free[i] = gemm_feat(v, m, ht3, 128 * c, 128, 8, lambda s_, b, mk: ac.act(
                        dst[:, c, 512 * s_:512 * s_ + 512], Bk[b], ACT.Copy, mk))
            ac.wait(m_x1)
            i, v, m = slab(w1, 1024, 512)
            for t in range(8):
                b, free = allb.next()
                mk = gemm(b, free, 512, lambda k: ht3[:, k, 128 * t:128 * t + 128], lambda k: v[:, k, :], 8, m)
                bank_free[b] = ac.act(V3[:, t, :], Bk[b], ACT.Copy, mk)
            W.free[i] = mk

            def dil_score(h, m_, i, n0, n1):
                o = 64 * (h % 2)
                return [(qT3[o:o + 64, h // 2, 128 * i:128 * i + 128], kT3[o:o + 64, h // 2, n0:n1])]

            def dil_done(i, h, p, r, d):
                c = (h // 2) * 1024 + i * 128 + 64 * (h % 2)
                return ve.ts(R0[:, c:c + 64], p, r[:, 0:1], ALU.mult, None, None, d)

            attention(8, 1, dil_score, lambda j, h: V3[:, j, 64 * h:64 * h + 64], 64, 0.125, dil_done)
            PH = all_wait()
            m_reset = cload(MASK, a["c_reset"], *PH)
            o4 = R0.rearrange("p (c t d) -> p t c d", c=4, t=8)
            ssa = stat(8)
            jm = None
            for t in range(8):
                jm = ac.act(SB[:, 0:512].rearrange("p (c d) -> p c d", c=4), o4[:, t], ACT.Square, jm, acc=ssa[:, t:t + 1])
            m = rstd(ssa, 8, 1.0 / 512, EPS, jm)
            mixA = R1.rearrange("p (c s) -> p c s", c=4)
            xs = Ring([SB[:, 512:1024], SB[:, 1024:1536]])
            for t in range(8):
                i, buf, free = xs.next()
                m1 = ve.ts(buf.rearrange("p (c d) -> p c d", c=4), o4[:, t], ssa[:, t:t + 1], ALU.mult, None, None, m, free)
                _, xs.free[i] = transposed(buf, 4, mixA, t, m1, allb, gain=g_att)
            PH = all_wait()
            m_mix = odma.go(md, R1, *PH)

            KAP, BET, KHT, RHO = (R[:, 4096 * j:4096 * j + 4096].rearrange("p (c s) -> p c s", c=4) for j in range(4))
            VT = R[:, 16384:20480].rearrange("p (t d) -> p t d", t=8)
            T1, T2, T3, T4 = (R[:, 20480 + 1024 * j:20480 + 1024 * j + 1024] for j in range(4))
            LW = R[:, 24576:25600]
            Zf = R[:, 25600:26632]
            Z = Zf[:, 8:1032]
            Zp = Zf[:, 7:1031]
            UPS = R[:, 26632:27144]
            XG = LW
            c_up = [cload(UPS[0:32, :], a["decay_up_2"][0], *PH), cload(UPS[32:64, :], a["aaa_up_2"][0], *PH)]
            ve.wait(m_mix); po.wait(m_mix); ac.wait(m_mix)
            m_z0 = ve.put(lambda e: e.memset(Zf[:, 0:8], 0.0))
            halfsl = [slice(0, 512), slice(512, 1024)]

            def stream(v, m, col, cols, muc, dst, before=()):
                zm = []

                def evac(s_, b, mk):
                    zm.append(ac.act(Z[0:cols, halfsl[s_]], Bk[b][0:cols, :], ACT.Copy, mk, *before))
                    return zm[-1]
                mk = gemm_feat(v, m, ht3, col, cols, 8, evac)
                m1 = po.tt(T1[0:cols, :], Zp[0:cols, :], Z[0:cols, :], ALU.subtract, zm, m_z0, ve.last)
                m2 = ve.stt(dst, T1[0:cols, :], muc, Z[0:cols, :], ALU.mult, ALU.add, m1)
                return mk, m2

            i, v, m = slab(w1, 3072, 64)
            mk, m2 = stream(v, m, 0, 64, mu_c[0:64, 12:13], LW[0:64, :])
            W.free[i] = mk
            m_lw = ac.act(LW[0:32, :], LW[0:32, :], ACT.Tanh, m2)
            slabs = [slab(w1, 1536 + 512 * j, 512) for j in range(3)]
            for p in range(4):
                r_, k_, b_, h_ = RHO[:, p, :], KAP[:, p, :], BET[:, p, :], KHT[:, p, :]
                mks = []
                for j, dst in ((0, r_), (1, h_), (2, T2)):
                    mk, mz = stream(slabs[j][1], slabs[j][2], 128 * p, 128, mu_c[:, 4 * j + p:4 * j + p + 1], dst,
                                    before=(ve.last, po.last, ac.last))
                    if p == 3:
                        W.free[slabs[j][0]] = mk
                em, d = transposed(T2, 8, VT, p, mz, allb)

                def lora(r0, up, dst, bias, *wait):
                    for s_ in range(2):
                        b, free = allb.next()
                        mk = pe.mm(Bk[b], UPS[r0:r0 + 32, 128 * p:128 * p + 128], LW[r0:r0 + 32, halfsl[s_]], True, True,
                                   free, c_up, m_lw, inc=True)
                        bank_free[b] = ac.act(dst[:, halfsl[s_]], Bk[b], ACT.Sigmoid, mk, *wait, bias=bias)
                    return bank_free[b]
                m = lora(0, None, T3, w0_c[:, p:p + 1])
                m = ve.ts(T3, T3, -math.exp(-0.5), ALU.mult, None, None, m)
                m_lc = ve.put(lambda e: e.tensor_tensor_scan(T1, MASK, T3, 0.0, ALU.mult, ALU.add), [m, m_reset, po.last])
                m_a = lora(32, None, T2, a0_c[:, p:p + 1], d)
                m_kk = ve.ts(k_, h_, kk_c[:, p:p + 1], ALU.mult, None, None)
                m = po.tt(Z, k_, k_, ALU.mult, m_kk)
                for s_ in range(2):
                    b, free = allb.next()
                    mk = pe.mm(Bk[b], bones, Z[:, halfsl[s_]], True, True, free, m, inc=True)
                    bank_free[b] = ac.act(T4[:, halfsl[s_]], Bk[b], ACT.Sqrt, mk)
                m = ve.ts(T4, T4, 1e-12, ALU.max, None, None, bank_free[b], ac.last)
                m = ve.recip(T4, T4, m)
                m_kk = ve.tt(k_, k_, T4, ALU.mult, m)
                m = ve.ts(T4, T2, -1.0, ALU.add, None, None, m_kk, m_a)
                m = ve.ts(T4, T4, ka_c[:, p:p + 1], ALU.mult, 1.0, ALU.add, m)
                m_km = ve.tt(h_, h_, T4, ALU.mult, m)
                m = ve.stt(Z, r_, rk_c[:, p:p + 1], h_, ALU.mult, ALU.mult, m_km, mk)
                b, free = allb.next()
                pe.wait(free, m)
                for t in range(8):
                    mb = pe.mm(Bk[b][:, 2 * t:2 * t + 2], Z[:, 128 * t:128 * t + 128], hsel, True, True, inc=(t == 7))
                bank_free[b] = ve.copy(bon.rearrange("p (t h) -> p t h", t=8)[:, :, 2 * p:2 * p + 2],
                                       Bk[b][:, 0:16].rearrange("p (t h) -> p t h", t=8), mb)
                m_b = po.tt(b_, k_, T2, ALU.mult, m_kk, m_a)
                me = ac.act(T4, T1, ACT.Exp, m_km, m_lc)
                m = ve.tt(r_, r_, T4, ALU.mult, me, ve.last)
                mw = ve.copy(WC.rearrange("p (k c) -> p k c", k=4)[:, p, :], T4.rearrange("p (c n) -> p n c", n=64)[:, 63, :])
                me = ac.act(T2, T1, ACT.Exp, m_b, scale=-1.0)
                po.tt(b_, b_, T2, ALU.mult, me, m_b)
                m = ve.tt(h_, h_, T2, ALU.mult, me)
                m = ve.tt(T3, T1, T3, ALU.subtract)
                me = ac.act(T3, T3, ACT.Exp, m)
                m = po.tt(k_, k_, T3, ALU.mult, me)
            i, v, m = slab(w1, 3136, 96)
            mk, m2 = stream(v, m, 0, 96, mu_c[0:96, 13:14], T2[0:96, :], before=(ve.last, po.last, ac.last, mb))
            W.free[i] = mk
            m_xg = ac.act(XG[0:96, :], T2[0:96, :], ACT.Sigmoid, m2, pe.last)

            PH = all_wait()
            ac.wait(m_xg)
            c_gn = [cload(MASK[:, 0:512], bass_rows(a["gn_w_2"], 128), *PH),
                    cload(MASK[:, 512:1024], bass_rows(a["gn_b_2"], 128), *PH)]
            c_g = cload(UPS[0:96, :], a["gate_up_2"][0], *PH)
            GW, GB = MASK[:, 0:512], MASK[:, 512:1024]
            ab2 = Banks([0, 1, 2, 3])
            cb2 = Banks([4, 5, 6, 7])
            spare = [HT[:, 1024 * j:1024 * j + 1024] for j in range(8)] + [T1, T2, T3, T4]
            w2 = Wb[2]
            PH3 = [W.free[2]]
            for q in (pe, ve, ac, po):
                q.wait(*PH3)
            Tt, T_, XP, Ll, L_ = spare[0:5]
            AB = [spare[5], spare[6]]
            AK = [spare[7], spare[8]]
            NB = [spare[9][:, 0:512], spare[9][:, 512:1024]]
            KH = [spare[10][:, 0:512], spare[10][:, 512:1024]]
            PT = [spare[11][:, 0:512], spare[11][:, 512:1024]]
            QS = [w2[:, 0:512], w2[:, 512:1024]]
            KTk, Xv = w2[:, 1024:1536], w2[:, 1536:2048]
            SH = [w2[:, 2048 + 256 * j:2304 + 256 * j] for j in range(4)]
            YB, Y2 = w2[:, 3072:3584], w2[:, 3584:4096]
            U_ = R[:, 25600:26112]
            Y3 = R[:, 26112:26624]
            MR = R[:, 0:4096].rearrange("p (c s) -> p c s", c=4)
            m_s0 = ve.put(lambda e: e.memset(SH[0], 0.0))

            def pj(buf):
                return buf.rearrange("p (q j s) -> p q j s", q=2, j=4)

            def b3(b):
                return Bk[b].rearrange("p (j s) -> p j s", j=4)

            def mask3(mk_):
                return mk_.unsqueeze(1).to_broadcast([128, 4, 128])

            use = {}

            def prep(t):
                z = t % 2
                ts_ = slice(128 * t, 128 * t + 128)
                g = use.get(("tile", t - 2), [])
                for src, dst, sc in ((KAP, KTk, 1.0), (BET, NB[z], -1.0), (KHT, KH[z], 1.0)):
                    b, free = ab2.next()
                    pe.wait(free, c_id)
                    for p in range(4):
                        d = pe.tr(Bk[b][:, 128 * p:128 * p + 128], src[:, p, ts_], ident, inc=(p == 3))
                    bank_free[b] = ac.act(dst, Bk[b], ACT.Copy, d, g, use.get("ktk") if dst is KTk else None, scale=sc)
                m_tok = bank_free[b]

                def products(l3, r3, dst, mask, op_neg, *wait):
                    for q in range(2):
                        b, free = ab2.next()
                        pe.wait(free)
                        for j in range(4):
                            d = pe.mm(Bk[b][:, 128 * j:128 * j + 128], l3[64 * q:64 * q + 64, j, ts_],
                                      r3[64 * q:64 * q + 64, j, ts_], True, True, inc=(j == 3))
                        if op_neg:
                            m = ve.stt(pj(dst)[:, q], b3(b), -1.0, mask3(mask), ALU.mult, ALU.mult, d, *wait)
                        else:
                            m = ve.tt(pj(dst)[:, q], b3(b), mask3(mask), ALU.mult, d, *wait)
                        bank_free[b] = m
                    return m
                m_l = products(KAP, BET, L_, slow, False, use.get("L"))
                m_x = products(KHT, KAP, XP, supt, False, use.get("XP"))
                m = po.tt(T_.rearrange("p (h s) -> p h s", h=8), L_.rearrange("p (h s) -> p h s", h=8),
                          lvl[:, 0:128].unsqueeze(1).to_broadcast([128, 8, 128]), ALU.mult, m_l, use.get("T"))
                m_t = ve.stt(T_.rearrange("p (h s) -> p h s", h=8), T_.rearrange("p (h s) -> p h s", h=8), -1.0,
                             ident.unsqueeze(1).to_broadcast([128, 8, 128]), ALU.mult, ALU.add, m)
                m_ll = po.tt(Ll.rearrange("p (h s) -> p h s", h=8), L_.rearrange("p (h s) -> p h s", h=8),
                             lvl[:, 128:256].unsqueeze(1).to_broadcast([128, 8, 128]), ALU.mult, use.get("Ll"))
                b, free = ab2.next()
                pe.wait(free, m_x)
                for h in range(8):
                    c = (h % 2) * 512 + (h // 2) * 128
                    d = pe.mm(Bk[b][:, 64 * h:64 * h + 64], XP[:, c:c + 128], VT[:, t, 64 * h:64 * h + 64], True, True, inc=(h == 7))
                m_xv = bank_free[b] = ac.act(Xv, Bk[b], ACT.Copy, d, use.get("Xv"))
                use["XP"] = d
                m_ab = products(BET, RHO, AB[z], incl, True, g)
                m_ak = products(KHT, RHO, AK[z], incl, False, g)
                use["feat"] = pe.last
                mtt = []
                for q in range(2):
                    b, free = ab2.next()
                    pe.wait(free, m_t)
                    for j in range(4):
                        d = pe.tr(Bk[b][:, 128 * j:128 * j + 128], pj(T_)[:, q, j, :], ident, inc=(j == 3))
                    m = ac.act(pj(Tt)[:, q], b3(b), ACT.Copy, d, use.get("Tt"))
                    bank_free[b] = m
                    mtt.append(m)
                yield
                for l in range(1, 6):
                    mx = []
                    for q in range(2):
                        b, free = ab2.next()
                        pe.wait(free, m_ll, mtt[q])
                        for j in range(4):
                            d = pe.mm(Bk[b][:, 128 * j:128 * j + 128], pj(Ll)[:, q, j, :], pj(Tt)[:, q, j, :], True, True, inc=(j == 3))
                        m = ac.act(pj(XP)[:, q], b3(b), ACT.Copy, d, use["XP"])
                        bank_free[b] = m
                        mx.append(m)
                    if l < 5:
                        m_ll = po.tt(Ll.rearrange("p (h s) -> p h s", h=8), L_.rearrange("p (h s) -> p h s", h=8),
                                     lvl[:, 128 * l + 128:128 * l + 256].unsqueeze(1).to_broadcast([128, 8, 128]), ALU.mult, d)
                    nt = []
                    for q in range(2):
                        b, free = ab2.next()
                        pe.wait(free, mx[q], m_t if l == 1 else mt_[q])
                        for j in range(4):
                            d = pe.mm(Bk[b][:, 128 * j:128 * j + 128], pj(T_)[:, q, j, :], pj(XP)[:, q, j, :], True, True, inc=(j == 3))
                        m = ve.tt(pj(Tt)[:, q], pj(Tt)[:, q], b3(b), ALU.subtract, d, mtt[q])
                        bank_free[b] = m
                        nt.append(m)
                    use["XP"] = d
                    mtt = nt
                    if l < 5:
                        mt_ = []
                        for q in range(2):
                            b, free = ab2.next()
                            pe.wait(free, mtt[q])
                            for j in range(4):
                                d = pe.tr(Bk[b][:, 128 * j:128 * j + 128], pj(Tt)[:, q, j, :], ident, inc=(j == 3))
                            m = ac.act(pj(T_)[:, q], b3(b), ACT.Copy, d)
                            bank_free[b] = m
                            mt_.append(m)
                    else:
                        use["T"] = d
                        use["Ll"] = d
                        use["L"] = m_ll
                    yield
                b, free = ab2.next()
                pe.wait(free, m_tok, mtt)
                for h in range(8):
                    q, j = h % 2, h // 2
                    d = pe.mm(Bk[b][64 * q:64 * q + 64, 128 * j:128 * j + 128], KTk[:, 64 * h:64 * h + 64], pj(Tt)[:, q, j, :],
                              True, True, inc=(h == 7))
                m_p = bank_free[b] = ac.act(PT[z], Bk[b], ACT.Copy, d, g)
                use["ktk"] = d
                b, free = ab2.next()
                pe.wait(free, m_xv)
                for h in range(8):
                    q, j = h % 2, h // 2
                    d = pe.mm(Bk[b][:, 64 * h:64 * h + 64], pj(Tt)[:, q, j, :], Xv[:, 64 * h:64 * h + 64], True, True, inc=(h == 7))
                m_q = bank_free[b] = ac.act(QS[z], Bk[b], ACT.Copy, d, g)
                use["Tt"] = use["Xv"] = d
                use[("ready", t)] = [m_p, m_q, m_ab, m_ak, m_tok]

            WC3 = WC.rearrange("p (k c) -> p k c", k=4)
            chain = {"s": m_s0}

            def chain_tile(t):
                z = t % 2
                rdy = use[("ready", t)]
                um = []
                for c in range(2):
                    n = 2 * t + c
                    o = 64 * c
                    Sn, Sx = SH[n % 4], SH[(n + 1) % 4]
                    bs = []
                    for q in range(2):
                        b, free = cb2.next()
                        pe.wait(free, chain["s"], rdy)
                        for j in range(4):
                            d = pe.mm(Bk[b][o:o + 64, 64 * j:64 * j + 64], PT[z][64 * q:64 * q + 64, 128 * j + o:128 * j + o + 64],
                                      Sn[64 * q:64 * q + 64, 64 * j:64 * j + 64], True, True, inc=(j == 3))
                        m = ve.tt(U_[o:o + 64, :].rearrange("p (j q d) -> p q j d", j=4, q=2)[:, q],
                                  Bk[b][o:o + 64, 0:256].rearrange("p (j d) -> p j d", j=4),
                                  QS[z][o:o + 64, :].rearrange("p (j q d) -> p q j d", j=4, q=2)[:, q], ALU.add, d, use.get("U"))
                        bank_free[b] = m
                    um.append(m)
                    yield
                    b, free = cb2.next()
                    pe.wait(free, m)
                    for h in range(8):
                        q, j = h % 2, h // 2
                        ov = Bk[b][64 * q:64 * q + 64, 64 * j:64 * j + 64]
                        pe.mm(ov, NB[z][o:o + 64, 64 * h:64 * h + 64], U_[o:o + 64, 64 * h:64 * h + 64], True, False)
                        d = pe.mm(ov, KH[z][o:o + 64, 64 * h:64 * h + 64], VT[o:o + 64, t, 64 * h:64 * h + 64], False, True, inc=(h == 7))
                    m = ve.tt(Sx, Bk[b][:, 0:256], Sn, ALU.add, d, use.get(("y", t - 2)), chain["s"])
                    bank_free[b] = m
                    chain["s"] = ve.tt(Sx.rearrange("p (j d) -> p j d", j=4), Sx.rearrange("p (j d) -> p j d", j=4),
                                       bc(WC3[:, :, n], 64), ALU.mult, m)
                    yield
                ym = []
                for q in range(2):
                    b, free = cb2.next()
                    pe.wait(free, um)
                    for j in range(4):
                        h = 2 * j + q
                        ov = Bk[b][:, 64 * j:64 * j + 64]
                        pe.mm(ov, pj(AK[z])[:, q, j, :], VT[:, t, 64 * h:64 * h + 64], True, False)
                        pe.mm(ov, pj(AB[z])[:, q, j, :], U_[:, 64 * h:64 * h + 64], False, False)
                        for c in range(2):
                            o = 64 * c
                            d = pe.mm(Bk[b][o:o + 64, 64 * j:64 * j + 64], RHO[64 * q:64 * q + 64, j, 128 * t + o:128 * t + o + 64],
                                      SH[(2 * t + c) % 4][64 * q:64 * q + 64, 64 * j:64 * j + 64], False, True, inc=(j == 3 and c == 1))
                    m = ac.act(YB.rearrange("p (j q d) -> p q j d", j=4, q=2)[:, q], Bk[b][:, 0:256].rearrange("p (j d) -> p j d", j=4),
                               ACT.Copy, d, use.get("YB"))
                    bank_free[b] = m
                    ym.append(m)
                use["U"] = use[("y", t)] = d
                use[("tile", t)] = [d]
                yield
                y3 = YB.rearrange("p (h d) -> p h d", h=8)
                s1, s2 = stat(8), stat(8)
                m = ve.red(s1, y3, ALU.add, ym)
                m = ve.ts(s1, s1, 1.0 / 64, ALU.mult, None, None, m)
                m = ve.tt(y3, y3, bc(s1, 64), ALU.subtract, m)
                y2 = Y2.rearrange("p (h d) -> p h d", h=8)
                m = po.tt(Y2, YB, YB, ALU.mult, m, use.get("Y2"))
                m = ve.red(s2, y2, ALU.add, m)
                m = rstd(s2, 8, 1.0 / 64, GN_EPS, m)
                m = ve.tt(y3, y3, bc(s2, 64), ALU.mult, m)
                m = po.tt(YB, YB, GW, ALU.mult, m, c_gn)
                m = po.tt(YB, YB, GB, ALU.add, m)
                m2 = ve.tt(y2, VT[:, t, :].rearrange("p (h d) -> p h d", h=8), bc(bon[:, 8 * t:8 * t + 8], 64), ALU.mult)
                m = po.tt(YB, YB, Y2, ALU.add, m, m2)
                b, free = cb2.next()
                mk = pe.mm(Bk[b], XG[0:96, 128 * t:128 * t + 128], UPS[0:96, :], True, True, free, c_g, inc=True)
                m = ve.tt(Y3, YB, Bk[b], ALU.mult, m, mk, use.get("Y3"))
                bank_free[b] = use["YB"] = use["Y2"] = m
                yield
                marks, d = transposed(Y3, 4, MR, t, m, cb2)
                use["Y3"] = d

            for t in range(9):
                A_ = prep(t) if t < 8 else iter(())
                B_ = chain_tile(t - 1) if t >= 1 else iter(())
                live = [A_, B_]
                while live:
                    live = [x for x in live if next(x, "end") != "end"]
            PH = all_wait()
            W.free[2] = [W.free[2]] + PH
            W.free[2] = PH

            MA = R[:, 4096:8192].rearrange("p (c s) -> p c s", c=4)
            m_ma = cload(R[:, 4096:8192], md, *PH, m_mix)
            X2 = R[:, 16384:24576].rearrange("p (t d) -> p t d", t=8)
            xd3 = xd.rearrange("p (t d) -> p t d", t=8)
            m_xl = [cload(X2[:, 2 * j:2 * j + 2, :], xd3[:, 2 * j:2 * j + 2, :], *PH, m_x1) for j in range(4)]
            GP = R[:, 24576:25600]
            m_gp = cload(GP, bass_rows(a["norm_mix_post_2"], 128), *PH)
            MX = R[:, 8192:16384].rearrange("p (t d) -> p t d", t=8)

            def mixsrc(k, sl_):
                return MA[:, k, sl_] if k < 4 else MR[:, k - 4, sl_]

            def post_norm(Y, X, G, mG, ready, junk, done=None):
                ss = stat(8)
                m = None
                for t in range(8):
                    m = ac.act(junk, Y[:, t, :], ACT.Square, m, ready, acc=ss[:, t:t + 1])
                m = rstd(ss, 8, 1.0 / D, EPS, m)
                for t in range(8):
                    m1 = ve.stt(Y[:, t, :], Y[:, t, :], ss[:, t:t + 1], G, ALU.mult, ALU.mult, m, mG)
                    m2 = ve.tt(X[:, t, :], X[:, t, :], Y[:, t, :], ALU.add, m1)
                    if done:
                        done(t, m2)

            for c in range(2):
                i, v, m = slab(a["w_out_2"][0], 512 * c, 512)
                for t in range(8):
                    b, free = allb.next()
                    mk = gemm(b, free, 512, lambda k: mixsrc(k, slice(128 * t, 128 * t + 128)), lambda k: v[:, k, :], 8, m, m_ma)
                    bank_free[b] = ac.act(MX[:, t, 512 * c:512 * c + 512], Bk[b], ACT.Copy, mk)
                W.free[i] = mk
            ve.wait(m_xl)
            post_norm(MX, X2, GP, m_gp, ac.last, R[:, 25600:26624])
            PH = all_wait()
            norm_T(X2, g_ffn, [R[:, 0:1024], R[:, 1024:2048], R[:, 2048:3072]])
            PH = all_wait()
            m_gp = cload(GP, bass_rows(a["norm_ffn_post_2"], 128), *PH)
            FO = MX
            ub = Ring([R[:, 0:4096], R[:, 4096:8192]])
            fm = [[None, None] for _ in range(8)]
            for g in range(8):
                i, v, m = slab(a["w_ffn_up_2"][0], 512 * g, 512)
                ui, ubuf, uf = ub.next()
                u3 = ubuf.rearrange("p (c s) -> p c s", c=4)
                um = []
                for c in range(4):
                    def relu2(s_, b, mk):
                        dst = u3[:, c, 512 * s_:512 * s_ + 512]
                        m = ac.act(dst, Bk[b], ACT.Relu, mk, uf)
                        um.append(po.tt(dst, dst, dst, ALU.mult, m))
                        return m
                    W.free[i] = gemm_feat(v, m, ht3, 128 * c, 128, 8, relu2)
                i, v, m = slab(a["w_ffn_down_2"][0], 0, 1024, k0=4 * g, K=4)
                for t in range(8):
                    for c in range(2):
                        b, free = allb.next()
                        mk = gemm(b, free, 512, lambda k: u3[:, k, 128 * t:128 * t + 128], lambda k: v[:, k, 512 * c:512 * c + 512], 4, m, um)
                        dst = FO[:, t, 512 * c:512 * c + 512]
                        if g == 0:
                            fm[t][c] = ve.copy(dst, Bk[b], mk)
                        else:
                            fm[t][c] = ve.tt(dst, Bk[b], dst, ALU.add, mk, fm[t][c])
                        bank_free[b] = fm[t][c]
                W.free[i] = ub.free[ui] = mk
            osrc = out.rearrange("b (t p) d -> p (b t) d", p=128)
            post_norm(FO, X2, GP, m_gp, ve.last, R[:, 25600:26624], lambda t, m: odma.go(osrc[:, t, :], X2[:, t, :], m))



        block1()
        block2()
        finish_up(nc, queues)


def bass_rows(row, n):
    return row.to_broadcast([n, row.shape[1]])


def finish_up(nc, L):
    sp, po, pe, ve, ac = L["sp"], L["po"], L["pe"], L["ve"], L["ac"]
    sp.wait(*L["odma"].all())
    sp.wait(*L["cdma"].all())
    sp.wait(*L["wdma"].all())
    with nc.Block() as block:
        block.sync(sp.emit)
        block.gpsimd(po.emit)
        block.scalar(ac.emit)
        block.tensor(pe.emit)
        block.vector(ve.emit)


def kernel(**inputs):
    import concourse.bacc as bacc
    from concourse.bass_utils import run_bass_kernel_spmd

    nc = bacc.Bacc("TRN2", target_bir_lowering=False, num_devices=1)
    arrays = {n: np.ascontiguousarray(v) for n, v in inputs.items() if np.asarray(v).size}
    for n, v in constants().items():
        arrays["c_" + n] = v
    aps = {n: nc.dram_tensor(n, v.shape, mybir.dt.from_np(v.dtype), kind="ExternalInput").ap() for n, v in arrays.items()}
    out = nc.dram_tensor("out", (1, S, D), F32, kind="ExternalOutput").ap()
    program(nc, aps, out)
    r = run_bass_kernel_spmd(nc, [arrays], core_ids=[0])
    return r.results[0]["out"]
```

```python
import concourse.bass as bass
from concourse import mybir
from concourse.alu_op_type import AluOpType as ALU
from contextlib import ExitStack
import math
import numpy as np

F32 = mybir.dt.float32
F32R = mybir.dt.float32r
I32 = mybir.dt.int32
ACT = mybir.ActivationFunctionType
AX = mybir.AxisListType

NT = 8
S = 1024
D = 1024
NEG = -1.0e30
EPS = 1e-6
GN_EPS = 64e-5
LAMBDA_INIT = 0.2
TWO_PI = 2.0 * math.pi


class Queue:

    def __init__(self, sem):
        self.sem, self.n, self.ops, self.seen = sem, 0, [], {}

    def wait(self, *marks):
        for m in marks:
            if m is None:
                continue
            if isinstance(m, list):
                self.wait(*m)
                continue
            s, v = m
            if self.seen.get(s.name, 0) < v:
                self.seen[s.name] = v
                self.ops.append(lambda e, s=s, v=v: e.wait_ge(s, v))

    def put(self, make, wait=(), inc=True):
        self.wait(*wait)
        if not inc:
            self.ops.append(make)
            return None
        self.n += 1
        self.ops.append(lambda e: make(e).then_inc(self.sem, 1))
        return (self.sem, self.n)

    @property
    def last(self):
        return (self.sem, self.n)

    def emit(self, e):
        for op in self.ops:
            op(e)

    def tt(self, out, a, b, op, *wait):
        return self.put(lambda e: e.tensor_tensor(out, a, b, op), wait)

    def ts(self, out, a, s1, op0, s2, op1, *wait):
        if op1 is None:
            return self.put(lambda e: e.tensor_scalar(out, a, s1, None, op0), wait)
        return self.put(lambda e: e.tensor_scalar(out, a, s1, s2, op0, op1), wait)

    def stt(self, out, a, s, b, op0, op1, *wait):
        return self.put(lambda e: e.scalar_tensor_tensor(out, a, s, b, op0, op1), wait)

    def copy(self, out, a, *wait):
        return self.put(lambda e: e.tensor_copy(out, a), wait)

    def recip(self, out, a, *wait):
        return self.put(lambda e: e.reciprocal(out, a), wait)

    def red(self, out, a, op, *wait):
        return self.put(lambda e: e.tensor_reduce(out, a, AX.X, op), wait)

    def act(self, out, a, f, *wait, bias=0.0, scale=1.0, acc=None):
        if acc is None:
            return self.put(lambda e: e.activation(out, a, f, bias=bias, scale=scale), wait)
        return self.put(lambda e: e.activation(out, a, f, bias=bias, scale=scale, accum_out=acc), wait)

    def mm(self, out, l, r, start, stop, *wait, inc=False):
        return self.put(lambda e: e.matmul(out, l, r, start=start, stop=stop), wait, inc)

    def tr(self, out, a, ident, *wait, inc=False):
        return self.put(lambda e: e.transpose(out, a, ident), wait, inc)


class Dma:

    def __init__(self, q, lanes):
        self.q, self.lanes, self.k = q, lanes, [0] * len(lanes)
        self.at = 0

    def go(self, out, in_, *wait, lane=None):
        if lane is None:
            lane = self.at
            self.at = (self.at + 1) % len(self.lanes)
        s = self.lanes[lane]
        if self.k[lane]:
            self.q.wait((s, 16 * self.k[lane]))
        self.q.wait(*wait)
        self.k[lane] += 1
        self.q.ops.append(lambda e: e.dma_start(out, in_).then_inc(s, 16))
        return (s, 16 * self.k[lane])

    def all(self):
        return [(s, 16 * k) for s, k in zip(self.lanes, self.k) if k]


class Ring:

    def __init__(self, bufs):
        self.bufs, self.free, self.i = bufs, [None] * len(bufs), -1

    def next(self):
        self.i = (self.i + 1) % len(self.bufs)
        return self.i, self.bufs[self.i], self.free[self.i]


def constants():
    f = np.float32
    c = {}
    c["ident"] = np.eye(128, dtype=f)
    q = np.arange(128)
    caus = np.zeros((128, 1024), f)
    caus[:, 896:] = np.where(q[None, :] <= q[:, None], 0.0, NEG)
    c["caus"] = caus
    dist = (q[:, None] + 896) - np.arange(1024)[None, :]
    cnt = ((dist >= 0) & (dist <= 128)).astype(int)
    cnt += (dist >= 0) & (dist % 4 == 0) & (dist <= 512)
    cnt += (dist >= 0) & (dist % 16 == 0)
    c["dil"] = np.where(cnt > 0, 8.0 * np.log(np.maximum(cnt, 1)), NEG).astype(f)
    same = (q[:, None] // 64) == (q[None, :] // 64)
    lv = []
    for l in range(6):
        m = 1 << l
        t, s_ = q[:, None], q[None, :]
        lv.append(((t // (2 * m) == s_ // (2 * m)) & ((t // m) % 2 == 1) & ((s_ // m) % 2 == 0)))
    c["lvl"] = np.concatenate([x.astype(f) for x in lv], 1)
    c["lvl0t"] = lv[0].T.astype(f)
    c["slow"] = (same & (q[:, None] > q[None, :])).astype(f)
    c["supt"] = (same & (q[None, :] > q[:, None])).astype(f)
    c["incl"] = (same & (q[None, :] >= q[:, None])).astype(f)
    c["bones"] = same.astype(f)
    hs = np.zeros((128, 2), f)
    hs[:64, 0] = 1
    hs[64:, 1] = 1
    c["hsel"] = hs
    rs = np.ones((128, 1024), f)
    rs[:, ::64] = 0
    c["reset"] = rs
    inv = (10000.0 ** (-np.arange(0, 64, 2, dtype=np.float64) / 64)).astype(f)
    c["invf"] = np.broadcast_to(inv, (128, 32)).copy()
    return c


def program(nc, a, out):
    ctx = ExitStack()
    with ctx, nc.allow_non_contiguous_dma(reason="small vectors onto partitions"):
        def place(name, n, parts=True):
            two = None
            if parts:
                with nc.sbuf_tensor(name + "r", [128, n], F32R) as two:
                    pass
            return ctx.enter_context(nc.sbuf_tensor(name, [128, n], F32)), two

        C, _ = place("C", 3848, False)
        RAWS, _ = place("RAWS", 3072, False)
        WF, WR = place("W", 12288)
        AF, AR = place("A", 16384)
        R, RR = place("R", 16504)
        PS = ctx.enter_context(nc.psum_tensor("PS", [128, 4096], F32))
        Bk = [PS[:, 512 * b:512 * b + 512] for b in range(8)]

        def sem(n):
            return ctx.enter_context(nc.semaphore(n))

        pe, ve, ac, po, sp = (Queue(sem(n)) for n in ("s_pe", "s_ve", "s_act", "s_pool", "s_sp"))
        NW = 3
        wdma = Dma(sp, [sem(f"s_w{i}") for i in range(NW)])
        cdma = Dma(sp, [sem(f"s_c{i}") for i in range(6)])
        odma = Dma(po, [sem(f"s_o{i}") for i in range(8)])

        def fence():
            return [q.last for q in (pe, ve, ac, po) if q.n]

        top = [0]

        def take(n):
            top[0] += n
            return C[:, top[0] - n:top[0]]

        ident = take(128)
        MASK = take(1024)
        lvl = take(768)
        lvl0t, slow, supt, incl, bones = (take(128) for _ in range(5))
        hsel = take(2)
        invf = take(32)
        trig = take(512)
        cosT, sinT = trig[:, 0:256], trig[:, 256:512]
        st = take(512)
        g_q, g_kv, g_sub = take(3), take(2), take(1)
        g_att = take(4)
        posi, posf = take(8), take(8)
        lamv = take(8)
        mu_c, w0_c, a0_c, kk_c, ka_c, rk_c = take(14), take(4), take(4), take(4), take(4), take(4)
        WC = take(64)
        bon = take(64)
        assert top[0] <= 3848
        AH = AR[:, 0:8192].rearrange("p (k s) -> p k s", k=8)
        AL = AR[:, 8192:16384].rearrange("p (k s) -> p k s", k=8)
        SB = AF[:, 8192:16384]

        def cload(dst, src, *wait):
            return cdma.go(dst, src, *wait)

        c_id = cload(ident, a["c_ident"])
        queues = dict(sp=sp, po=po, pe=pe, ve=ve, ac=ac, odma=odma, cdma=cdma, wdma=wdma)

        class Weights:

            def __init__(self):
                self.plan, self.have, self.made, self.used = [], [], 0, 0
                self.raws = [RAWS[:, 1024 * j:1024 * j + 1024] for j in range(3)]
                self.rawfree = [None] * 3
                self.raw_n, self.raw_i = 3, 0
                self.slots = 6
                self.slotfree = [None] * 6
                self.slot_i = 0
                self.held = [False] * 6

            def add(self, src, K, n, slots=6, raws=3):
                self.plan.append((src, K, n, slots, raws))

            def block(self, w, c0, n, k0=0, K=8, **kw):
                src = w[k0 * 128:(k0 + K) * 128, c0:c0 + n].rearrange("(k p) n -> p k n", p=128)
                self.add(src, K, n, **kw)

            def slab(self, w, c0):
                for j in range(4):
                    self.block(w, c0, 512, k0=2 * j, K=2)

            def pump(self, force=False):
                if self.made >= len(self.plan):
                    return False
                src, K, n, slots, raws = self.plan[self.made]
                if (slots, raws) != (self.slots, self.raw_n):
                    if self.used < self.made or any(self.held) or (slots > self.slots and not self.may_grow):
                        assert not force
                        return False
                    self.slots, self.raw_n, self.slot_i, self.raw_i = slots, raws, 0, 0
                if self.held[self.slot_i]:
                    assert not force
                    return False
                i, r = self.slot_i, self.raw_i
                self.slot_i, self.raw_i = (i + 1) % self.slots, (r + 1) % self.raw_n
                raw = self.raws[r][:, 0:K * n]
                mr = wdma.go(raw.rearrange("p (k n) -> p k n", k=K), src, self.rawfree[r], lane=r)
                o = 2048 * i
                hi, lo = WR[:, o:o + K * n], WR[:, o + 1024:o + 1024 + K * n]
                m1 = ac.act(hi, raw, ACT.Copy, mr, self.slotfree[i])
                m2 = ve.tt(lo, raw, hi.bitcast(F32), ALU.subtract, mr, m1)
                self.rawfree[r] = m2
                self.held[i] = True
                self.have.append((i, hi.rearrange("p (k n) -> p k n", k=K), lo.rearrange("p (k n) -> p k n", k=K), m2))
                self.made += 1
                return True

            may_grow = True

            def take(self):
                while self.made <= self.used:
                    self.pump(force=True)
                u = self.have[self.used]
                self.used += 1
                return u

            def done(self, u, mark):
                self.slotfree[u[0]] = mark
                self.held[u[0]] = False

            def take4(self):
                return [self.take() for _ in range(4)]

        W = Weights()

        class Banks:
            def __init__(self, ids):
                self.ids, self.i = ids, -1

            def next(self):
                self.i = (self.i + 1) % len(self.ids)
                b = self.ids[self.i]
                return b, bank_free[b]

        bank_free = [None] * 8
        allb = Banks(list(range(8)))

        def gemm(b, free, n, L, Rr, K, *wait, m=128):
            pe.wait(free, *wait)
            for k in range(K):
                mark = pe.mm(Bk[b][0:m, 0:n], L(k), Rr(k), k == 0, k == K - 1, inc=(k == K - 1))
            W.pump()
            return mark

        def gemm_tok(b, free, n, t, us, wait, last):
            pe.wait(free, *wait)
            tok = slice(128 * t, 128 * t + 128)
            for j, u in enumerate(us):
                pe.wait(u[3])
                for k in range(2):
                    e = j == 3 and k == 1
                    hi, lo = u[1][:, k, 0:n], u[2][:, k, 0:n]
                    pe.mm(Bk[b][:, 0:n], AH[:, 2 * j + k, tok], hi, j + k == 0, False)
                    pe.mm(Bk[b][:, 0:n], AH[:, 2 * j + k, tok], lo, False, False)
                    mark = pe.mm(Bk[b][:, 0:n], AL[:, 2 * j + k, tok], hi, False, e, inc=e or (last and k == 1))
                if last:
                    W.done(u, mark)
            W.pump()
            return mark

        def gemm_half(u, m, s_, evac, last=True):
            b, free = allb.next()
            pe.wait(u[3], free)
            tok = slice(512 * s_, 512 * s_ + 512)
            for k in range(8):
                hi, lo = u[1][:, k, 0:m], u[2][:, k, 0:m]
                pe.mm(Bk[b][0:m, :], hi, AH[:, k, tok], k == 0, False)
                pe.mm(Bk[b][0:m, :], hi, AL[:, k, tok], False, False)
                mk = pe.mm(Bk[b][0:m, :], lo, AH[:, k, tok], False, k == 7, inc=k == 7)
            if last:
                W.done(u, mk)
            bank_free[b] = evac(s_, b, mk)
            W.pump()
            return mk

        def gemm_feat(u, m, evac, wait=()):
            pe.wait(*wait)
            for s_ in range(2):
                mk = gemm_half(u, m, s_, evac, s_ == 1)
            return mk

        stn = [0]

        def stat(n):
            if stn[0] + n > 512:
                stn[0] = 0
            stn[0] += n
            return st[:, stn[0] - n:stn[0]]

        def bc(ap, n):
            return ap.unsqueeze(2).to_broadcast([ap.shape[0], ap.shape[1], n])

        def transposed(src, n, dst3, t, ready, banks, gain=None, lo=0):
            marks = []
            for j0 in range(0, n, 4):
                m = min(4, n - j0)
                b, free = banks.next()
                pe.wait(free, ready, c_id)
                for j in range(m):
                    d = pe.tr(Bk[b][:, 128 * j:128 * j + 128], src[:, (j0 + j) * 128:(j0 + j + 1) * 128],
                              ident, inc=(j == m - 1))
                o = dst3[:, lo + j0:lo + j0 + m, t * 128:(t + 1) * 128]
                p = Bk[b][:, 0:128 * m].rearrange("p (j s) -> p j s", j=m)
                if gain is None:
                    e = ac.act(o, p, ACT.Copy, d)
                else:
                    e = ve.tt(o, p, bc(gain[:, j0:j0 + m], 128), ALU.mult, d)
                bank_free[b] = e
                marks.append(e)
            return marks, d

        def transposed_parts(src, n, t, ready, banks, lo=0):
            for j0 in range(0, n, 4):
                m = min(4, n - j0)
                b, free = banks.next()
                pe.wait(free, ready, c_id)
                for j in range(m):
                    d = pe.tr(Bk[b][:, 128 * j:128 * j + 128], src[:, (j0 + j) * 128:(j0 + j + 1) * 128],
                              ident, inc=(j == m - 1))
                tok = slice(128 * t, 128 * t + 128)
                h_ = AH[:, lo + j0:lo + j0 + m, tok]
                p = Bk[b][:, 0:128 * m].rearrange("p (j s) -> p j s", j=m)
                e = ac.act(h_, p, ACT.Copy, d)
                bank_free[b] = ve.tt(AL[:, lo + j0:lo + j0 + m, tok], p, h_.bitcast(F32), ALU.subtract, e)
            return d

        def rstd(ss, n, inv_n, eps, *wait):
            m = ve.ts(ss, ss, inv_n, ALU.mult, eps, ALU.add, *wait)
            m = ac.act(ss, ss, ACT.Sqrt, m)
            return ve.recip(ss, ss, m)

        def all_wait():
            m = fence()
            for q in (pe, ve, ac, po):
                q.wait(*m)
            return m

        def attention(H, maps, score, v_of, dv, scale, finish, diff=None):
            PH = all_wait()
            pair = Ring([(0, 1), (2, 3)])
            slots = Ring([SB[:, 1024 * j:1024 * j + 1024] for j in range(6)])
            pts = Ring([SB[:, 6144:7168], SB[:, 7168:8192]])
            tb = Banks([4, 5])
            ob = Banks([6, 7])
            units = [(i, h) for i in range(8) for h in range(H)]
            state = {}

            def stage_a(u):
                i, h = u
                N = 128 * (i + 1)
                mx, nm, l, r = stat(maps), stat(maps), stat(maps), stat(maps)
                sl = []
                for m_ in range(maps):
                    pi, (b0, b1), pf = pair.next()
                    pe.wait(pf)
                    for n0 in range(0, N, 512):
                        n1 = min(N, n0 + 512)
                        parts = score(h, m_, i, n0, n1)
                        for k, (l_, r_) in enumerate(parts):
                            mk = pe.mm(PS[:, 512 * b0 + n0:512 * b0 + n1], l_, r_, k == 0, k == len(parts) - 1,
                                       inc=(k == len(parts) - 1 and n1 == N))
                    si, buf, sf = slots.next()
                    mt = ve.put(lambda e, buf=buf, b0=b0, m_=m_: e.tensor_tensor_reduce(
                        out=buf[:, 0:N], in0=PS[:, 512 * b0:512 * b0 + N], in1=MASK[:, 1024 - N:1024], scale=1.0,
                        scalar=-3.0e38, op0=ALU.add, op1=ALU.max, accum_out=mx[:, m_:m_ + 1]), [mk, sf])
                    pair.free[pi] = mt
                    sl.append((si, buf))
                mn = ve.ts(nm, mx, -scale, ALU.mult, None, None, mt)
                for m_ in range(maps):
                    buf = sl[m_][1]
                    me = ac.act(buf[:, 0:N], buf[:, 0:N], ACT.Exp, mn, bias=nm[:, m_:m_ + 1], scale=scale,
                                acc=l[:, m_:m_ + 1])
                if diff:
                    mr = ve.recip(r, l, me)
                    mr = ve.ts(r[:, 1:2], r[:, 1:2], lamv[:, 5:6], ALU.mult, None, None, mr, diff)
                    m2 = ve.ts(sl[1][1][:, 0:N], sl[1][1][:, 0:N], r[:, 1:2], ALU.mult, None, None, mr)
                    me = ve.stt(sl[0][1][:, 0:N], sl[0][1][:, 0:N], r[:, 0:1], sl[1][1][:, 0:N], ALU.mult, ALU.add, m2)
                    slots.free[sl[1][0]] = me
                    mr = None
                else:
                    mr = ve.recip(r, l, me)
                state[u] = (sl[0], me, r, mr)

            def stage_b(u):
                i, h = u
                (si, buf), me, r, mr = state[u]
                pi, pt, pf = pts.next()
                for j0 in range(0, i + 1, 4):
                    n = min(4, i + 1 - j0)
                    b, free = tb.next()
                    pe.wait(free, me)
                    for j in range(n):
                        d = pe.tr(Bk[b][:, 128 * j:128 * j + 128], buf[:, (j0 + j) * 128:(j0 + j + 1) * 128], ident,
                                  inc=(j == n - 1))
                    mc = ac.act(pt[:, 128 * j0:128 * (j0 + n)], Bk[b][:, 0:128 * n], ACT.Copy, d, pf)
                    bank_free[b] = mc
                slots.free[si] = d
                state[u] = (pi, pt, mc, r, mr)

            def stage_c(u):
                i, h = u
                pi, pt, mc, r, mr = state.pop(u)
                b, free = ob.next()
                pe.wait(free, mc)
                for j in range(i + 1):
                    d = pe.mm(Bk[b][:, 0:dv], pt[:, 128 * j:128 * j + 128], v_of(j, h), j == 0, j == i, inc=(j == i))
                pts.free[pi] = d
                bank_free[b] = finish(i, h, Bk[b][:, 0:dv], r, d)

            U = len(units)
            lag = 2 if maps == 2 else 4
            for s_ in range(U + lag + 1):
                if s_ < U:
                    stage_a(units[s_])
                if lag <= s_ < U + lag:
                    stage_b(units[s_ - lag])
                if s_ > lag:
                    stage_c(units[s_ - lag - 1])

        R0, R1, R2, R3 = (R[:, 4096 * j:4096 * j + 4096] for j in range(4))
        ALf = AR[:, 8192:16384].bitcast(F32)
        xd = nc.dram_tensor("x1_kept", [128, 8192], F32, kind="Internal").ap()
        od = nc.dram_tensor("odiff_kept", [128, 4096], F32, kind="Internal").ap()
        gd = nc.dram_tensor("merged_kept", [128, 4096], F32, kind="Internal").ap()
        hd = nc.dram_tensor("hlow_kept", [128, 8192], F32, kind="Internal").ap()
        vd = nc.dram_tensor("v_kept", [128, 4096], F32, kind="Internal").ap()
        md = nc.dram_tensor("mix_kept", [128, 4096], F32, kind="Internal").ap()

        later = []

        def flush():
            while later:
                later.pop(0)()

        def proj(us, n, each, wait=()):
            for t in range(8):
                b, free = allb.next()
                mk = gemm_tok(b, free, n, t, us, wait, t == 7)
                bank_free[b], post = each(t, b, mk)
                flush()
                if post:
                    later.append(post)

        def norm_T(X, grow, c_g, scratch, reads=()):
            ss = stat(8)
            jm = [bank_free[0], bank_free[1], bank_free[2], bank_free[3]]
            for t in range(8):
                o = 1024 * (t % 2)
                jm[2 * (t % 2)] = jm[2 * (t % 2) + 1] = ac.act(PS[:, o:o + 1024], X[t], ACT.Square, jm[2 * (t % 2)],
                                                              jm[2 * (t % 2) + 1], reads[t] if reads else None, acc=ss[:, t:t + 1])
            for b in range(4):
                bank_free[b] = jm[b]
            m = rstd(ss, 8, 1.0 / D, EPS, ac.last)
            xs = Ring(scratch)
            q = []
            for t in range(8):
                i, buf, free = xs.next()
                m1 = ve.stt(buf, X[t], ss[:, t:t + 1], grow, ALU.mult, ALU.mult, m, free, c_g)
                q.append((i, buf, m1, t))
                if t:
                    i, buf, m1, t_ = q.pop(0)
                    xs.free[i] = transposed_parts(buf, 8, t_, m1, allb)
            i, buf, m1, t_ = q.pop(0)
            transposed_parts(buf, 8, t_, m1, allb)

        def plan1():
            w_in = a["w_in"][0]
            for c0 in (0, 512, 1024):
                W.slab(w_in, c0)
            for c0, n in ((2048, 384), (2432, 320)):
                for j in range(4):
                    W.block(w_in, c0, n, k0=2 * j, K=2)
            for c0 in (1536, 2752, 3264, 4288, 3264 + 512, 4288 + 512):
                W.slab(w_in, c0)
            for c in range(2):
                W.slab(a["w_out"][0], 512 * c)

        def plan2():
            w1 = a["w_in_first_2"]
            for c in range(8):
                W.block(w1, 128 * c, 128)
            W.slab(w1, 1024)
            kw = dict(slots=2, raws=2)
            W.block(w1, 3072, 128, **kw)
            for p in range(4):
                for j in range(3):
                    W.block(w1, 1536 + 512 * j + 128 * p, 128, **kw)
            W.block(w1, 3136, 96, **kw)
            for c in range(2):
                W.slab(a["w_out_2"][0], 512 * c)
            up, down = a["w_ffn_up_2"][0], a["w_ffn_down_2"][0]
            for g in range(17):
                for j in range(2):
                    if g < 16:
                        W.block(up, 128 * (2 * g + j), 128)
                for j in range(2):
                    if g:
                        W.block(down, 0, 1024, k0=2 * g - 2 + j, K=1)

        def spill(dst, src, *wait):
            return odma.go(dst, src, *wait)

        def block1():
            xsrc = a["x"].rearrange("b (t p) d -> p (b t) d", p=128)
            xr = R[:, 0:8192].rearrange("p (t d) -> p t d", t=8)
            cx = [cload(xr[:, 2 * j:2 * j + 2, :], xsrc[:, 2 * j:2 * j + 2, :]) for j in range(4)]
            grow = R[:, 10240:11264]
            c_grow = cload(grow, bass_rows(a["norm_in"], 128))
            lrow = R[:, 14336:14592]
            for dst, src in (
                    (MASK, a["c_caus"]), (posi.bitcast(I32), a["positions"].rearrange("b (t p) -> p (b t)", p=128)),
                    (invf, a["c_invf"]), (g_q, a["mla_q_norm"].rearrange("l (k p) -> p (l k)", p=128)),
                    (g_kv, a["mla_kv_norm"].rearrange("l (k p) -> p (l k)", p=128)),
                    (g_sub, a["diff_subln"].rearrange("l (k p) -> p (l k)", p=128))):
                cload(dst, src)
            for j, n in enumerate(("diff_lambda_q1", "diff_lambda_k1", "diff_lambda_q2", "diff_lambda_k2")):
                cload(lrow[:, 64 * j:64 * j + 64], bass_rows(a[n], 128))
            c_small = cdma.all()
            norm_T([xr[:, t, :] for t in range(8)], grow, c_grow, [R[:, 8192:9216], R[:, 9216:10240]],
                   [cx[t // 2] for t in range(8)])

            m = ve.copy(posf, posi.bitcast(I32), c_small)
            tmpA, tmpB = R[:, 14592:14848], R[:, 14848:15104]
            pos3, inv3 = bc(posf, 32), invf.unsqueeze(1).to_broadcast([128, 8, 32])
            A3 = tmpA.rearrange("p (t f) -> p t f", t=8)
            m = ve.tt(A3, pos3, inv3, ALU.mult, m)
            MAGIC = 12582912.0
            m = ve.ts(tmpB, tmpA, 1.0 / TWO_PI, ALU.mult, MAGIC, ALU.add, m)
            m = ve.ts(tmpB, tmpB, MAGIC, ALU.subtract, None, None, m)
            c1 = 6.28125
            c2 = float(np.float32(np.floor((TWO_PI - c1) * 2 ** 21) / 2 ** 21))
            c3 = TWO_PI - c1 - c2
            for c_ in (c1, c2, c3):
                m = ve.stt(tmpA, tmpB, -c_, tmpA, ALU.mult, ALU.add, m)
            PI = 3.1415925
            m = ve.ts(tmpB, tmpA, math.pi / 2, ALU.add, None, None, m)
            m2 = ve.ts(cosT, tmpB, PI, ALU.is_gt, None, None, m)
            m2 = ve.stt(tmpB, cosT, -TWO_PI, tmpB, ALU.mult, ALU.add, m2)
            m2 = ve.ts(tmpB, tmpB, PI, ALU.min, -PI, ALU.max, m2)
            m = ve.ts(tmpA, tmpA, PI, ALU.min, -PI, ALU.max, m2)
            c_rope = [ac.act(cosT, tmpB, ACT.Sin, m), ac.act(sinT, tmpA, ACT.Sin, m)]
            cos3 = cosT.rearrange("p (t f) -> p t f", t=8)
            sin3 = sinT.rearrange("p (t f) -> p t f", t=8)

            m = ve.put(lambda e: e.tensor_tensor_reduce(out=lrow[:, 0:64], in0=lrow[:, 0:64], in1=lrow[:, 64:128], scale=1.0,
                       scalar=0.0, op0=ALU.mult, op1=ALU.add, accum_out=lamv[:, 0:1]), [c_small])
            m = ve.put(lambda e: e.tensor_tensor_reduce(out=lrow[:, 128:192], in0=lrow[:, 128:192], in1=lrow[:, 192:256], scale=1.0,
                       scalar=0.0, op0=ALU.mult, op1=ALU.add, accum_out=lamv[:, 1:2]), [])
            m = ac.act(lamv[:, 2:4], lamv[:, 0:2], ACT.Exp, m)
            m = ve.tt(lamv[:, 4:5], lamv[:, 3:4], lamv[:, 2:3], ALU.subtract, m)
            c_lam = ve.ts(lamv[:, 5:6], lamv[:, 4:5], -LAMBDA_INIT, ALU.add, None, None, m)
            PH = all_wait()
            m_h = spill(hd, ALf, *PH)

            rings = {}

            def rope_rings(base):
                rings["a"] = Ring([base[:, 0:512], base[:, 512:1024]])
                rings["b"] = Ring([base[:, 1024:1536], base[:, 1536:2048]])

            def rope(b, mark, t, groups, c0=0):
                n = groups * 64
                x4 = Bk[b][:, c0:c0 + n].rearrange("p (g h f) -> p g h f", g=groups, h=2)
                i1, b1, f1 = rings["a"].next()
                i2, b2, f2 = rings["b"].next()
                t1 = b1[:, 0:n].rearrange("p (g h f) -> p g h f", g=groups, h=2)
                t2 = b2[:, 0:n].rearrange("p (g h f) -> p g h f", g=groups, h=2)
                cb = cos3[:, t, :].unsqueeze(1).unsqueeze(1).to_broadcast([128, groups, 2, 32])
                sb_ = sin3[:, t, :].unsqueeze(1).unsqueeze(1).to_broadcast([128, groups, 2, 32])
                ve.tt(t1, x4, cb, ALU.mult, mark, c_rope, f1)
                m = ve.tt(t2, x4, sb_, ALU.mult, f2)
                po.tt(t1[:, :, 0, :], t1[:, :, 0, :], t2[:, :, 1, :], ALU.subtract, m)
                m2 = po.tt(t1[:, :, 1, :], t1[:, :, 1, :], t2[:, :, 0, :], ALU.add)
                rings["b"].free[i2] = m2
                return i1, b1, m2, m

            def rope_into(dst3, groups):
                def each(t, b, mk):
                    i1, buf, m, free = rope(b, mk, t, groups)

                    def post():
                        _, rings["a"].free[i1] = transposed(buf, groups // 2, dst3, t, m, allb)
                    return free, post
                return each

            qT3 = R0.rearrange("p (c s) -> p c s", c=4)
            kT3 = R1.rearrange("p (c s) -> p c s", c=4)
            V3 = R2.rearrange("p (t d) -> p t d", t=8)
            rope_rings(R[:, 12288:14336])
            proj(W.take4(), 512, rope_into(qT3, 8))
            proj(W.take4(), 512, rope_into(kT3, 8))
            proj(W.take4(), 512, lambda t, b, mk: (ac.act(V3[:, t, :], Bk[b], ACT.Copy, mk), None))
            flush()
            for q in (pe, ve, ac, po):
                q.wait(m_h)

            def diff_score(h, m_, i, n0, n1):
                return [(qT3[64 * m_:64 * m_ + 64, h, 128 * i:128 * i + 128], kT3[64 * m_:64 * m_ + 64, h, n0:n1])]

            def o_place(i, h):
                return R0[:, h * 1024 + i * 128:h * 1024 + (i + 1) * 128]

            attention(4, 2, diff_score, lambda j, h: V3[:, j, 128 * h:128 * h + 128], 128, 0.125,
                      lambda i, h, p, r, d: ve.copy(o_place(i, h), p, d), diff=c_lam)
            PH = all_wait()
            m_al = cload(ALf, hd, *PH)
            ssd = stat(32)
            od3 = R0.rearrange("p (h t d) -> p h t d", h=4, t=8)
            sq = [R[:, 4096 + 1024 * h:5120 + 1024 * h].rearrange("p (t d) -> p t d", t=8) for h in range(4)]
            for h in range(4):
                m = po.tt(sq[h], od3[:, h], od3[:, h], ALU.mult)
                m = ve.red(ssd[:, 8 * h:8 * h + 8], sq[h], ALU.add, m)
            m = rstd(ssd, 32, 1.0 / 128, EPS, m)
            m = ve.ts(ssd, ssd, 1.0 - LAMBDA_INIT, ALU.mult, None, None, m)
            for h in range(4):
                m_od = ve.tt(od3[:, h], od3[:, h], bc(ssd[:, 8 * h:8 * h + 8], 128), ALU.mult, m)
            m_os = spill(od, R0, m_od)
            ac.wait(m_os, *PH)
            cqr = R[:, 0:3072].rearrange("p (t d) -> p t d", t=8)
            ckr = R[:, 3072:5120].rearrange("p (t d) -> p t d", t=8)
            qn3 = R0.rearrange("p (c s) -> p c s", c=4)
            kn3 = R1.rearrange("p (c s) -> p c s", c=4)
            mV3 = R2.rearrange("p (t d) -> p t d", t=8)
            wq3 = R[:, 8192:10496].rearrange("p (k n) -> p k n", k=3)
            wkv3 = R[:, 10496:12544].rearrange("p (k n) -> p k n", k=2)
            qr3 = R[:, 12544:14592].rearrange("p (c s) -> p c s", c=2)
            krT = R[:, 14592:15616]
            kr3 = krT.rearrange("p (c s) -> p c s", c=1)
            ssq, ssk = stat(8), stat(8)
            c_wq = cload(wq3, a["w_uq"][0].rearrange("(k p) n -> p k n", p=128), *PH)
            c_wkv = cload(wkv3, a["w_ukv"][0].rearrange("(k p) n -> p k n", p=128), *PH)
            junk = R[:, 11264 + 1280:11264 + 1280 + 384]
            junk = R[:, 15616:16000]
            ac.wait(m_od)
            rope_rings(R[:, 12544:14592])

            def cq_each(t, b, mk):
                ac.act(cqr[:, t, :], Bk[b][:, 0:384], ACT.Copy, mk)
                return ac.act(junk, Bk[b][:, 0:384], ACT.Square, ac.last, acc=ssq[:, t:t + 1]), None

            def ckv_each(t, b, mk):
                ac.act(ckr[:, t, :], Bk[b][:, 0:256], ACT.Copy, mk)
                m = ac.act(junk[:, 0:256], Bk[b][:, 0:256], ACT.Square, ac.last, acc=ssk[:, t:t + 1])
                i1, b1, f1 = rings["a"].next()
                i2, b2, f2 = rings["b"].next()
                x = Bk[b][:, 256:320].rearrange("p (h f) -> p h f", h=2)
                t1 = b1[:, 0:64].rearrange("p (h f) -> p h f", h=2)
                t2 = b2[:, 0:64].rearrange("p (h f) -> p h f", h=2)
                cb = cos3[:, t, :].unsqueeze(1).to_broadcast([128, 2, 32])
                sb_ = sin3[:, t, :].unsqueeze(1).to_broadcast([128, 2, 32])
                ve.tt(t1, x, cb, ALU.mult, m, f1)
                free = ve.tt(t2, x, sb_, ALU.mult, f2)
                po.tt(t1[:, 0, :], t1[:, 0, :], t2[:, 1, :], ALU.subtract, free)
                m = po.tt(t1[:, 1, :], t1[:, 1, :], t2[:, 0, :], ALU.add)
                m = po.copy(b1[:, 64:128], b1[:, 0:64], m)
                rings["b"].free[i2] = m

                def post():
                    _, rings["a"].free[i1] = transposed(b1, 1, kr3, t, m, allb)
                return free, post

            proj(W.take4(), 384, cq_each, wait=[m_al])
            proj(W.take4(), 320, ckv_each)
            flush()
            PH = all_wait()
            mq_ = rstd(ssq, 8, 1.0 / 384, EPS)
            mk_ = rstd(ssk, 8, 1.0 / 256, EPS)
            cqT = SB[:, 0:3072].rearrange("p (c s) -> p c s", c=3)
            ckT = SB[:, 3072:5120].rearrange("p (c s) -> p c s", c=2)
            tr_ = Ring([SB[:, 7168:7552], SB[:, 7552:7936]])
            q = []

            def tpost(buf, n, dst, t, m1, gain, i):
                def f():
                    _, tr_.free[i] = transposed(buf, n, dst, t, m1, allb, gain=gain)
                return f
            for t in range(8):
                i, buf, free = tr_.next()
                m1 = ve.ts(buf, cqr[:, t, :], ssq[:, t:t + 1], ALU.mult, None, None, mq_, free)
                tpost(buf, 3, cqT, t, m1, g_q, i)()
                i, buf, free = tr_.next()
                m1 = ve.ts(buf[:, 0:256], ckr[:, t, :], ssk[:, t:t + 1], ALU.mult, None, None, mk_, free)
                tpost(buf, 2, ckT, t, m1, g_kv, i)()
            PH = all_wait()
            rope_rings(SB[:, 5120:7168])
            for h in range(4):
                for s_ in range(2):
                    b, free = allb.next()
                    mk = gemm(b, free, 512, lambda k: wq3[:, k, 192 * h:192 * h + 128], lambda k: cqT[:, k, 512 * s_:512 * s_ + 512], 3, c_wq)
                    bank_free[b] = ac.act(qn3[:, h, 512 * s_:512 * s_ + 512], Bk[b], ACT.Copy, mk)
            vr = wq3.rearrange("p k (h c) -> p k h c", h=4)
            for t in range(8):
                b, free = allb.next()
                pe.wait(free)
                for h in range(4):
                    for k in range(3):
                        mk = pe.mm(Bk[b][:, 64 * h:64 * h + 64], cqT[:, k, 128 * t:128 * t + 128], vr[:, k, h, 128:192],
                                   k == 0, k == 2, inc=(k == 2 and h == 3))
                i1, buf, m1, free = rope(b, mk, t, 4)
                bank_free[b] = free
                flush()

                def post(i1=i1, buf=buf, t=t, m1=m1):
                    _, rings["a"].free[i1] = transposed(buf, 2, qr3, t, m1, allb)
                later.append(post)
            for h in range(4):
                for s_ in range(2):
                    b, free = allb.next()
                    mk = gemm(b, free, 512, lambda k: wkv3[:, k, 256 * h:256 * h + 128], lambda k: ckT[:, k, 512 * s_:512 * s_ + 512], 2, c_wkv)
                    bank_free[b] = ac.act(kn3[:, h, 512 * s_:512 * s_ + 512], Bk[b], ACT.Copy, mk)
                if h == 0:
                    flush()
            vr2 = wkv3.rearrange("p k (h c) -> p k h c", h=4)
            mvA = []
            for t in range(8):
                b, free = allb.next()
                pe.wait(free)
                for h in range(4):
                    for k in range(2):
                        mk = pe.mm(Bk[b][:, 128 * h:128 * h + 128], ckT[:, k, 128 * t:128 * t + 128], vr2[:, k, h, 128:256],
                                   k == 0, k == 1, inc=(k == 1 and h == 3))
                mvA.append(b)
            for t in range(8):
                bank_free[mvA[t]] = ac.act(mV3[:, t, :], Bk[mvA[t]], ACT.Copy, mk)

            def mla_score(h, m_, i, n0, n1):
                c, o = h // 2, 64 * (h % 2)
                return [(qn3[:, h, 128 * i:128 * i + 128], kn3[:, h, n0:n1]),
                        (qr3[o:o + 64, c, 128 * i:128 * i + 128], krT[o:o + 64, n0:n1])]

            attention(4, 1, mla_score, lambda j, h: mV3[:, j, 128 * h:128 * h + 128], 128, 192.0 ** -0.5,
                      lambda i, h, p, r, d: ve.ts(o_place(i, h), p, r[:, 0:1], ALU.mult, None, None, d))

            PH = all_wait()
            m_al = [cload(ALf[:, 2048 * j:2048 * j + 2048], hd[:, 2048 * j:2048 * j + 2048], *PH) for j in range(4)]
            m_od = cload(R1, od, *PH, m_os)
            oT = [R2.rearrange("p (c s) -> p c s", c=4), R3.rearrange("p (c s) -> p c s", c=4)]
            gb = Ring([MASK[:, 0:512], MASK[:, 512:1024]])
            gsub = g_sub.to_broadcast([128, 4])

            def gate_each(reg, dst, gain, got=None):
                r4 = reg.rearrange("p (h t d) -> p h t d", h=4, t=8)

                def each(t, b, mk):
                    gi, buf, gf = gb.next()
                    m = ac.act(buf, Bk[b], ACT.Silu, mk, gf)
                    b4 = buf.rearrange("p (h d) -> p h d", h=4)
                    m2 = po.tt(b4, b4, r4[:, :, t, :], ALU.mult, m, got)

                    def post():
                        _, gb.free[gi] = transposed(buf, 4, dst, t, m2, allb, gain=gain)
                    return m, post
                return each

            proj(W.take4(), 512, gate_each(R1, oT[0], gsub, m_od), wait=m_al)
            proj(W.take4(), 512, gate_each(R0, oT[1], None))
            flush()
            PH = all_wait()
            MG = R[:, 0:4096].rearrange("p (t d) -> p t d", t=8)
            gd3 = gd.rearrange("p (t d) -> p t d", t=8)
            WP = [R[:, 4096:6144].rearrange("p (k n) -> p k n", k=4), R[:, 6144:8192].rearrange("p (k n) -> p k n", k=4)]
            g1 = Ring([MASK[:, 0:512], MASK[:, 512:1024]])
            wpfree = [None, None]
            kept = [None] * 8
            for c in range(2):
                for kind, wp in enumerate(("w_proj_diff", "w_proj_mla")):
                    o_ = oT[kind]
                    mp = cload(WP[kind], a[wp][0][:, 512 * c:512 * c + 512].rearrange("(k p) n -> p k n", p=128), *PH, wpfree[kind])
                    us = W.take4()
                    for t in range(8):
                        b, free = allb.next()
                        mk = gemm_tok(b, free, 512, t, us, [], t == 7)
                        gi, buf, gf = g1.next()
                        m = ac.act(buf, Bk[b], ACT.Sigmoid, mk, gf)
                        bank_free[b] = m
                        b, free = allb.next()
                        mk = gemm(b, free, 512, lambda k: o_[:, k, 128 * t:128 * t + 128], lambda k: WP[kind][:, k, :], 4, mp)
                        if kind == 0:
                            m = ve.tt(MG[:, t, :], Bk[b], buf, ALU.mult, m, mk, kept[t])
                            bank_free[b] = m
                            g1.free[gi] = m
                        else:
                            m = ve.tt(buf, Bk[b], buf, ALU.mult, m, mk)
                            bank_free[b] = m
                            g1.free[gi] = m = po.tt(MG[:, t, :], MG[:, t, :], buf, ALU.add, m)
                            if c == 0:
                                kept[t] = spill(gd3[:, t, :], MG[:, t, :], m)
                    wpfree[kind] = mk
            PH = all_wait()
            M0 = R[:, 12288:16384].rearrange("p (t d) -> p t d", t=8)
            m_m0 = cload(R[:, 12288:16384], gd, *PH, kept)
            X1 = R[:, 4096:12288].rearrange("p (t d) -> p t d", t=8)
            cx = [cload(X1[:, 2 * j:2 * j + 2, :], xsrc[:, 2 * j:2 * j + 2, :], PH) for j in range(4)]
            gfin = MASK
            c_gf = cload(gfin, bass_rows(a["norm_final"].rearrange("(a n) -> a n", a=1), 128), PH)
            for t in range(8):
                transposed_parts(MG[:, t, :], 4, t, None, allb, lo=4)
            for t in range(8):
                transposed_parts(M0[:, t, :], 4, t, m_m0, allb)
            mT = fence()
            for c in range(2):
                us = W.take4()
                for t in range(8):
                    b, free = allb.next()
                    mk = gemm_tok(b, free, 512, t, us, mT, t == 7)
                    dst = X1[:, t, 512 * c:512 * c + 512]
                    bank_free[b] = ve.tt(dst, Bk[b], dst, ALU.add, mk, cx)
            ssf = stat(8)
            junk2 = [R[:, 0:1024], R[:, 1024:2048]]
            jm = [None, None]
            for t in range(8):
                jm[t % 2] = ac.act(junk2[t % 2], X1[:, t, :], ACT.Square, ve.last, jm[t % 2], acc=ssf[:, t:t + 1])
            m = rstd(ssf, 8, 1.0 / D, EPS, ac.last)
            for t in range(8):
                ve.stt(X1[:, t, :], X1[:, t, :], ssf[:, t:t + 1], gfin, ALU.mult, ALU.mult, m, c_gf)

        def vec_cols(name, c0, n):
            return a[name].rearrange("l n -> (l n)")[c0:c0 + n].rearrange("(k p) -> p k", p=128 if n >= 128 else n)

        def block2():
            X1f = R[:, 4096:12288]
            X1 = X1f.rearrange("p (t d) -> p t d", t=8)
            PH = all_wait()
            m_x1 = odma.go(xd, X1f, *PH)
            for dst, name, c0, n in (
                    (g_att, "attn_out_gain_2", 0, 512),
                    (mu_c[:, 0:12], "mu_shift_2", 0, 1536), (mu_c[0:64, 12:13], "mu_shift_2", 1536, 64),
                    (mu_c[0:96, 13:14], "mu_shift_2", 1600, 96), (w0_c, "decay_w0_2", 0, 512), (a0_c, "aaa_a0_2", 0, 512),
                    (kk_c, "k_k_2", 0, 512), (ka_c, "k_a_2", 0, 512)):
                cload(dst, vec_cols(name, c0, n))
            cload(rk_c, a["r_k_2"].rearrange("l (k h) c -> (h c) (l k)", h=2))
            for dst, name in ((lvl, "lvl"), (lvl0t, "lvl0t"), (slow, "slow"), (supt, "supt"), (incl, "incl"),
                              (bones, "bones"), (hsel, "hsel")):
                cload(dst, a["c_" + name])
            cload(MASK, a["c_dil"], *PH)
            C2 = cdma.all()
            w1 = a["w_in_first_2"]

            grow = R[:, 12288:13312]
            c_grow = cload(grow, bass_rows(a["norm_mix_pre_2"], 128), *PH)
            ve.wait(C2)
            norm_T([X1[:, t, :] for t in range(8)], grow, c_grow, [R[:, 0:1024], R[:, 1024:2048]])
            PH = all_wait()
            m_h = spill(hd, ALf, *PH)
            q2 = R[:, 0:8192].rearrange("p (c q s) -> p c q s", c=4, q=2)
            kT3 = R2.rearrange("p (c s) -> p c s", c=4)
            V3 = R3.rearrange("p (t d) -> p t d", t=8)
            ac.wait(m_x1)
            ve.wait(m_x1)
            po.put(lambda e: e.memset(q2[64:128, :, 0, :], 0.0), [m_x1])
            m_z = po.put(lambda e: e.memset(q2[0:64, :, 1, :], 0.0))

            def q_evac(s_, b, mk):
                tok = slice(512 * s_, 512 * s_ + 512)
                return [ac.act(q2[0:64, c, 0, tok], Bk[b][0:64, :], ACT.Copy, mk),
                        ve.copy(q2[64:128, c, 1, tok], Bk[b][64:128, :], mk)]
            for c in range(4):
                gemm_feat(W.take(), 128, q_evac)
            for c in range(4):
                gemm_feat(W.take(), 128, lambda s_, b, mk: ac.act(
                    kT3[:, c, 512 * s_:512 * s_ + 512], Bk[b], ACT.Copy, mk))
            proj(W.take4(), 512, lambda t, b, mk: (ac.act(V3[:, t, :], Bk[b], ACT.Copy, mk), None))
            for q in (pe, ve, ac, po):
                q.wait(m_h, m_z)

            def dil_score(h, m_, i, n0, n1):
                return [(q2[:, h // 2, h % 2, 128 * i:128 * i + 128], kT3[:, h // 2, n0:n1])]

            def dil_done(i, h, p, r, d):
                c = h * 1024 + i * 128
                return ve.ts(R[:, c:c + 64], p, r[:, 0:1], ALU.mult, None, None, d)

            attention(8, 1, dil_score, lambda j, h: V3[:, j, 64 * h:64 * h + 64], 64, 0.125, dil_done)
            PH = all_wait()
            m_reset = cload(MASK, a["c_reset"], *PH)
            m_al = cload(ALf, hd, *PH)
            SQ = R[:, 12288:13824]
            o4 = R[:, 0:8192].rearrange("p (c t d) -> p t c d", c=8, t=8)[:, :, :, 0:64]
            ssa = stat(8)
            jm = None
            for t in range(8):
                jm = ac.act(SQ[:, 0:512].rearrange("p (c d) -> p c d", c=8), o4[:, t], ACT.Square, jm, acc=ssa[:, t:t + 1])
            m = rstd(ssa, 8, 1.0 / 512, EPS, jm)
            mixA = R2.rearrange("p (c s) -> p c s", c=4)
            xs = Ring([SQ[:, 512:1024], SQ[:, 1024:1536]])
            for t in range(8):
                i, buf, free = xs.next()
                m1 = ve.ts(buf.rearrange("p (c d) -> p c d", c=8), o4[:, t], ssa[:, t:t + 1], ALU.mult, None, None, m, free)
                _, xs.free[i] = transposed(buf, 4, mixA, t, m1, allb, gain=g_att)
            PH = all_wait()
            m_mix = odma.go(md, R2, *PH)

            KAP, BET, KHT, RHO = (R[:, 4096 * j:4096 * j + 4096].rearrange("p (c s) -> p c s", c=4) for j in range(4))
            TR = WF[:, 4096:12288]
            T1 = RAWS[:, 2048:3072]
            T2, T3, T4 = (TR[:, 1024 * j:1024 * j + 1024] for j in range(3))
            LW = TR[:, 3072:4096]
            Zf = [TR[:, 4096:5128], TR[:, 5128:6160]]
            TS = TR[:, 6160:7184]
            UPS, UPW = TR[:, 7184:7696], trig
            W.may_grow = False
            XG = LW
            m_z0 = [ve.put(lambda e: e.memset(UPS, 0.0)), ve.put(lambda e: e.memset(UPW, 0.0)),
                    ve.put(lambda e: e.memset(LW[64:128, :], 0.0)),
                    ve.put(lambda e: e.memset(Zf[0][:, 0:8], 0.0)), ve.put(lambda e: e.memset(Zf[1][:, 0:8], 0.0))]
            c_up = [cload(UPW[0:32, :], a["decay_up_2"][0], *PH, m_z0), cload(UPS[32:64, :], a["aaa_up_2"][0])]
            halfsl = [slice(0, 512), slice(512, 1024)]
            zr = Ring(Zf)
            tsf = [None]

            def stream(cols, muc, dst, got):
                u = W.take()
                zi, zf, free = zr.next()
                zm = []

                def evac(s_, b, mk):
                    zm.append(ac.act(zf[0:cols, 8 + 512 * s_:520 + 512 * s_], Bk[b][0:cols, :], ACT.Copy, mk, free))
                    return zm[-1]
                gemm_half(u, 96 if cols == 96 else 128, 0, evac, False)
                yield
                gemm_half(u, 96 if cols == 96 else 128, 1, evac)
                z = zf[0:cols, 8:1032]
                m1 = po.tt(TS[0:cols, :], zf[0:cols, 7:1031], z, ALU.subtract, zm, m_z0, tsf[0])
                m2 = ve.stt(dst, TS[0:cols, :], muc, z, ALU.mult, ALU.add, m1)
                tsf[0] = zr.free[zi] = m2
                got.append((m2, zi, zf))
                yield

            pe.wait(m_al)
            got = []
            for _ in stream(64, mu_c[0:64, 12:13], LW[0:64, :], got):
                pass
            m_lw = ac.act(LW[0:32, :], LW[0:32, :], ACT.Tanh, got[0][0])
            vd3 = vd.rearrange("p (t d) -> p t d", t=8)
            m_vs = []
            ready = {}

            def streams(p):
                got = []
                for j, dst in ((0, RHO[:, p, :]), (1, KHT[:, p, :])):
                    if j:
                        ve.wait(m_mix)
                    yield from stream(128, mu_c[:, 4 * j + p:4 * j + p + 1], dst, got)
                ready[p] = [g[0] for g in got]
                yield from stream(128, mu_c[:, 8 + p:9 + p], TS, got)
                m, zi, zf = got[2]
                v3 = zf[:, 0:1024].rearrange("p (t d) -> p t d", t=8)
                em, tsf[0] = transposed(TS, 8, v3, 0, m, allb)
                m = spill(vd3[:, :, 128 * p:128 * p + 128], v3, em)
                m_vs.append(m)
                zr.free[zi] = m0 = ve.put(lambda e: e.memset(zf[:, 0:8], 0.0), [m])
                m_z0.append(m0)

            EL = [None]

            def elements(p):
                for q in (ve, ac, po):
                    q.wait(EL[0])
                r_, k_, b_, h_ = RHO[:, p, :], KAP[:, p, :], BET[:, p, :], KHT[:, p, :]
                ready_ = ready[p]

                def lora(up):
                    made = []
                    for s_ in range(2):
                        b, free = allb.next()
                        made.append((b, pe.mm(Bk[b], up[:, 128 * p:128 * p + 128], LW[:, halfsl[s_]], True, True,
                                              free, c_up, m_lw, m_z0, inc=True)))
                    return made

                def from_banks(made, dst, f, bias=0.0):
                    for s_, (b, mk) in enumerate(made):
                        bank_free[b] = ac.act(dst[:, halfsl[s_]], Bk[b], f, mk, bias=bias)
                    return ac.last
                pw, pa = lora(UPW), lora(UPS)
                m_kk = ve.ts(k_, h_, kk_c[:, p:p + 1], ALU.mult, None, None, ready_)
                m_sq = po.tt(b_, k_, k_, ALU.mult, m_kk)
                m_w = from_banks(pw, T3, ACT.Sigmoid, w0_c[:, p:p + 1])
                m_a = from_banks(pa, T2, ACT.Sigmoid, a0_c[:, p:p + 1])
                yield
                pn = []
                for s_ in range(2):
                    b, free = allb.next()
                    pn.append((b, pe.mm(Bk[b], bones, b_[:, halfsl[s_]], True, True, free, m_sq, inc=True)))
                mn_ = pe.last
                m = ve.ts(T3, T3, -math.exp(-0.5), ALU.mult, None, None, m_w)
                m_lc = ve.put(lambda e: e.tensor_tensor_scan(T1, MASK, T3, 0.0, ALU.mult, ALU.add), [m, m_reset])
                m_n = from_banks(pn, T4, ACT.Sqrt)
                m_t3 = ve.tt(T3, T1, T3, ALU.subtract, m_lc)
                yield
                m = ve.ts(T4, T4, 1e-12, ALU.max, None, None, m_n)
                m = ve.recip(T4[:, 0:512], T4[:, 0:512], m)
                yield
                m = ve.recip(T4[:, 512:1024], T4[:, 512:1024])
                m_kk = po.tt(k_, k_, T4, ALU.mult, m)
                m = ve.ts(T4, T2, -1.0, ALU.add, None, None, m_kk, m_a)
                m_e3 = ac.act(T3, T3, ACT.Exp, m_t3)
                yield
                m = ve.ts(T4, T4, ka_c[:, p:p + 1], ALU.mult, 1.0, ALU.add, m)
                m_km = ve.tt(h_, h_, T4, ALU.mult, m)
                m_b0 = ve.stt(b_, r_, rk_c[:, p:p + 1], h_, ALU.mult, ALU.mult, m_km, mn_)
                me = ac.act(T4, T1, ACT.Exp, m_km, m_lc)
                yield
                b, free = allb.next()
                pe.wait(free, m_b0)
                for t in range(8):
                    mb = pe.mm(Bk[b][:, 2 * t:2 * t + 2], b_[:, 128 * t:128 * t + 128], hsel, True, True, inc=(t == 7))
                m_r = ve.tt(r_, r_, T4, ALU.mult, me, m_b0)
                ve.copy(WC.rearrange("p (k c) -> p k c", k=4)[:, p, :], T4.rearrange("p (c n) -> p n c", n=64)[:, 63, :])
                m_b = po.tt(b_, k_, T2, ALU.mult, m_kk, m_a, mb)
                m_e2 = ac.act(T2, T1, ACT.Exp, m_b, scale=-1.0)
                m2 = po.tt(k_, k_, T3, ALU.mult, m_e3)
                yield
                bank_free[b] = ve.copy(bon.rearrange("p (t h) -> p t h", t=8)[:, :, 2 * p:2 * p + 2],
                                       Bk[b][:, 0:16].rearrange("p (t h) -> p t h", t=8), mb)
                m_h = ve.tt(h_, h_, T2, ALU.mult, m_e2, m_b0)
                m1 = po.tt(b_, b_, T2, ALU.mult, m_e2, m_b)
                EL[0] = [m1, m2, m_e3, m_h]

            for p in range(5):
                got = []
                S_ = streams(p) if p < 4 else stream(96, mu_c[0:96, 13:14], TS[0:96, :], got)
                E_ = elements(p - 1) if p else iter(())
                live = [S_, E_]
                while live:
                    live = [x for x in live if next(x, "end") != "end"]
            m_xg = ac.act(XG[0:96, :], TS[0:96, :], ACT.Sigmoid, got[0][0], pe.last)

            PH = all_wait()
            ac.wait(m_xg)
            c_gn = [cload(MASK[:, 0:512], bass_rows(a["gn_w_2"], 128), *PH),
                    cload(MASK[:, 512:1024], bass_rows(a["gn_b_2"], 128), *PH)]
            c_g = cload(UPS[0:96, :], a["gate_up_2"][0], *PH)
            GW, GB = MASK[:, 0:512], MASK[:, 512:1024]
            ab2 = Banks([0, 1, 2, 3])
            cb2 = Banks([4, 5, 6, 7])
            VT = AF[:, 0:4096].rearrange("p (t d) -> p t d", t=8)
            m_vt = cload(AF[:, 0:4096], vd, *PH, m_vs)
            pe.wait(m_vt)
            ve.wait(m_vt)
            spare = [AF[:, 4096 + 1024 * j:5120 + 1024 * j] for j in range(12)]
            Tt, T_, XP, Ll, L_ = spare[0:5]
            AB = [spare[5], spare[6]]
            AK = [spare[7], spare[8]]
            NB = [spare[9][:, 0:512], spare[9][:, 512:1024]]
            KH = [spare[10][:, 0:512], spare[10][:, 512:1024]]
            PT = [spare[11][:, 0:512], spare[11][:, 512:1024]]
            QS = [T2[:, 0:512], T2[:, 512:1024]]
            KTk, Xv = T3[:, 0:512], T3[:, 512:1024]
            SH = [T4[:, 256 * j:256 + 256 * j] for j in range(4)]
            YB, Y2 = T1[:, 0:512], T1[:, 512:1024]
            U_ = Zf[0][:, 0:512]
            Y3 = Zf[0][:, 512:1024]
            MR = R[:, 0:4096].rearrange("p (c s) -> p c s", c=4)
            m_s0 = ve.put(lambda e: e.memset(SH[0], 0.0))

            def pj(buf):
                return buf.rearrange("p (q j s) -> p q j s", q=2, j=4)

            def b3(b):
                return Bk[b].rearrange("p (j s) -> p j s", j=4)

            def mask3(mk_):
                return mk_.unsqueeze(1).to_broadcast([128, 4, 128])

            use = {}

            def prep(t):
                z = t % 2
                ts_ = slice(128 * t, 128 * t + 128)
                g = use.get(("tile", t - 2), [])
                for src, dst, sc in ((KAP, KTk, 1.0), (BET, NB[z], -1.0), (KHT, KH[z], 1.0)):
                    b, free = ab2.next()
                    pe.wait(free, c_id)
                    for p in range(4):
                        d = pe.tr(Bk[b][:, 128 * p:128 * p + 128], src[:, p, ts_], ident, inc=(p == 3))
                    bank_free[b] = ac.act(dst, Bk[b], ACT.Copy, d, g, use.get("ktk") if dst is KTk else None, scale=sc)
                m_tok = bank_free[b]

                def products(l3, r3, dst, mask, op_neg, *wait):
                    for q in range(2):
                        b, free = ab2.next()
                        pe.wait(free)
                        for j in range(4):
                            d = pe.mm(Bk[b][:, 128 * j:128 * j + 128], l3[64 * q:64 * q + 64, j, ts_],
                                      r3[64 * q:64 * q + 64, j, ts_], True, True, inc=(j == 3))
                        if op_neg:
                            m = ve.stt(pj(dst)[:, q], b3(b), -1.0, mask3(mask), ALU.mult, ALU.mult, d, *wait)
                        else:
                            m = ve.tt(pj(dst)[:, q], b3(b), mask3(mask), ALU.mult, d, *wait)
                        bank_free[b] = m
                    return m
                m_l = products(KAP, BET, L_, slow, False, use.get("L"))
                m_x = products(KHT, KAP, XP, supt, False, use.get("XP"))
                m = po.tt(T_.rearrange("p (h s) -> p h s", h=8), L_.rearrange("p (h s) -> p h s", h=8),
                          lvl[:, 0:128].unsqueeze(1).to_broadcast([128, 8, 128]), ALU.mult, m_l, use.get("T"))
                m_t = ve.stt(T_.rearrange("p (h s) -> p h s", h=8), T_.rearrange("p (h s) -> p h s", h=8), -1.0,
                             ident.unsqueeze(1).to_broadcast([128, 8, 128]), ALU.mult, ALU.add, m)
                m_ll = po.tt(Ll.rearrange("p (h s) -> p h s", h=8), L_.rearrange("p (h s) -> p h s", h=8),
                             lvl[:, 128:256].unsqueeze(1).to_broadcast([128, 8, 128]), ALU.mult, use.get("Ll"))
                b, free = ab2.next()
                pe.wait(free, m_x)
                for h in range(8):
                    c = (h % 2) * 512 + (h // 2) * 128
                    d = pe.mm(Bk[b][:, 64 * h:64 * h + 64], XP[:, c:c + 128], VT[:, t, 64 * h:64 * h + 64], True, True, inc=(h == 7))
                m_xv = bank_free[b] = ac.act(Xv, Bk[b], ACT.Copy, d, use.get("Xv"))
                use["XP"] = d
                m_ab = products(BET, RHO, AB[z], incl, True, g)
                m_ak = products(KHT, RHO, AK[z], incl, False, g)
                use["feat"] = pe.last
                mtt = []
                for q in range(2):
                    b, free = ab2.next()
                    pe.wait(free, m_t)
                    for j in range(4):
                        d = pe.tr(Bk[b][:, 128 * j:128 * j + 128], pj(T_)[:, q, j, :], ident, inc=(j == 3))
                    m = ac.act(pj(Tt)[:, q], b3(b), ACT.Copy, d, use.get("Tt"))
                    bank_free[b] = m
                    mtt.append(m)
                yield
                for l in range(1, 6):
                    mx = []
                    for q in range(2):
                        b, free = ab2.next()
                        pe.wait(free, m_ll, mtt[q])
                        for j in range(4):
                            d = pe.mm(Bk[b][:, 128 * j:128 * j + 128], pj(Ll)[:, q, j, :], pj(Tt)[:, q, j, :], True, True, inc=(j == 3))
                        m = ac.act(pj(XP)[:, q], b3(b), ACT.Copy, d, use["XP"])
                        bank_free[b] = m
                        mx.append(m)
                    if l < 5:
                        m_ll = po.tt(Ll.rearrange("p (h s) -> p h s", h=8), L_.rearrange("p (h s) -> p h s", h=8),
                                     lvl[:, 128 * l + 128:128 * l + 256].unsqueeze(1).to_broadcast([128, 8, 128]), ALU.mult, d)
                    nt = []
                    for q in range(2):
                        b, free = ab2.next()
                        pe.wait(free, mx[q], m_t if l == 1 else mt_[q])
                        for j in range(4):
                            d = pe.mm(Bk[b][:, 128 * j:128 * j + 128], pj(T_)[:, q, j, :], pj(XP)[:, q, j, :], True, True, inc=(j == 3))
                        m = ve.tt(pj(Tt)[:, q], pj(Tt)[:, q], b3(b), ALU.subtract, d, mtt[q])
                        bank_free[b] = m
                        nt.append(m)
                    use["XP"] = d
                    mtt = nt
                    if l < 5:
                        mt_ = []
                        for q in range(2):
                            b, free = ab2.next()
                            pe.wait(free, mtt[q])
                            for j in range(4):
                                d = pe.tr(Bk[b][:, 128 * j:128 * j + 128], pj(Tt)[:, q, j, :], ident, inc=(j == 3))
                            m = ac.act(pj(T_)[:, q], b3(b), ACT.Copy, d)
                            bank_free[b] = m
                            mt_.append(m)
                    else:
                        use["T"] = d
                        use["Ll"] = d
                        use["L"] = m_ll
                    yield
                b, free = ab2.next()
                pe.wait(free, m_tok, mtt)
                for h in range(8):
                    q, j = h % 2, h // 2
                    d = pe.mm(Bk[b][64 * q:64 * q + 64, 128 * j:128 * j + 128], KTk[:, 64 * h:64 * h + 64], pj(Tt)[:, q, j, :],
                              True, True, inc=(h == 7))
                m_p = bank_free[b] = ac.act(PT[z], Bk[b], ACT.Copy, d, g)
                use["ktk"] = d
                b, free = ab2.next()
                pe.wait(free, m_xv)
                for h in range(8):
                    q, j = h % 2, h // 2
                    d = pe.mm(Bk[b][:, 64 * h:64 * h + 64], pj(Tt)[:, q, j, :], Xv[:, 64 * h:64 * h + 64], True, True, inc=(h == 7))
                m_q = bank_free[b] = ac.act(QS[z], Bk[b], ACT.Copy, d, g)
                use["Tt"] = use["Xv"] = d
                use[("ready", t)] = [m_p, m_q, m_ab, m_ak, m_tok]

            WC3 = WC.rearrange("p (k c) -> p k c", k=4)
            chain = {"s": m_s0}

            def chain_tile(t):
                z = t % 2
                rdy = use[("ready", t)]
                um = []
                for c in range(2):
                    n = 2 * t + c
                    o = 64 * c
                    Sn, Sx = SH[n % 4], SH[(n + 1) % 4]
                    bs = []
                    for q in range(2):
                        b, free = cb2.next()
                        pe.wait(free, chain["s"], rdy)
                        for j in range(4):
                            d = pe.mm(Bk[b][o:o + 64, 64 * j:64 * j + 64], PT[z][64 * q:64 * q + 64, 128 * j + o:128 * j + o + 64],
                                      Sn[64 * q:64 * q + 64, 64 * j:64 * j + 64], True, True, inc=(j == 3))
                        m = ve.tt(U_[o:o + 64, :].rearrange("p (j q d) -> p q j d", j=4, q=2)[:, q],
                                  Bk[b][o:o + 64, 0:256].rearrange("p (j d) -> p j d", j=4),
                                  QS[z][o:o + 64, :].rearrange("p (j q d) -> p q j d", j=4, q=2)[:, q], ALU.add, d, use.get("U"))
                        bank_free[b] = m
                    um.append(m)
                    yield
                    b, free = cb2.next()
                    pe.wait(free, m)
                    for h in range(8):
                        q, j = h % 2, h // 2
                        ov = Bk[b][64 * q:64 * q + 64, 64 * j:64 * j + 64]
                        pe.mm(ov, NB[z][o:o + 64, 64 * h:64 * h + 64], U_[o:o + 64, 64 * h:64 * h + 64], True, False)
                        d = pe.mm(ov, KH[z][o:o + 64, 64 * h:64 * h + 64], VT[o:o + 64, t, 64 * h:64 * h + 64], False, True, inc=(h == 7))
                    m = ve.tt(Sx, Bk[b][:, 0:256], Sn, ALU.add, d, use.get(("y", t - 2)), chain["s"])
                    bank_free[b] = m
                    chain["s"] = ve.tt(Sx.rearrange("p (j d) -> p j d", j=4), Sx.rearrange("p (j d) -> p j d", j=4),
                                       bc(WC3[:, :, n], 64), ALU.mult, m)
                    yield
                ym = []
                for q in range(2):
                    b, free = cb2.next()
                    pe.wait(free, um)
                    for j in range(4):
                        h = 2 * j + q
                        ov = Bk[b][:, 64 * j:64 * j + 64]
                        pe.mm(ov, pj(AK[z])[:, q, j, :], VT[:, t, 64 * h:64 * h + 64], True, False)
                        pe.mm(ov, pj(AB[z])[:, q, j, :], U_[:, 64 * h:64 * h + 64], False, False)
                        for c in range(2):
                            o = 64 * c
                            d = pe.mm(Bk[b][o:o + 64, 64 * j:64 * j + 64], RHO[64 * q:64 * q + 64, j, 128 * t + o:128 * t + o + 64],
                                      SH[(2 * t + c) % 4][64 * q:64 * q + 64, 64 * j:64 * j + 64], False, True, inc=(j == 3 and c == 1))
                    m = ac.act(YB.rearrange("p (j q d) -> p q j d", j=4, q=2)[:, q], Bk[b][:, 0:256].rearrange("p (j d) -> p j d", j=4),
                               ACT.Copy, d, use.get("YB"))
                    bank_free[b] = m
                    ym.append(m)
                use["U"] = use[("y", t)] = d
                use[("tile", t)] = [d]
                yield
                y3 = YB.rearrange("p (h d) -> p h d", h=8)
                s1, s2 = stat(8), stat(8)
                m = ve.red(s1, y3, ALU.add, ym)
                m = ve.ts(s1, s1, 1.0 / 64, ALU.mult, None, None, m)
                m = ve.tt(y3, y3, bc(s1, 64), ALU.subtract, m)
                y2 = Y2.rearrange("p (h d) -> p h d", h=8)
                m = po.tt(Y2, YB, YB, ALU.mult, m, use.get("Y2"))
                m = ve.red(s2, y2, ALU.add, m)
                m = rstd(s2, 8, 1.0 / 64, GN_EPS, m)
                m = ve.tt(y3, y3, bc(s2, 64), ALU.mult, m)
                m = po.tt(YB, YB, GW, ALU.mult, m, c_gn)
                m = po.tt(YB, YB, GB, ALU.add, m)
                m2 = ve.tt(y2, VT[:, t, :].rearrange("p (h d) -> p h d", h=8), bc(bon[:, 8 * t:8 * t + 8], 64), ALU.mult)
                m = po.tt(YB, YB, Y2, ALU.add, m, m2)
                b, free = cb2.next()
                mk = pe.mm(Bk[b], XG[0:96, 128 * t:128 * t + 128], UPS[0:96, :], True, True, free, c_g, inc=True)
                m = ve.tt(Y3, YB, Bk[b], ALU.mult, m, mk, use.get("Y3"))
                bank_free[b] = use["YB"] = use["Y2"] = m
                yield
                marks, d = transposed(Y3, 4, MR, t, m, cb2)
                use["Y3"] = d

            for t in range(9):
                A_ = prep(t) if t < 8 else iter(())
                B_ = chain_tile(t - 1) if t >= 1 else iter(())
                live = [A_, B_]
                while live:
                    live = [x for x in live if next(x, "end") != "end"]
            PH = all_wait()
            W.may_grow = True
            W.slotfree = [PH] * 6
            W.rawfree[2] = PH

            MAf = R[:, 12288:16384]
            m_ma = cload(MAf, md, *PH, m_mix)
            GP = MASK
            m_gp = cload(GP, bass_rows(a["norm_mix_post_2"], 128), *PH)
            MX = R[:, 4096:12288].rearrange("p (t d) -> p t d", t=8)
            MA = MAf.rearrange("p (c s) -> p c s", c=4)
            m_parts = [None] * 8
            for k in (4, 5, 6, 7, 0, 1, 2, 3):
                src = MA[:, k, :] if k < 4 else MR[:, k - 4, :]
                m = ac.act(AH[:, k, :], src, ACT.Copy, m_ma if k < 4 else None)
                m_parts[k] = ve.tt(AL[:, k, :], src, AH[:, k, :].bitcast(F32), ALU.subtract, m, m_ma if k < 4 else None)
            X2 = [R[:, 1024 * t:1024 * t + 1024] if t < 4 else R[:, 8192 + 1024 * t:9216 + 1024 * t] for t in range(8)]
            xd3 = xd.rearrange("p (t d) -> p t d", t=8)
            m_xl = [cload(X2[t], xd3[:, t, :], m_parts, m_x1) for t in range(8)]

            def post_norm(Y, X, G, mG, ready, done=None):
                ss = stat(8)
                jm = [bank_free[b] for b in range(4)]
                for t in range(8):
                    o = t % 2
                    jm[2 * o] = jm[2 * o + 1] = ac.act(PS[:, 1024 * o:1024 * o + 1024], Y[:, t, :], ACT.Square, jm[2 * o], jm[2 * o + 1],
                                                       ready, acc=ss[:, t:t + 1])
                for b in range(4):
                    bank_free[b] = jm[b]
                m = rstd(ss, 8, 1.0 / D, EPS, ac.last)
                for t in range(8):
                    m1 = ve.stt(Y[:, t, :], Y[:, t, :], ss[:, t:t + 1], G, ALU.mult, ALU.mult, m, mG)
                    m2 = po.tt(X[t], X[t], Y[:, t, :], ALU.add, m1)
                    if done:
                        done(t, m2)

            for c in range(2):
                us = W.take4()
                for t in range(8):
                    b, free = allb.next()
                    mk = gemm_tok(b, free, 512, t, us, m_parts, t == 7)
                    bank_free[b] = ac.act(MX[:, t, 512 * c:512 * c + 512], Bk[b], ACT.Copy, mk)
            po.wait(m_xl)
            post_norm(MX, X2, GP, m_gp, ac.last)
            PH = all_wait()
            grow = R[:, 6144:7168]
            c_grow = cload(grow, bass_rows(a["norm_ffn_pre_2"], 128), *PH)
            m_gp = cload(GP, bass_rows(a["norm_ffn_post_2"], 128), *PH)
            m_x2 = [spill(xd3[:, t, :], X2[t], PH) for t in range(8)]
            norm_T(X2, grow, c_grow, [R[:, 4096:5120], R[:, 5120:6144]])
            PH = all_wait()
            FO = R[:, 8192:16384].rearrange("p (t d) -> p t d", t=8)
            ub = Ring([RR[:, 2048 * j:2048 * j + 2048] for j in range(4)])
            for q in (pe, ve, ac, po):
                q.wait(m_x2)
            rl = Ring([C[:, 1152:1664], C[:, 1664:2176]])
            fm = [[None, None] for _ in range(8)]
            groups = []

            def up(g):
                us = []
                for j in range(2):
                    ui, ubuf, uf = ub.next()
                    um = []

                    def relu2(s_, b, mk):
                        ri, rbuf, rf = rl.next()
                        hi = ubuf[:, 512 * s_:512 * s_ + 512]
                        lo = ubuf[:, 1024 + 512 * s_:1536 + 512 * s_]
                        m = ac.act(rbuf, Bk[b], ACT.Relu, mk, rf)
                        m1 = po.tt(rbuf, rbuf, rbuf, ALU.mult, m)
                        m2 = ac.act(hi, rbuf, ACT.Copy, m1, uf)
                        rl.free[ri] = m3 = ve.tt(lo, rbuf, hi.bitcast(F32), ALU.subtract, m2, uf)
                        um.append(m3)
                        return m
                    gemm_feat(W.take(), 128, relu2)
                    us.append((ui, ubuf, um))
                groups.append(us)

            def down(g):
                us = groups[g]
                ws = [W.take(), W.take()]
                for t in range(8):
                    for c in range(2):
                        b, free = allb.next()
                        pe.wait(free)
                        for j in range(2):
                            ui, ubuf, um = us[j]
                            pe.wait(um, ws[j][3])
                            uh, ul = ubuf[:, 128 * t:128 * t + 128], ubuf[:, 1024 + 128 * t:1152 + 128 * t]
                            wh, wl = ws[j][1][:, 0, 512 * c:512 * c + 512], ws[j][2][:, 0, 512 * c:512 * c + 512]
                            pe.mm(Bk[b], uh, wh, j == 0, False)
                            pe.mm(Bk[b], uh, wl, False, False)
                            last = t == 7 and c == 1
                            mk = pe.mm(Bk[b], ul, wh, False, j == 1, inc=j == 1 or last)
                            if last:
                                W.done(ws[j], mk)
                                ub.free[ui] = mk
                        dst = FO[:, t, 512 * c:512 * c + 512]
                        if g == 0:
                            fm[t][c] = ve.copy(dst, Bk[b], mk)
                        else:
                            fm[t][c] = ve.tt(dst, Bk[b], dst, ALU.add, mk, fm[t][c])
                        bank_free[b] = fm[t][c]
                        if t % 2:
                            W.pump()

            for g in range(17):
                if g < 16:
                    up(g)
                if g:
                    down(g - 1)
            PH = all_wait()
            X2 = [R[:, 1024 * t:1024 * t + 1024] for t in range(8)]
            m_xl = [cload(X2[t], xd3[:, t, :], PH, m_x2) for t in range(8)]
            po.wait(m_xl)
            osrc = out.rearrange("b (t p) d -> p (b t) d", p=128)
            post_norm(FO, X2, GP, m_gp, ve.last, lambda t, m: odma.go(osrc[:, t, :], X2[t], m))



        plan1()
        plan2()
        block1()
        block2()
        finish_up(nc, queues)


def bass_rows(row, n):
    return row.to_broadcast([n, row.shape[1]])


def finish_up(nc, L):
    sp, po, pe, ve, ac = L["sp"], L["po"], L["pe"], L["ve"], L["ac"]
    sp.wait(*L["odma"].all())
    sp.wait(*L["cdma"].all())
    sp.wait(*L["wdma"].all())
    with nc.Block() as block:
        block.sync(sp.emit)
        block.gpsimd(po.emit)
        block.scalar(ac.emit)
        block.tensor(pe.emit)
        block.vector(ve.emit)


def kernel(**inputs):
    import concourse.bacc as bacc
    from concourse.bass_utils import run_bass_kernel_spmd

    nc = bacc.Bacc("TRN2", target_bir_lowering=False, num_devices=1)
    arrays = {n: np.ascontiguousarray(v) for n, v in inputs.items() if np.asarray(v).size}
    for n, v in constants().items():
        arrays["c_" + n] = v
    aps = {n: nc.dram_tensor(n, v.shape, mybir.dt.from_np(v.dtype), kind="ExternalInput").ap() for n, v in arrays.items()}
    out = nc.dram_tensor("out", (1, S, D), F32, kind="ExternalOutput").ap()
    program(nc, aps, out)
    r = run_bass_kernel_spmd(nc, [arrays], core_ids=[0])
    return r.results[0]["out"]
```

```python
import concourse.bass as bass
from concourse import mybir
from concourse.alu_op_type import AluOpType as ALU
from contextlib import ExitStack
import math
import numpy as np

F32 = mybir.dt.float32
F32R = mybir.dt.float32r
I32 = mybir.dt.int32
ACT = mybir.ActivationFunctionType
AX = mybir.AxisListType

S = 1024
D = 1024
NEG = -1.0e30
EPS = 1e-6
GN_EPS = 64e-5
LAMBDA_INIT = 0.2
TWO_PI = 2.0 * math.pi


class Queue:

    def __init__(self, sem):
        self.sem, self.n, self.ops, self.seen = sem, 0, [], {}

    def wait(self, *marks):
        for m in marks:
            if m is None:
                continue
            if isinstance(m, list):
                self.wait(*m)
                continue
            s, v = m
            if self.seen.get(s.name, 0) < v:
                self.seen[s.name] = v
                self.ops.append(lambda e, s=s, v=v: e.wait_ge(s, v))

    def put(self, make, wait=(), inc=True):
        self.wait(*wait)
        if not inc:
            self.ops.append(make)
            return None
        self.n += 1
        self.ops.append(lambda e: make(e).then_inc(self.sem, 1))
        return (self.sem, self.n)

    @property
    def last(self):
        return (self.sem, self.n)

    def emit(self, e):
        for op in self.ops:
            op(e)

    def tt(self, out, a, b, op, *wait):
        return self.put(lambda e: e.tensor_tensor(out, a, b, op), wait)

    def ts(self, out, a, s1, op0, s2, op1, *wait):
        if op1 is None:
            return self.put(lambda e: e.tensor_scalar(out, a, s1, None, op0), wait)
        return self.put(lambda e: e.tensor_scalar(out, a, s1, s2, op0, op1), wait)

    def stt(self, out, a, s, b, op0, op1, *wait):
        return self.put(lambda e: e.scalar_tensor_tensor(out, a, s, b, op0, op1), wait)

    def copy(self, out, a, *wait):
        return self.put(lambda e: e.tensor_copy(out, a), wait)

    def recip(self, out, a, *wait):
        return self.put(lambda e: e.reciprocal(out, a), wait)

    def red(self, out, a, op, *wait):
        return self.put(lambda e: e.tensor_reduce(out, a, AX.X, op), wait)

    def act(self, out, a, f, *wait, bias=0.0, scale=1.0, acc=None):
        if acc is None:
            return self.put(lambda e: e.activation(out, a, f, bias=bias, scale=scale), wait)
        return self.put(lambda e: e.activation(out, a, f, bias=bias, scale=scale, accum_out=acc), wait)

    def mm(self, out, l, r, start, stop, *wait, inc=False):
        return self.put(lambda e: e.matmul(out, l, r, start=start, stop=stop), wait, inc)

    def tr(self, out, a, ident, *wait, inc=False):
        return self.put(lambda e: e.transpose(out, a, ident), wait, inc)


class Dma:

    def __init__(self, q, lanes):
        self.q, self.lanes, self.k = q, lanes, [0] * len(lanes)
        self.at = 0

    def go(self, out, in_, *wait, lane=None):
        if lane is None:
            lane = self.at
            self.at = (self.at + 1) % len(self.lanes)
        s = self.lanes[lane]
        if self.k[lane]:
            self.q.wait((s, 16 * self.k[lane]))
        self.q.wait(*wait)
        self.k[lane] += 1
        self.q.ops.append(lambda e: e.dma_start(out, in_).then_inc(s, 16))
        return (s, 16 * self.k[lane])

    def all(self):
        return [(s, 16 * k) for s, k in zip(self.lanes, self.k) if k]


class Ring:

    def __init__(self, bufs):
        self.bufs, self.free, self.i = bufs, [None] * len(bufs), -1

    def next(self):
        self.i = (self.i + 1) % len(self.bufs)
        return self.i, self.bufs[self.i], self.free[self.i]


def constants():
    f = np.float32
    c = {}
    c["ident"] = np.eye(128, dtype=f)
    q = np.arange(128)
    caus = np.zeros((128, 1024), f)
    caus[:, 896:] = np.where(q[None, :] <= q[:, None], 0.0, NEG)
    c["caus"] = caus
    dist = (q[:, None] + 896) - np.arange(1024)[None, :]
    cnt = ((dist >= 0) & (dist <= 128)).astype(int)
    cnt += (dist >= 0) & (dist % 4 == 0) & (dist <= 512)
    cnt += (dist >= 0) & (dist % 16 == 0)
    c["dil"] = np.where(cnt > 0, 8.0 * np.log(np.maximum(cnt, 1)), NEG).astype(f)
    same = (q[:, None] // 64) == (q[None, :] // 64)
    lv = []
    for l in range(6):
        m = 1 << l
        t, s_ = q[:, None], q[None, :]
        lv.append(((t // (2 * m) == s_ // (2 * m)) & ((t // m) % 2 == 1) & ((s_ // m) % 2 == 0)))
    c["lvl"] = np.concatenate([x.astype(f) for x in lv], 1)
    c["lvl0t"] = lv[0].T.astype(f)
    c["slow"] = (same & (q[:, None] > q[None, :])).astype(f)
    c["supt"] = (same & (q[None, :] > q[:, None])).astype(f)
    c["incl"] = (same & (q[None, :] >= q[:, None])).astype(f)
    c["bones"] = same.astype(f)
    hs = np.zeros((128, 2), f)
    hs[:64, 0] = 1
    hs[64:, 1] = 1
    c["hsel"] = hs
    rs = np.ones((128, 1024), f)
    rs[:, ::64] = 0
    c["reset"] = rs
    inv = (10000.0 ** (-np.arange(0, 64, 2, dtype=np.float64) / 64)).astype(f)
    c["invf"] = np.broadcast_to(inv, (128, 32)).copy()
    return c


def program(nc, a, out):
    ctx = ExitStack()
    with ctx, nc.allow_non_contiguous_dma(reason="small vectors onto partitions"):
        def place(name, n, parts=True):
            two = None
            if parts:
                with nc.sbuf_tensor(name + "r", [128, n], F32R) as two:
                    pass
            return ctx.enter_context(nc.sbuf_tensor(name, [128, n], F32)), two

        C, _ = place("C", 3848, False)
        RAWS, _ = place("RAWS", 3072, False)
        WF, WR = place("W", 12288)
        AF, AR = place("A", 16384)
        R, RR = place("R", 16504)
        PS = ctx.enter_context(nc.psum_tensor("PS", [128, 4096], F32))
        Bk = [PS[:, 512 * b:512 * b + 512] for b in range(8)]

        def sem(n):
            return ctx.enter_context(nc.semaphore(n))

        pe, ve, ac, po, sp = (Queue(sem(n)) for n in ("s_pe", "s_ve", "s_act", "s_pool", "s_sp"))
        NW = 3
        wdma = Dma(sp, [sem(f"s_w{i}") for i in range(NW)])
        cdma = Dma(sp, [sem(f"s_c{i}") for i in range(6)])
        odma = Dma(po, [sem(f"s_o{i}") for i in range(8)])

        def fence():
            return [q.last for q in (pe, ve, ac, po) if q.n]

        top = [0]

        def take(n):
            top[0] += n
            return C[:, top[0] - n:top[0]]

        ident = take(128)
        MASK = take(1024)
        lvl = take(768)
        lvl0t, slow, supt, incl, bones = (take(128) for _ in range(5))
        hsel = take(2)
        invf = take(32)
        trig = take(512)
        cosT, sinT = trig[:, 0:256], trig[:, 256:512]
        st = take(512)
        g_q, g_kv, g_sub = take(3), take(2), take(1)
        g_att = take(4)
        posi, posf = take(8), take(8)
        lamv = take(8)
        mu_c, w0_c, a0_c, kk_c, ka_c, rk_c = take(14), take(4), take(4), take(4), take(4), take(4)
        WC = take(64)
        bon = take(64)
        assert top[0] <= 3848
        AH = AR[:, 0:8192].rearrange("p (k s) -> p k s", k=8)
        AL = AR[:, 8192:16384].rearrange("p (k s) -> p k s", k=8)
        SB = AF[:, 8192:16384]

        def cload(dst, src, *wait):
            return cdma.go(dst, src, *wait)

        c_id = cload(ident, a["c_ident"])
        queues = dict(sp=sp, po=po, pe=pe, ve=ve, ac=ac, odma=odma, cdma=cdma, wdma=wdma)

        class Weights:

            def __init__(self):
                self.plan, self.have, self.made, self.used = [], [], 0, 0
                self.raws = [RAWS[:, 1024 * j:1024 * j + 1024] for j in range(3)]
                self.rawfree = [None] * 3
                self.raw_n, self.raw_i = 3, 0
                self.slots = 6
                self.slotfree = [None] * 6
                self.slot_i = 0
                self.held = [False] * 6

            def add(self, src, K, n, slots=6, raws=3):
                self.plan.append((src, K, n, slots, raws))

            def block(self, w, c0, n, k0=0, K=8, **kw):
                src = w[k0 * 128:(k0 + K) * 128, c0:c0 + n].rearrange("(k p) n -> p k n", p=128)
                self.add(src, K, n, **kw)

            def slab(self, w, c0):
                for j in range(4):
                    self.block(w, c0, 512, k0=2 * j, K=2)

            def pump(self, force=False):
                if self.made >= len(self.plan):
                    return False
                src, K, n, slots, raws = self.plan[self.made]
                if (slots, raws) != (self.slots, self.raw_n):
                    if slots > self.slots:
                        if not self.may_grow:
                            assert not force
                            return False
                        assert self.slot_i == 0
                        self.slots, self.raw_n, self.slot_i, self.raw_i = slots, raws, self.slots, self.raw_n
                    else:
                        if self.used < self.made or any(self.held):
                            assert not force
                            return False
                        self.slots, self.raw_n, self.slot_i, self.raw_i = slots, raws, 0, 0
                if self.held[self.slot_i]:
                    assert not force
                    return False
                i, r = self.slot_i, self.raw_i
                self.slot_i, self.raw_i = (i + 1) % self.slots, (r + 1) % self.raw_n
                raw = self.raws[r][:, 0:K * n]
                mr = wdma.go(raw.rearrange("p (k n) -> p k n", k=K), src, self.rawfree[r], lane=r)
                o = 2048 * i
                hi, lo = WR[:, o:o + K * n], WR[:, o + 1024:o + 1024 + K * n]
                m1 = ac.act(hi, raw, ACT.Copy, mr, self.slotfree[i])
                m2 = ve.tt(lo, raw, hi.bitcast(F32), ALU.subtract, mr, m1)
                self.rawfree[r] = m2
                self.held[i] = True
                self.have.append((i, hi.rearrange("p (k n) -> p k n", k=K), lo.rearrange("p (k n) -> p k n", k=K), m2))
                self.made += 1
                return True

            may_grow = True

            def take(self):
                while self.made <= self.used:
                    self.pump(force=True)
                u = self.have[self.used]
                self.used += 1
                return u

            def done(self, u, mark):
                self.slotfree[u[0]] = mark
                self.held[u[0]] = False

            def take4(self):
                return [self.take() for _ in range(4)]

        W = Weights()

        class Banks:
            def __init__(self, ids):
                self.ids, self.i = ids, -1

            def next(self):
                self.i = (self.i + 1) % len(self.ids)
                b = self.ids[self.i]
                return b, bank_free[b]

        bank_free = [None] * 8
        allb = Banks(list(range(8)))

        def gemm(b, free, n, L, Rr, K, *wait, m=128):
            pe.wait(free, *wait)
            for k in range(K):
                mark = pe.mm(Bk[b][0:m, 0:n], L(k), Rr(k), k == 0, k == K - 1, inc=(k == K - 1))
            W.pump()
            return mark

        def gemm_tok(b, free, n, t, us, wait, last):
            pe.wait(free, *wait)
            tok = slice(128 * t, 128 * t + 128)
            for j, u in enumerate(us):
                pe.wait(u[3])
                for k in range(2):
                    e = j == 3 and k == 1
                    hi, lo = u[1][:, k, 0:n], u[2][:, k, 0:n]
                    pe.mm(Bk[b][:, 0:n], AH[:, 2 * j + k, tok], hi, j + k == 0, False)
                    pe.mm(Bk[b][:, 0:n], AH[:, 2 * j + k, tok], lo, False, False)
                    mark = pe.mm(Bk[b][:, 0:n], AL[:, 2 * j + k, tok], hi, False, e, inc=e or (last and k == 1))
                if last:
                    W.done(u, mark)
            W.pump()
            return mark

        def gemm_half(u, m, s_, evac, last=True):
            b, free = allb.next()
            pe.wait(u[3], free)
            tok = slice(512 * s_, 512 * s_ + 512)
            for k in range(8):
                hi, lo = u[1][:, k, 0:m], u[2][:, k, 0:m]
                pe.mm(Bk[b][0:m, :], hi, AH[:, k, tok], k == 0, False)
                pe.mm(Bk[b][0:m, :], hi, AL[:, k, tok], False, False)
                mk = pe.mm(Bk[b][0:m, :], lo, AH[:, k, tok], False, k == 7, inc=k == 7)
            if last:
                W.done(u, mk)
            bank_free[b] = evac(s_, b, mk)
            W.pump()
            return mk

        def gemm_feat(u, m, evac, wait=()):
            pe.wait(*wait)
            for s_ in range(2):
                mk = gemm_half(u, m, s_, evac, s_ == 1)
            return mk

        stn = [0]

        def stat(n):
            if stn[0] + n > 512:
                stn[0] = 0
            stn[0] += n
            return st[:, stn[0] - n:stn[0]]

        def bc(ap, n):
            return ap.unsqueeze(2).to_broadcast([ap.shape[0], ap.shape[1], n])

        def transposed(src, n, dst3, t, ready, banks, gain=None, lo=0):
            marks = []
            for j0 in range(0, n, 4):
                m = min(4, n - j0)
                b, free = banks.next()
                pe.wait(free, ready, c_id)
                for j in range(m):
                    d = pe.tr(Bk[b][:, 128 * j:128 * j + 128], src[:, (j0 + j) * 128:(j0 + j + 1) * 128],
                              ident, inc=(j == m - 1))
                o = dst3[:, lo + j0:lo + j0 + m, t * 128:(t + 1) * 128]
                p = Bk[b][:, 0:128 * m].rearrange("p (j s) -> p j s", j=m)
                if gain is None:
                    e = ac.act(o, p, ACT.Copy, d)
                else:
                    e = ve.tt(o, p, bc(gain[:, j0:j0 + m], 128), ALU.mult, d)
                bank_free[b] = e
                marks.append(e)
            return marks, d

        def transposed_parts(src, n, t, ready, banks, lo=0, over=None):
            for j0 in range(0, n, 4):
                m = min(4, n - j0)
                b, free = banks.next()
                pe.wait(free, ready, c_id)
                for j in range(m):
                    d = pe.tr(Bk[b][:, 128 * j:128 * j + 128], src[:, (j0 + j) * 128:(j0 + j + 1) * 128],
                              ident, inc=(j == m - 1))
                tok = slice(128 * t, 128 * t + 128)
                h_ = AH[:, lo + j0:lo + j0 + m, tok]
                p = Bk[b][:, 0:128 * m].rearrange("p (j s) -> p j s", j=m)
                e = ac.act(h_, p, ACT.Copy, d, over)
                bank_free[b] = ve.tt(AL[:, lo + j0:lo + j0 + m, tok], p, h_.bitcast(F32), ALU.subtract, e, over)
            return d, bank_free[b]

        def rstd(ss, n, inv_n, eps, *wait):
            m = ve.ts(ss, ss, inv_n, ALU.mult, eps, ALU.add, *wait)
            m = ac.act(ss, ss, ACT.Sqrt, m)
            return ve.recip(ss, ss, m)

        def all_wait():
            m = fence()
            for q in (pe, ve, ac, po):
                q.wait(*m)
            return m

        def attention(H, maps, score, v_of, dv, scale, finish, diff=None):
            PH = all_wait()
            pair = Ring([(0, 1), (2, 3)])
            slots = Ring([SB[:, 1024 * j:1024 * j + 1024] for j in range(6)])
            pts = Ring([SB[:, 6144:7168], SB[:, 7168:8192]])
            tb = Banks([4, 5])
            ob = Banks([6, 7])
            units = [(i, h) for i in range(8) for h in range(H)]
            state = {}

            def stage_a(u):
                i, h = u
                N = 128 * (i + 1)
                mx, nm, l, r = stat(maps), stat(maps), stat(maps), stat(maps)
                sl = []
                for m_ in range(maps):
                    pi, (b0, b1), pf = pair.next()
                    pe.wait(pf)
                    for n0 in range(0, N, 512):
                        n1 = min(N, n0 + 512)
                        parts = score(h, m_, i, n0, n1)
                        for k, (l_, r_) in enumerate(parts):
                            mk = pe.mm(PS[:, 512 * b0 + n0:512 * b0 + n1], l_, r_, k == 0, k == len(parts) - 1,
                                       inc=(k == len(parts) - 1 and n1 == N))
                    si, buf, sf = slots.next()
                    mt = ve.put(lambda e, buf=buf, b0=b0, m_=m_: e.tensor_tensor_reduce(
                        out=buf[:, 0:N], in0=PS[:, 512 * b0:512 * b0 + N], in1=MASK[:, 1024 - N:1024], scale=1.0,
                        scalar=-3.0e38, op0=ALU.add, op1=ALU.max, accum_out=mx[:, m_:m_ + 1]), [mk, sf])
                    pair.free[pi] = mt
                    sl.append((si, buf))
                mn = ve.ts(nm, mx, -scale, ALU.mult, None, None, mt)
                for m_ in range(maps):
                    buf = sl[m_][1]
                    me = ac.act(buf[:, 0:N], buf[:, 0:N], ACT.Exp, mn, bias=nm[:, m_:m_ + 1], scale=scale,
                                acc=l[:, m_:m_ + 1])
                state[u] = (sl, me, l, r, N)

            def stage_n(u):
                sl, me, l, r, N = state[u]
                mr = ve.recip(r, l, me)
                if diff:
                    mc = ve.ts(r[:, 1:2], r[:, 1:2], lamv[:, 5:6], ALU.mult, l[:, 0:1], ALU.mult, mr, diff)
                    me = ve.stt(sl[0][1][:, 0:N], sl[1][1][:, 0:N], r[:, 1:2], sl[0][1][:, 0:N], ALU.mult, ALU.add, mc)
                    slots.free[sl[1][0]] = me
                state[u] = (sl[0], me, r, mr)

            def stage_b(u):
                i, h = u
                (si, buf), me, r, mr = state[u]
                pi, pt, pf = pts.next()
                for j0 in range(0, i + 1, 4):
                    n = min(4, i + 1 - j0)
                    b, free = tb.next()
                    pe.wait(free, me)
                    for j in range(n):
                        d = pe.tr(Bk[b][:, 128 * j:128 * j + 128], buf[:, (j0 + j) * 128:(j0 + j + 1) * 128], ident,
                                  inc=(j == n - 1))
                    mc = ac.act(pt[:, 128 * j0:128 * (j0 + n)], Bk[b][:, 0:128 * n], ACT.Copy, d, pf)
                    bank_free[b] = mc
                slots.free[si] = d
                state[u] = (pi, pt, mc, r, mr)

            def stage_c(u):
                i, h = u
                pi, pt, mc, r, mr = state.pop(u)
                b, free = ob.next()
                pe.wait(free, mc)
                for j in range(i + 1):
                    d = pe.mm(Bk[b][:, 0:dv], pt[:, 128 * j:128 * j + 128], v_of(j, h), j == 0, j == i, inc=(j == i))
                pts.free[pi] = d
                bank_free[b] = finish(i, h, Bk[b][:, 0:dv], r, d)

            U = len(units)
            lag = 2 if maps == 2 else 4
            for s_ in range(U + lag + 1):
                if s_ < U:
                    stage_a(units[s_])
                    W.pump()
                if 1 <= s_ < U + 1:
                    stage_n(units[s_ - 1])
                if lag <= s_ < U + lag:
                    stage_b(units[s_ - lag])
                if s_ > lag:
                    stage_c(units[s_ - lag - 1])

        R0, R1, R2, R3 = (R[:, 4096 * j:4096 * j + 4096] for j in range(4))
        ALf = AR[:, 8192:16384].bitcast(F32)
        xd = nc.dram_tensor("x1_kept", [128, 8192], F32, kind="Internal").ap()
        od = nc.dram_tensor("odiff_kept", [128, 4096], F32, kind="Internal").ap()
        gd = nc.dram_tensor("merged_kept", [128, 4096], F32, kind="Internal").ap()
        hd = nc.dram_tensor("hlow_kept", [128, 8192], F32, kind="Internal").ap()
        vd = nc.dram_tensor("v_kept", [128, 4096], F32, kind="Internal").ap()
        md = nc.dram_tensor("mix_kept", [128, 4096], F32, kind="Internal").ap()

        def al_back(*wait):
            d3 = hd.rearrange("p (k s) -> p k s", k=8)
            s3 = ALf.rearrange("p (k s) -> p k s", k=8)
            return [cload(s3[:, :, 256 * j:256 * j + 256], d3[:, :, 256 * j:256 * j + 256], *wait) for j in range(4)]

        later = []

        def flush():
            while later:
                later.pop(0)()

        class Ahead:

            def __init__(self, first, second):
                self.first, self.second, self.m1, self.m2 = first, second, [], []

            def upto(self, t):
                while len(self.m2) <= min(t, 7):
                    while len(self.m1) <= min(len(self.m2) + 1, 7):
                        self.m1.append(self.first(len(self.m1)))
                    self.m2.append(self.second(len(self.m2)))

        class Line:

            def __init__(self, *stages):
                self.stages, self.t = stages, 0
                self.marks = [[] for _ in stages]
                self.m1, self.m2 = self.marks[-2:]

            def step(self):
                for (lag, f), made in zip(self.stages, self.marks):
                    if 0 <= self.t - lag < 8:
                        made.append(f(self.t - lag))
                self.t += 1

            def upto(self, t):
                if self.t <= 7 + self.stages[-1][0]:
                    self.step()

        junk = [None]

        def mean_sq(x, *wait):
            ss = stat(1)
            junk[0] = ac.act(PS[:, 3072:4096], x, ACT.Square, junk[0], bank_free[6], bank_free[7], *wait, acc=ss)
            return ss, rstd(ss, 1, 1.0 / D, EPS, junk[0])

        def six_banks():
            allb.ids, allb.i = list(range(6)), -1

        def eight_banks():
            allb.ids, allb.i = list(range(8)), -1
            bank_free[6] = bank_free[7] = junk[0]

        def proj(us, n, each, wait=None, ahead=None):
            for t in range(8):
                if ahead:
                    ahead.upto(t + 1)
                b, free = allb.next()
                mk = gemm_tok(b, free, n, t, us, [wait[t // 2] if wait else None, ahead.m2[t] if ahead else None], t == 7)
                bank_free[b], post = each(t, b, mk)
                flush()
                if post:
                    later.append(post)

        def norm_ahead(X, grow, c_g, scratch, reads):
            xs = Ring(scratch)
            bufs = {}

            def first(t):
                ss, m = mean_sq(X[t], reads[t])
                i, buf, free = xs.next()
                bufs[t] = (i, buf)
                return ve.stt(buf, X[t], ss, grow, ALU.mult, ALU.mult, m, free, c_g)

            def second(t):
                i, buf = bufs[t]
                d, m = transposed_parts(buf, 8, t, ah.m1[t], allb)
                xs.free[i] = d
                return m
            ah = Ahead(first, second)
            return ah

        def plan1():
            w_in = a["w_in"][0]
            for c0 in (0, 512, 1024):
                W.slab(w_in, c0)
            for c0, n in ((2048, 384), (2432, 320)):
                for j in range(4):
                    W.block(w_in, c0, n, k0=2 * j, K=2)
            for c0 in (1536, 2752, 3264, 4288, 3264 + 512, 4288 + 512):
                W.slab(w_in, c0)
            for c in range(2):
                W.slab(a["w_out"][0], 512 * c)

        STREAMS = (((0, 0), (1, 0)), ((0, 1), (1, 1)), ((0, 2), (1, 2), (2, 0)), ((0, 3), (1, 3), (2, 1)), ((2, 2), (2, 3)))

        N_EARLY = 2

        def plan2():
            w1 = a["w_in_first_2"]
            W.slab(w1, 1024)
            for c in range(8):
                W.block(w1, 128 * c, 128)
            kw = dict(slots=2, raws=2)
            W.block(w1, 3072, 128, **kw)
            for group in STREAMS:
                for j, p in group:
                    W.block(w1, 1536 + 512 * j + 128 * p, 128, **kw)
            W.block(w1, 3136, 96, **kw)
            for c in range(2):
                for j in range(4):
                    W.block(a["w_out_2"][0], 512 * c, 512, k0=2 * j, K=2, **(kw if c == 0 and j < N_EARLY else {}))
            up, down = a["w_ffn_up_2"][0], a["w_ffn_down_2"][0]
            for g in range(17):
                for j in range(2):
                    if g < 16:
                        W.block(up, 128 * (2 * g + j), 128)
                for j in range(2):
                    if g:
                        W.block(down, 0, 1024, k0=2 * g - 2 + j, K=1)

        def spill(dst, src, *wait):
            return odma.go(dst, src, *wait)

        g2row = R[:, 3072:4096]
        m_xs = []

        def block1():
            xsrc = a["x"].rearrange("b (t p) d -> p (b t) d", p=128)
            xr = R[:, 0:8192].rearrange("p (t d) -> p t d", t=8)
            grow = R[:, 10240:11264]
            cx = [cload(xr[:, 0, :], xsrc[:, 0, :])]
            c_grow = cload(grow, bass_rows(a["norm_in"], 128))
            cx.append(cload(xr[:, 1, :], xsrc[:, 1, :]))
            six_banks()
            na = norm_ahead([xr[:, t, :] for t in range(8)], grow, c_grow, [R[:, 8192:9216], R[:, 9216:10240]], cx)
            na.upto(0)
            W.pump()
            cx.append(cload(xr[:, 2, :], xsrc[:, 2, :]))
            lrow = R[:, 14336:14592]
            c_small = [cload(dst, src) for dst, src in (
                (posi.bitcast(I32), a["positions"].rearrange("b (t p) -> p (b t)", p=128)), (invf, a["c_invf"]))]
            for _ in range(2):
                W.pump()
            cx += [cload(xr[:, t, :], xsrc[:, t, :]) for t in range(3, 8)]
            c_small2 = [cload(dst, src) for dst, src in (
                (g_q, a["mla_q_norm"].rearrange("l (k p) -> p (l k)", p=128)),
                (g_kv, a["mla_kv_norm"].rearrange("l (k p) -> p (l k)", p=128)),
                (g_sub, a["diff_subln"].rearrange("l (k p) -> p (l k)", p=128)), (MASK, a["c_caus"]))]
            c_small2 += [cload(lrow[:, 64 * j:64 * j + 64], bass_rows(a[n], 128)) for j, n in enumerate(
                ("diff_lambda_q1", "diff_lambda_k1", "diff_lambda_q2", "diff_lambda_k2"))]

            m = ve.copy(posf, posi.bitcast(I32), c_small)
            tmpA, tmpB = R[:, 14592:14848], R[:, 14848:15104]
            pos3, inv3 = bc(posf, 32), invf.unsqueeze(1).to_broadcast([128, 8, 32])
            A3 = tmpA.rearrange("p (t f) -> p t f", t=8)
            m = ve.tt(A3, pos3, inv3, ALU.mult, m)
            MAGIC = 12582912.0
            m = ve.ts(tmpB, tmpA, 1.0 / TWO_PI, ALU.mult, MAGIC, ALU.add, m)
            m = ve.ts(tmpB, tmpB, MAGIC, ALU.subtract, None, None, m)
            c1 = 6.28125
            c2 = float(np.float32(np.floor((TWO_PI - c1) * 2 ** 21) / 2 ** 21))
            c3 = TWO_PI - c1 - c2
            for c_ in (c1, c2, c3):
                m = ve.stt(tmpA, tmpB, -c_, tmpA, ALU.mult, ALU.add, m)
            PI = 3.1415925
            m = ve.ts(tmpB, tmpA, math.pi / 2, ALU.add, None, None, m)
            m2 = ve.ts(cosT, tmpB, PI, ALU.is_gt, None, None, m)
            m2 = ve.stt(tmpB, cosT, -TWO_PI, tmpB, ALU.mult, ALU.add, m2)
            m2 = ve.ts(tmpB, tmpB, PI, ALU.min, -PI, ALU.max, m2)
            m = ve.ts(tmpA, tmpA, PI, ALU.min, -PI, ALU.max, m2)
            c_rope = [ac.act(cosT, tmpB, ACT.Sin, m), ac.act(sinT, tmpA, ACT.Sin, m)]
            cos3 = cosT.rearrange("p (t f) -> p t f", t=8)
            sin3 = sinT.rearrange("p (t f) -> p t f", t=8)


            rings = {}

            def rope_rings(base):
                rings["a"] = Ring([base[:, 0:512], base[:, 512:1024]])
                rings["b"] = Ring([base[:, 1024:1536], base[:, 1536:2048]])

            def rope(b, mark, t, groups, c0=0):
                n = groups * 64
                x4 = Bk[b][:, c0:c0 + n].rearrange("p (g h f) -> p g h f", g=groups, h=2)
                i1, b1, f1 = rings["a"].next()
                i2, b2, f2 = rings["b"].next()
                t1 = b1[:, 0:n].rearrange("p (g h f) -> p g h f", g=groups, h=2)
                t2 = b2[:, 0:n].rearrange("p (g h f) -> p g h f", g=groups, h=2)
                cb = cos3[:, t, :].unsqueeze(1).unsqueeze(1).to_broadcast([128, groups, 2, 32])
                sb_ = sin3[:, t, :].unsqueeze(1).unsqueeze(1).to_broadcast([128, groups, 2, 32])
                ve.tt(t1, x4, cb, ALU.mult, mark, c_rope, f1)
                m = ve.tt(t2, x4, sb_, ALU.mult, f2)
                po.tt(t1[:, :, 0, :], t1[:, :, 0, :], t2[:, :, 1, :], ALU.subtract, m)
                m2 = po.tt(t1[:, :, 1, :], t1[:, :, 1, :], t2[:, :, 0, :], ALU.add)
                rings["b"].free[i2] = m2
                return i1, b1, m2, m

            def rope_into(dst3, groups, over=None):
                def each(t, b, mk):
                    i1, buf, m, free = rope(b, mk, t, groups)

                    def post():
                        if over:
                            ac.wait(over())
                        _, rings["a"].free[i1] = transposed(buf, groups // 2, dst3, t, m, allb)
                    return free, post
                return each

            qT3 = R0.rearrange("p (c s) -> p c s", c=4)
            kT3 = R1.rearrange("p (c s) -> p c s", c=4)
            V3 = R2.rearrange("p (t d) -> p t d", t=8)
            rope_rings(R[:, 12288:14336])
            proj(W.take4(), 512, rope_into(qT3, 8, lambda: na.m1[3]), ahead=na)
            m_h = spill(hd, ALf, na.m2[7])
            flush()
            m = ve.put(lambda e: e.tensor_tensor_reduce(out=lrow[:, 0:64], in0=lrow[:, 0:64], in1=lrow[:, 64:128], scale=1.0,
                       scalar=0.0, op0=ALU.mult, op1=ALU.add, accum_out=lamv[:, 0:1]), [c_small2])
            m = ve.put(lambda e: e.tensor_tensor_reduce(out=lrow[:, 128:192], in0=lrow[:, 128:192], in1=lrow[:, 192:256], scale=1.0,
                       scalar=0.0, op0=ALU.mult, op1=ALU.add, accum_out=lamv[:, 1:2]), [])
            m = ac.act(lamv[:, 2:4], lamv[:, 0:2], ACT.Exp, m)
            m = ve.tt(lamv[:, 4:5], lamv[:, 3:4], lamv[:, 2:3], ALU.subtract, m)
            c_lam = ve.ts(lamv[:, 5:6], lamv[:, 4:5], -LAMBDA_INIT, ALU.add, None, None, m)
            ac.wait(na.m1[7])
            eight_banks()
            proj(W.take4(), 512, rope_into(kT3, 8))
            proj(W.take4(), 512, lambda t, b, mk: (ac.act(V3[:, t, :], Bk[b], ACT.Copy, mk), None))
            flush()
            for q in (pe, ve, ac, po):
                q.wait(m_h)

            def diff_score(h, m_, i, n0, n1):
                return [(qT3[64 * m_:64 * m_ + 64, h, 128 * i:128 * i + 128], kT3[64 * m_:64 * m_ + 64, h, n0:n1])]

            def o_place(i, h):
                return R0[:, h * 1024 + i * 128:h * 1024 + (i + 1) * 128]

            attention(4, 2, diff_score, lambda j, h: V3[:, j, 128 * h:128 * h + 128], 128, 0.125,
                      lambda i, h, p, r, d: ve.ts(o_place(i, h), p, r[:, 0:1], ALU.mult, None, None, d), diff=c_lam)
            PH = all_wait()
            m_al = al_back(*PH)
            ssd = stat(32)
            od3 = R0.rearrange("p (h t d) -> p h t d", h=4, t=8)
            sq = [R[:, 4096 + 1024 * h:5120 + 1024 * h].rearrange("p (t d) -> p t d", t=8) for h in range(4)]
            for h in range(4):
                m = po.tt(sq[h], od3[:, h], od3[:, h], ALU.mult)
                m_rd = m = ve.red(ssd[:, 8 * h:8 * h + 8], sq[h], ALU.add, m)
            m = rstd(ssd, 32, 1.0 / 128, EPS, m)
            m = ve.ts(ssd, ssd, 1.0 - LAMBDA_INIT, ALU.mult, None, None, m)
            for h in range(4):
                m_od = ve.tt(od3[:, h], od3[:, h], bc(ssd[:, 8 * h:8 * h + 8], 128), ALU.mult, m)
            ac.wait(m_rd)
            m_os = spill(od, R0, m_od)
            cqr = R[:, 4096:7168].rearrange("p (t d) -> p t d", t=8)
            ckr = R[:, 7168:9216].rearrange("p (t d) -> p t d", t=8)
            qn3 = R0.rearrange("p (c s) -> p c s", c=4)
            kn3 = R1.rearrange("p (c s) -> p c s", c=4)
            mV3 = R[:, 9216:13312].rearrange("p (t d) -> p t d", t=8)
            wkv3 = R[:, 9216:11264].rearrange("p (k n) -> p k n", k=2)
            wq3 = R[:, 11264:13568].rearrange("p (k n) -> p k n", k=3)
            qr3 = [R[:, 8192:9216].rearrange("p (c s) -> p c s", c=1), R[:, 13568:14592].rearrange("p (c s) -> p c s", c=1)]
            krT = R[:, 14592:15616]
            kr3 = krT.rearrange("p (c s) -> p c s", c=1)
            ssq, ssk = stat(8), stat(8)
            c_wq = cload(wq3, a["w_uq"][0].rearrange("(k p) n -> p k n", p=128), *PH)
            c_wkv = cload(wkv3, a["w_ukv"][0].rearrange("(k p) n -> p k n", p=128), *PH)
            jsq = R[:, 13568:13952]
            rings["a"] = Ring([R[:, 15616:15744], R[:, 15744:15872]])
            rings["b"] = Ring([R[:, 15872:16000], R[:, 16000:16128]])

            def cq_each(t, b, mk):
                ac.act(cqr[:, t, :], Bk[b][:, 0:384], ACT.Copy, mk)
                return ac.act(jsq, Bk[b][:, 0:384], ACT.Square, ac.last, acc=ssq[:, t:t + 1]), None

            def ckv_each(t, b, mk):
                ac.act(ckr[:, t, :], Bk[b][:, 0:256], ACT.Copy, mk)
                m = ac.act(jsq[:, 0:256], Bk[b][:, 0:256], ACT.Square, ac.last, acc=ssk[:, t:t + 1])
                i1, b1, f1 = rings["a"].next()
                i2, b2, f2 = rings["b"].next()
                x = Bk[b][:, 256:320].rearrange("p (h f) -> p h f", h=2)
                t1 = b1[:, 0:64].rearrange("p (h f) -> p h f", h=2)
                t2 = b2[:, 0:64].rearrange("p (h f) -> p h f", h=2)
                cb = cos3[:, t, :].unsqueeze(1).to_broadcast([128, 2, 32])
                sb_ = sin3[:, t, :].unsqueeze(1).to_broadcast([128, 2, 32])
                ve.tt(t1, x, cb, ALU.mult, m, f1)
                free = ve.tt(t2, x, sb_, ALU.mult, f2)
                po.tt(t1[:, 0, :], t1[:, 0, :], t2[:, 1, :], ALU.subtract, free)
                m = po.tt(t1[:, 1, :], t1[:, 1, :], t2[:, 0, :], ALU.add)
                m = po.copy(b1[:, 64:128], b1[:, 0:64], m)
                rings["b"].free[i2] = m

                def post():
                    _, rings["a"].free[i1] = transposed(b1, 1, kr3, t, m, allb)
                return free, post

            proj(W.take4(), 384, cq_each, wait=m_al)
            proj(W.take4(), 320, ckv_each)
            flush()
            PH = all_wait()
            mq_ = rstd(ssq, 8, 1.0 / 384, EPS)
            mk_ = rstd(ssk, 8, 1.0 / 256, EPS)
            cqT = SB[:, 0:3072].rearrange("p (c s) -> p c s", c=3)
            ckT = SB[:, 3072:5120].rearrange("p (c s) -> p c s", c=2)
            tr_ = Ring([SB[:, 5120 + 512 * k:5632 + 512 * k] for k in range(6)])
            for t in range(8):
                for src, ss, n, m0, dst, gain in ((cqr, ssq, 3, mq_, cqT, g_q), (ckr, ssk, 2, mk_, ckT, g_kv)):
                    i, buf, free = tr_.next()
                    m1 = (ve if n == 3 else po).ts(buf[:, 0:128 * n], src[:, t, :], ss[:, t:t + 1], ALU.mult, None, None, m0, free)

                    def post(buf=buf, n=n, dst=dst, t=t, m1=m1, gain=gain, i=i):
                        _, tr_.free[i] = transposed(buf, n, dst, t, m1, allb, gain=gain)
                    later.append(post)
                    if len(later) > 3:
                        later.pop(0)()
            flush()
            PH = all_wait()
            ac.wait(m_os)
            rope_rings(SB[:, 5120:7168])
            for h in range(4):
                for s_ in range(2):
                    b, free = allb.next()
                    mk = gemm(b, free, 512, lambda k: wq3[:, k, 192 * h:192 * h + 128], lambda k: cqT[:, k, 512 * s_:512 * s_ + 512], 3, c_wq)
                    bank_free[b] = ac.act(qn3[:, h, 512 * s_:512 * s_ + 512], Bk[b], ACT.Copy, mk)
            vr = wq3.rearrange("p k (h c) -> p k h c", h=4)
            for t in range(8):
                b, free = allb.next()
                pe.wait(free)
                for k in range(3):
                    mk = pe.mm(Bk[b][:, 0:256].rearrange("p (h c) -> p h c", h=4), cqT[:, k, 128 * t:128 * t + 128],
                               vr[:, k, :, 128:192], k == 0, k == 2, inc=(k == 2))
                i1, buf, m1, free = rope(b, mk, t, 4)
                bank_free[b] = free
                flush()

                def post(i1=i1, buf=buf, t=t, m1=m1):
                    for c in range(2):
                        _, rings["a"].free[i1] = transposed(buf[:, 128 * c:128 * c + 128], 1, qr3[c], t, m1, allb)
                later.append(post)
            for h in range(4):
                for s_ in range(2):
                    b, free = allb.next()
                    mk = gemm(b, free, 512, lambda k: wkv3[:, k, 256 * h:256 * h + 128], lambda k: ckT[:, k, 512 * s_:512 * s_ + 512], 2, c_wkv)
                    bank_free[b] = ac.act(kn3[:, h, 512 * s_:512 * s_ + 512], Bk[b], ACT.Copy, mk)
                if h == 0:
                    flush()
            vr2 = wkv3.rearrange("p k (h c) -> p k h c", h=4)
            mvA = []
            for t in range(8):
                b, free = allb.next()
                pe.wait(free)
                for k in range(2):
                    mk = pe.mm(Bk[b].rearrange("p (h c) -> p h c", h=4), ckT[:, k, 128 * t:128 * t + 128],
                               vr2[:, k, :, 128:256], k == 0, k == 1, inc=(k == 1))
                mvA.append(b)
            for t in range(8):
                bank_free[mvA[t]] = ac.act(mV3[:, t, :], Bk[mvA[t]], ACT.Copy, mk)

            def mla_score(h, m_, i, n0, n1):
                c, o = h // 2, 64 * (h % 2)
                return [(qn3[:, h, 128 * i:128 * i + 128], kn3[:, h, n0:n1]),
                        (qr3[c][o:o + 64, 0, 128 * i:128 * i + 128], krT[o:o + 64, n0:n1])]

            attention(4, 1, mla_score, lambda j, h: mV3[:, j, 128 * h:128 * h + 128], 128, 192.0 ** -0.5,
                      lambda i, h, p, r, d: ve.ts(o_place(i, h), p, r[:, 0:1], ALU.mult, None, None, d))

            PH = all_wait()
            m_al = al_back(*PH)
            m_od = cload(R1, od, *PH, m_os)
            oT = [R2.rearrange("p (c s) -> p c s", c=4), R3.rearrange("p (c s) -> p c s", c=4)]
            gb = Ring([MASK[:, 0:512], MASK[:, 512:1024]])
            gsub = g_sub.to_broadcast([128, 4])

            def gate_each(reg, dst, gain, got=None):
                r4 = reg.rearrange("p (h t d) -> p h t d", h=4, t=8)

                def each(t, b, mk):
                    gi, buf, gf = gb.next()
                    m = ac.act(buf, Bk[b], ACT.Silu, mk, gf)
                    b4 = buf.rearrange("p (h d) -> p h d", h=4)
                    m2 = po.tt(b4, b4, r4[:, :, t, :], ALU.mult, m, got)

                    def post():
                        _, gb.free[gi] = transposed(buf, 4, dst, t, m2, allb, gain=gain)
                    return m, post
                return each

            proj(W.take4(), 512, gate_each(R1, oT[0], gsub, m_od), wait=m_al)
            proj(W.take4(), 512, gate_each(R0, oT[1], None))
            flush()
            PH = all_wait()
            MG = R[:, 0:4096].rearrange("p (t d) -> p t d", t=8)
            gd3 = gd.rearrange("p (t d) -> p t d", t=8)
            WP = [R[:, 4096:6144].rearrange("p (k n) -> p k n", k=4), R[:, 6144:8192].rearrange("p (k n) -> p k n", k=4)]
            g1 = Ring([MASK[:, 0:512], MASK[:, 512:1024]])
            wpfree = [None, None]
            kept = [None] * 8
            for c in range(2):
                for kind, wp in enumerate(("w_proj_diff", "w_proj_mla")):
                    o_ = oT[kind]
                    mp = cload(WP[kind], a[wp][0][:, 512 * c:512 * c + 512].rearrange("(k p) n -> p k n", p=128), *PH, wpfree[kind])
                    us = W.take4()
                    for t in range(8):
                        b, free = allb.next()
                        mk = gemm_tok(b, free, 512, t, us, [], t == 7)
                        gi, buf, gf = g1.next()
                        m = ac.act(buf, Bk[b], ACT.Sigmoid, mk, gf)
                        bank_free[b] = m
                        b, free = allb.next()
                        mk = gemm(b, free, 512, lambda k: o_[:, k, 128 * t:128 * t + 128], lambda k: WP[kind][:, k, :], 4, mp)
                        if kind == 0:
                            m = ve.tt(MG[:, t, :], Bk[b], buf, ALU.mult, m, mk, kept[t])
                            bank_free[b] = m
                            g1.free[gi] = m
                        else:
                            m = ve.tt(buf, Bk[b], buf, ALU.mult, m, mk)
                            bank_free[b] = m
                            g1.free[gi] = m = po.tt(MG[:, t, :], MG[:, t, :], buf, ALU.add, m)
                            if c == 0:
                                kept[t] = spill(gd3[:, t, :], MG[:, t, :], m)
                    wpfree[kind] = mk
            PH = all_wait()
            M0 = R[:, 12288:16384].rearrange("p (t d) -> p t d", t=8)
            m_m0 = cload(R[:, 12288:16384], gd, *PH, kept)
            X1 = R[:, 4096:12288].rearrange("p (t d) -> p t d", t=8)
            cx = [cload(X1[:, 2 * j:2 * j + 2, :], xsrc[:, 2 * j:2 * j + 2, :], PH) for j in range(4)]
            gfin = MASK
            c_gf = cload(gfin, bass_rows(a["norm_final"].rearrange("(a n) -> a n", a=1), 128), PH)
            for t in range(8):
                transposed_parts(MG[:, t, :], 4, t, None, allb, lo=4)
            for t in range(8):
                transposed_parts(M0[:, t, :], 4, t, m_m0, allb)
            mT = fence()
            cload(g2row, bass_rows(a["norm_mix_pre_2"], 128), *PH, mT)
            c_g2 = cdma.all()
            six_banks()
            xd3 = xd.rearrange("p (t d) -> p t d", t=8)
            m_add, m_c1 = [], []

            def final_first(t):
                ss, m = mean_sq(X1[:, t, :], m_add[t])
                m = ve.stt(X1[:, t, :], X1[:, t, :], ss, gfin, ALU.mult, ALU.mult, m, c_gf)
                m_xs.append(spill(xd3[:, t, :], X1[:, t, :], m))
                return m

            def final_norm(t):
                ss, m = mean_sq(X1[:, t, :], fa.marks[0][t])
                i, buf, free = hbuf.next()
                hb[t] = (i, buf)
                return ve.stt(buf, X1[:, t, :], ss, g2row, ALU.mult, ALU.mult, m, free, c_g2)

            def final_second(t):
                i, buf = hb[t]
                d, m = transposed_parts(buf, 8, t, fa.m1[t], allb, over=m_c1[t])
                hbuf.free[i] = d
                return m
            hbuf, hb = Ring([R[:, 0:1024], R[:, 1024:2048], R[:, 2048:3072]]), {}
            fa = Line((0, final_first), (1, final_norm), (3, final_second))
            for c in range(2):
                us = W.take4()
                for t in range(8):
                    b, free = allb.next()
                    mk = gemm_tok(b, free, 512, t, us, mT, t == 7)
                    dst = X1[:, t, 512 * c:512 * c + 512]
                    bank_free[b] = ve.tt(dst, Bk[b], dst, ALU.add, mk, cx)
                    if c == 1:
                        m_add.append(bank_free[b])
                        m_c1.append(mk)
                        fa.step()
            return fa

        def vec_cols(name, c0, n):
            return a[name].rearrange("l n -> (l n)")[c0:c0 + n].rearrange("(k p) -> p k", p=128 if n >= 128 else n)

        def block2(fa):
            PH = [q.last for q in (ve, ac, po) if q.n]
            for dst, name, c0, n in (
                    (g_att, "attn_out_gain_2", 0, 512),
                    (mu_c[:, 0:12], "mu_shift_2", 0, 1536), (mu_c[0:64, 12:13], "mu_shift_2", 1536, 64),
                    (mu_c[0:96, 13:14], "mu_shift_2", 1600, 96), (w0_c, "decay_w0_2", 0, 512), (a0_c, "aaa_a0_2", 0, 512),
                    (kk_c, "k_k_2", 0, 512), (ka_c, "k_a_2", 0, 512)):
                cload(dst, vec_cols(name, c0, n))
            cload(rk_c, a["r_k_2"].rearrange("l (k h) c -> (h c) (l k)", h=2))
            for dst, name in ((lvl, "lvl"), (lvl0t, "lvl0t"), (slow, "slow"), (supt, "supt"), (incl, "incl"),
                              (bones, "bones"), (hsel, "hsel")):
                cload(dst, a["c_" + name])
            w1 = a["w_in_first_2"]
            q2 = R[:, 0:8192].rearrange("p (c q s) -> p c q s", c=4, q=2)
            kT3 = R2.rearrange("p (c s) -> p c s", c=4)
            V3 = R3.rearrange("p (t d) -> p t d", t=8)
            proj(W.take4(), 512, lambda t, b, mk: (ac.act(V3[:, t, :], Bk[b], ACT.Copy, mk), None), ahead=fa)
            m_h = spill(hd, ALf, fa.m2)
            eight_banks()
            cload(MASK, a["c_dil"], fa.m1)
            C2 = cdma.all()
            m_gone = [fa.m1, fa.m2, m_xs]
            for q in (ac, ve, po):
                q.wait(m_gone)
            pe.wait(C2)
            m_free = fence()
            po.put(lambda e: e.memset(q2[64:128, :, 0, :], 0.0), m_free)
            m_z = po.put(lambda e: e.memset(q2[0:64, :, 1, :], 0.0))

            def q_evac(s_, b, mk):
                tok = slice(512 * s_, 512 * s_ + 512)
                return [ac.act(q2[0:64, c, 0, tok], Bk[b][0:64, :], ACT.Copy, mk),
                        ve.copy(q2[64:128, c, 1, tok], Bk[b][64:128, :], mk)]
            for c in range(4):
                gemm_feat(W.take(), 128, q_evac)
            for c in range(4):
                gemm_feat(W.take(), 128, lambda s_, b, mk: ac.act(
                    kT3[:, c, 512 * s_:512 * s_ + 512], Bk[b], ACT.Copy, mk))
            for q in (pe, ve, ac, po):
                q.wait(m_h, m_z, C2)

            def dil_score(h, m_, i, n0, n1):
                return [(q2[:, h // 2, h % 2, 128 * i:128 * i + 128], kT3[:, h // 2, n0:n1])]

            def dil_done(i, h, p, r, d):
                c = h * 1024 + i * 128
                return ve.ts(R[:, c:c + 64], p, r[:, 0:1], ALU.mult, None, None, d)

            attention(8, 1, dil_score, lambda j, h: V3[:, j, 64 * h:64 * h + 64], 64, 0.125, dil_done)
            PH = all_wait()
            m_al = al_back(*PH)
            m_reset = cload(MASK, a["c_reset"], *PH)
            SQ = R[:, 12288:13824]
            o4 = R[:, 0:8192].rearrange("p (c t d) -> p t c d", c=8, t=8)[:, :, :, 0:64]
            ssa = stat(8)
            jm = None
            for t in range(8):
                jm = ac.act(SQ[:, 0:512].rearrange("p (c d) -> p c d", c=8), o4[:, t], ACT.Square, jm, acc=ssa[:, t:t + 1])
            m = rstd(ssa, 8, 1.0 / 512, EPS, jm)
            mixA = R2.rearrange("p (c s) -> p c s", c=4)
            xs = Ring([SQ[:, 512:1024], SQ[:, 1024:1536]])
            for t in range(8):
                i, buf, free = xs.next()
                m1 = ve.ts(buf.rearrange("p (c d) -> p c d", c=8), o4[:, t], ssa[:, t:t + 1], ALU.mult, None, None, m, free)
                _, xs.free[i] = transposed(buf, 4, mixA, t, m1, allb, gain=g_att)
            PH = all_wait()
            m_mix = odma.go(md, R2, *PH)

            KAP, BET, KHT, RHO = (R[:, 4096 * j:4096 * j + 4096].rearrange("p (c s) -> p c s", c=4) for j in range(4))
            TR = WF[:, 4096:12288]
            T1 = RAWS[:, 2048:3072]
            T2, T3, T4 = (TR[:, 1024 * j:1024 * j + 1024] for j in range(3))
            LW = TR[:, 3072:4096]
            Zf = [TR[:, 4096:5128], TR[:, 5128:6160]]
            TS = TR[:, 6160:7184]
            UPS, UPW = TR[:, 7184:7696], trig
            W.may_grow = False
            XG = LW
            m_z0 = [ve.put(lambda e: e.memset(UPS, 0.0)), ve.put(lambda e: e.memset(UPW, 0.0)),
                    ve.put(lambda e: e.memset(LW[64:128, :], 0.0)),
                    ve.put(lambda e: e.memset(Zf[0][:, 0:8], 0.0)), ve.put(lambda e: e.memset(Zf[1][:, 0:8], 0.0))]
            c_up = [cload(UPW[0:32, :], a["decay_up_2"][0], *PH, m_z0), cload(UPS[32:64, :], a["aaa_up_2"][0])]
            halfsl = [slice(0, 512), slice(512, 1024)]
            zr = Ring(Zf)
            tsf = [None]

            def stream(cols, muc, dst, got):
                u = W.take()
                zi, zf, free = zr.next()
                zm = []

                def evac(s_, b, mk):
                    zm.append(ac.act(zf[0:cols, 8 + 512 * s_:520 + 512 * s_], Bk[b][0:cols, :], ACT.Copy, mk, free))
                    return zm[-1]
                pe.wait(m_al[0:2])
                gemm_half(u, 96 if cols == 96 else 128, 0, evac, False)
                yield
                pe.wait(m_al)
                gemm_half(u, 96 if cols == 96 else 128, 1, evac)
                z = zf[0:cols, 8:1032]
                m1 = po.tt(TS[0:cols, :], zf[0:cols, 7:1031], z, ALU.subtract, zm, m_z0, tsf[0])
                m2 = ve.stt(dst, TS[0:cols, :], muc, z, ALU.mult, ALU.add, m1)
                tsf[0] = zr.free[zi] = m2
                got.append((m2, zi, zf))
                yield

            got = []
            for _ in stream(64, mu_c[0:64, 12:13], LW[0:64, :], got):
                pass
            m_lw = ac.act(LW[0:32, :], LW[0:32, :], ACT.Tanh, got[0][0])
            vd3 = vd.rearrange("p (t d) -> p t d", t=8)
            m_vs = []
            ready = {}

            def streams(p):
                for j, c in STREAMS[p]:
                    got = []
                    muc = mu_c[:, 4 * j + c:4 * j + c + 1]
                    if j < 2:
                        if j:
                            ve.wait(m_mix)
                        yield from stream(128, muc, (RHO, KHT)[j][:, c, :], got)
                        ready.setdefault(c, []).append(got[0][0])
                        continue
                    yield from stream(128, muc, TS, got)
                    m, zi, zf = got[0]
                    v3 = zf[:, 0:1024].rearrange("p (t d) -> p t d", t=8)
                    em, tsf[0] = transposed(TS, 8, v3, 0, m, allb)
                    m = spill(vd3[:, :, 128 * c:128 * c + 128], v3, em)
                    m_vs.append(m)
                    zr.free[zi] = m0 = ve.put(lambda e, zf=zf: e.memset(zf[:, 0:8], 0.0), [m])
                    m_z0.append(m0)
                if p == 4:
                    yield from stream(96, mu_c[0:96, 13:14], TS[0:96, :], got_g)

            EL = [None]

            def elements(p):
                for q in (ve, ac, po):
                    q.wait(EL[0])
                r_, k_, b_, h_ = RHO[:, p, :], KAP[:, p, :], BET[:, p, :], KHT[:, p, :]
                ready_ = ready[p]

                def lora(up):
                    made = []
                    for s_ in range(2):
                        b, free = allb.next()
                        made.append((b, pe.mm(Bk[b], up[:, 128 * p:128 * p + 128], LW[:, halfsl[s_]], True, True,
                                              free, c_up, m_lw, m_z0, inc=True)))
                    return made

                def from_banks(made, dst, f, bias=0.0):
                    for s_, (b, mk) in enumerate(made):
                        bank_free[b] = ac.act(dst[:, halfsl[s_]], Bk[b], f, mk, bias=bias)
                    return ac.last
                pw, pa = lora(UPW), lora(UPS)
                m_kk = ve.ts(k_, h_, kk_c[:, p:p + 1], ALU.mult, None, None, ready_)
                m_sq = po.tt(b_, k_, k_, ALU.mult, m_kk)
                m_w = from_banks(pw, T3, ACT.Sigmoid, w0_c[:, p:p + 1])
                m_a = from_banks(pa, T2, ACT.Sigmoid, a0_c[:, p:p + 1])
                yield
                pn = []
                for s_ in range(2):
                    b, free = allb.next()
                    pn.append((b, pe.mm(Bk[b], bones, b_[:, halfsl[s_]], True, True, free, m_sq, inc=True)))
                mn_ = pe.last
                m = ve.ts(T3, T3, -math.exp(-0.5), ALU.mult, None, None, m_w)
                m_lc = ve.put(lambda e: e.tensor_tensor_scan(T1, MASK, T3, 0.0, ALU.mult, ALU.add), [m, m_reset])
                m_n = from_banks(pn, T4, ACT.Sqrt)
                m_t3 = ve.tt(T3, T1, T3, ALU.subtract, m_lc)
                yield
                m = ve.ts(T4, T4, 1e-12, ALU.max, None, None, m_n)
                m = ve.recip(T4[:, 0:512], T4[:, 0:512], m)
                yield
                m = ve.recip(T4[:, 512:1024], T4[:, 512:1024])
                m_kk = ve.tt(k_, k_, T4, ALU.mult, m)
                m = ve.ts(T4, T2, -1.0, ALU.add, None, None, m_kk, m_a)
                m_e3 = ac.act(T3, T3, ACT.Exp, m_t3)
                yield
                m = ve.ts(T4, T4, ka_c[:, p:p + 1], ALU.mult, 1.0, ALU.add, m)
                m_km = ve.tt(h_, h_, T4, ALU.mult, m)
                m_b0 = ve.stt(b_, r_, rk_c[:, p:p + 1], h_, ALU.mult, ALU.mult, m_km, mn_)
                me = ac.act(T4, T1, ACT.Exp, m_km, m_lc)
                yield
                b, free = allb.next()
                pe.wait(free, m_b0)
                for t in range(8):
                    mb = pe.mm(Bk[b][:, 2 * t:2 * t + 2], b_[:, 128 * t:128 * t + 128], hsel, True, True, inc=(t == 7))
                ve.tt(r_, r_, T4, ALU.mult, me, m_b0)
                ve.copy(WC.rearrange("p (k c) -> p k c", k=4)[:, p, :], T4.rearrange("p (c n) -> p n c", n=64)[:, 63, :])
                m_b = po.tt(b_, k_, T2, ALU.mult, m_kk, m_a, mb)
                m_e2 = ac.act(T2, T1, ACT.Exp, m_b, scale=-1.0)
                m2 = po.tt(k_, k_, T3, ALU.mult, m_e3)
                yield
                bank_free[b] = ve.copy(bon.rearrange("p (t h) -> p t h", t=8)[:, :, 2 * p:2 * p + 2],
                                       Bk[b][:, 0:16].rearrange("p (t h) -> p t h", t=8), mb)
                m_h = ve.tt(h_, h_, T2, ALU.mult, m_e2, m_b0)
                m1 = po.tt(b_, b_, T2, ALU.mult, m_e2, m_b)
                EL[0] = [m1, m2, m_e3, m_h]

            got_g = []
            for p in range(5):
                S_ = streams(p)
                E_ = elements(p - 1) if p else iter(())
                live = [S_, E_]
                while live:
                    live = [x for x in live if next(x, "end") != "end"]
            m_xg = ac.act(XG[0:96, :], TS[0:96, :], ACT.Sigmoid, got_g[0][0], pe.last)

            PH = all_wait()
            ac.wait(m_xg)
            c_gn = [cload(MASK[:, 0:512], bass_rows(a["gn_w_2"], 128), *PH),
                    cload(MASK[:, 512:1024], bass_rows(a["gn_b_2"], 128), *PH)]
            c_g = cload(UPS[0:96, :], a["gate_up_2"][0], *PH)
            GW, GB = MASK[:, 0:512], MASK[:, 512:1024]
            ab2 = Banks([0, 1, 2, 3])
            cb2 = Banks([4, 5, 6, 7])
            VT = AF[:, 0:4096].rearrange("p (t d) -> p t d", t=8)
            m_vt = [cload(VT[:, 2 * j:2 * j + 2, :], vd3[:, 2 * j:2 * j + 2, :], *PH, m_vs) for j in range(4)]
            spare = [AF[:, 4096 + 1024 * j:5120 + 1024 * j] for j in range(12)]
            Tt, T_, XP, Ll, L_ = spare[0:5]
            AB = [spare[5], spare[6]]
            AK = [spare[7], spare[8]]
            NB = [spare[9][:, 0:512], spare[9][:, 512:1024]]
            KH = [spare[10][:, 0:512], spare[10][:, 512:1024]]
            PT = [spare[11][:, 0:512], spare[11][:, 512:1024]]
            QS = [T2[:, 0:512], T2[:, 512:1024]]
            KTk, Xv = T3[:, 0:512], T3[:, 512:1024]
            SH = [T4[:, 256 * j:256 + 256 * j] for j in range(4)]
            YB, Y2 = T1[:, 0:512], T1[:, 512:1024]
            U_ = Zf[0][:, 0:512]
            Y3 = Zf[0][:, 512:1024]
            MR = R[:, 0:4096].rearrange("p (c s) -> p c s", c=4)
            m_s0 = ve.put(lambda e: e.memset(SH[0], 0.0))

            def pj(buf):
                return buf.rearrange("p (q j s) -> p q j s", q=2, j=4)

            def b3(b):
                return Bk[b].rearrange("p (j s) -> p j s", j=4)

            def mask3(mk_):
                return mk_.unsqueeze(1).to_broadcast([128, 4, 128])

            use = {}

            def prep(t):
                z = t % 2
                ts_ = slice(128 * t, 128 * t + 128)
                g = use.get(("tile", t - 2), [])
                for src, dst, sc in ((KAP, KTk, 1.0), (BET, NB[z], -1.0), (KHT, KH[z], 1.0)):
                    b, free = ab2.next()
                    pe.wait(free, c_id)
                    for p in range(4):
                        d = pe.tr(Bk[b][:, 128 * p:128 * p + 128], src[:, p, ts_], ident, inc=(p == 3))
                    bank_free[b] = ac.act(dst, Bk[b], ACT.Copy, d, g, use.get("ktk") if dst is KTk else None, scale=sc)
                m_tok = bank_free[b]

                def products(l3, r3, dst, mask, op_neg, *wait):
                    for q in range(2):
                        b, free = ab2.next()
                        pe.wait(free)
                        for j in range(4):
                            d = pe.mm(Bk[b][:, 128 * j:128 * j + 128], l3[64 * q:64 * q + 64, j, ts_],
                                      r3[64 * q:64 * q + 64, j, ts_], True, True, inc=(j == 3))
                        if op_neg:
                            m = ve.stt(pj(dst)[:, q], b3(b), -1.0, mask3(mask), ALU.mult, ALU.mult, d, *wait)
                        else:
                            m = ve.tt(pj(dst)[:, q], b3(b), mask3(mask), ALU.mult, d, *wait)
                        bank_free[b] = m
                    return m
                m_l = products(KAP, BET, L_, slow, False, use.get("L"))
                m_x = products(KHT, KAP, XP, supt, False, use.get("XP"))
                m = po.tt(T_.rearrange("p (h s) -> p h s", h=8), L_.rearrange("p (h s) -> p h s", h=8),
                          lvl[:, 0:128].unsqueeze(1).to_broadcast([128, 8, 128]), ALU.mult, m_l, use.get("T"))
                m_t = ve.stt(T_.rearrange("p (h s) -> p h s", h=8), T_.rearrange("p (h s) -> p h s", h=8), -1.0,
                             ident.unsqueeze(1).to_broadcast([128, 8, 128]), ALU.mult, ALU.add, m)
                def level(l, q, *wait):
                    return po.tt(pj(Ll)[:, q], pj(L_)[:, q], mask3(lvl[:, 128 * l:128 * l + 128]), ALU.mult, *wait)
                m_ll = [level(1, 0, use.get("Ll")), level(1, 1)]
                b, free = ab2.next()
                pe.wait(free, m_x, m_vt[t // 2])
                for h in range(8):
                    c = (h % 2) * 512 + (h // 2) * 128
                    d = pe.mm(Bk[b][:, 64 * h:64 * h + 64], XP[:, c:c + 128], VT[:, t, 64 * h:64 * h + 64], True, True, inc=(h == 7))
                m_xv = bank_free[b] = ac.act(Xv, Bk[b], ACT.Copy, d, use.get("Xv"))
                use["XP"] = d
                m_ab = products(BET, RHO, AB[z], incl, True, g)
                m_ak = products(KHT, RHO, AK[z], incl, False, g)
                use["feat"] = pe.last
                mtt = []
                for q in range(2):
                    b, free = ab2.next()
                    pe.wait(free, m_t)
                    for j in range(4):
                        d = pe.tr(Bk[b][:, 128 * j:128 * j + 128], pj(T_)[:, q, j, :], ident, inc=(j == 3))
                    m = ac.act(pj(Tt)[:, q], b3(b), ACT.Copy, d, use.get("Tt"))
                    bank_free[b] = m
                    mtt.append(m)
                yield
                for l in range(1, 6):
                    mx = []
                    for q in range(2):
                        b, free = ab2.next()
                        pe.wait(free, m_ll[q], mtt[q])
                        for j in range(4):
                            d = pe.mm(Bk[b][:, 128 * j:128 * j + 128], pj(Ll)[:, q, j, :], pj(Tt)[:, q, j, :], True, True, inc=(j == 3))
                        m = ac.act(pj(XP)[:, q], b3(b), ACT.Copy, d, use["XP"])
                        bank_free[b] = m
                        mx.append(m)
                        if l < 5:
                            m_ll[q] = level(l + 1, q, d)
                    yield
                    nt = []
                    for q in range(2):
                        b, free = ab2.next()
                        pe.wait(free, mx[q], m_t if l == 1 else mt_[q])
                        for j in range(4):
                            d = pe.mm(Bk[b][:, 128 * j:128 * j + 128], pj(T_)[:, q, j, :], pj(XP)[:, q, j, :], True, True, inc=(j == 3))
                        m = ve.tt(pj(Tt)[:, q], pj(Tt)[:, q], b3(b), ALU.subtract, d, mtt[q])
                        bank_free[b] = m
                        nt.append(m)
                    use["XP"] = d
                    yield
                    mtt = nt
                    if l < 5:
                        mt_ = []
                        for q in range(2):
                            b, free = ab2.next()
                            pe.wait(free, mtt[q])
                            for j in range(4):
                                d = pe.tr(Bk[b][:, 128 * j:128 * j + 128], pj(Tt)[:, q, j, :], ident, inc=(j == 3))
                            m = ac.act(pj(T_)[:, q], b3(b), ACT.Copy, d)
                            bank_free[b] = m
                            mt_.append(m)
                    else:
                        use["T"] = d
                        use["Ll"] = d
                        use["L"] = m_ll[1]
                    yield
                b, free = ab2.next()
                pe.wait(free, m_tok, mtt)
                for h in range(8):
                    q, j = h % 2, h // 2
                    d = pe.mm(Bk[b][64 * q:64 * q + 64, 128 * j:128 * j + 128], KTk[:, 64 * h:64 * h + 64], pj(Tt)[:, q, j, :],
                              True, True, inc=(h == 7))
                m_p = bank_free[b] = ac.act(PT[z], Bk[b], ACT.Copy, d, g)
                use["ktk"] = d
                b, free = ab2.next()
                pe.wait(free, m_xv)
                for h in range(8):
                    q, j = h % 2, h // 2
                    d = pe.mm(Bk[b][:, 64 * h:64 * h + 64], pj(Tt)[:, q, j, :], Xv[:, 64 * h:64 * h + 64], True, True, inc=(h == 7))
                m_q = bank_free[b] = ac.act(QS[z], Bk[b], ACT.Copy, d, g)
                use["Tt"] = use["Xv"] = d
                use[("ready", t)] = [m_p, m_q, m_ab, m_ak, m_tok]

            WC3 = WC.rearrange("p (k c) -> p k c", k=4)
            chain = {"s": m_s0}

            def chain_tile(t):
                z = t % 2
                rdy = use[("ready", t)]
                um = []
                for c in range(2):
                    n = 2 * t + c
                    o = 64 * c
                    Sn, Sx = SH[n % 4], SH[(n + 1) % 4]
                    for q in range(2):
                        b, free = cb2.next()
                        pe.wait(free, chain["s"], rdy)
                        for j in range(4):
                            d = pe.mm(Bk[b][o:o + 64, 64 * j:64 * j + 64], PT[z][64 * q:64 * q + 64, 128 * j + o:128 * j + o + 64],
                                      Sn[64 * q:64 * q + 64, 64 * j:64 * j + 64], True, True, inc=(j == 3))
                        m = ve.tt(U_[o:o + 64, :].rearrange("p (j q d) -> p q j d", j=4, q=2)[:, q],
                                  Bk[b][o:o + 64, 0:256].rearrange("p (j d) -> p j d", j=4),
                                  QS[z][o:o + 64, :].rearrange("p (j q d) -> p q j d", j=4, q=2)[:, q], ALU.add, d, use.get("U"))
                        bank_free[b] = m
                        if q == 0:
                            yield
                    um.append(m)
                    yield
                    b, free = cb2.next()
                    pe.wait(free, m)
                    for h in range(8):
                        q, j = h % 2, h // 2
                        ov = Bk[b][64 * q:64 * q + 64, 64 * j:64 * j + 64]
                        pe.mm(ov, NB[z][o:o + 64, 64 * h:64 * h + 64], U_[o:o + 64, 64 * h:64 * h + 64], True, False)
                        d = pe.mm(ov, KH[z][o:o + 64, 64 * h:64 * h + 64], VT[o:o + 64, t, 64 * h:64 * h + 64], False, True, inc=(h == 7))
                    m = ve.tt(Sx, Bk[b][:, 0:256], Sn, ALU.add, d, use.get(("y", t - 2)), chain["s"])
                    bank_free[b] = m
                    chain["s"] = ve.tt(Sx.rearrange("p (j d) -> p j d", j=4), Sx.rearrange("p (j d) -> p j d", j=4),
                                       bc(WC3[:, :, n], 64), ALU.mult, m)
                    yield
                ym = []
                for q in range(2):
                    b, free = cb2.next()
                    pe.wait(free, um)
                    for j in range(4):
                        h = 2 * j + q
                        ov = Bk[b][:, 64 * j:64 * j + 64]
                        pe.mm(ov, pj(AK[z])[:, q, j, :], VT[:, t, 64 * h:64 * h + 64], True, False)
                        pe.mm(ov, pj(AB[z])[:, q, j, :], U_[:, 64 * h:64 * h + 64], False, False)
                        for c in range(2):
                            o = 64 * c
                            d = pe.mm(Bk[b][o:o + 64, 64 * j:64 * j + 64], RHO[64 * q:64 * q + 64, j, 128 * t + o:128 * t + o + 64],
                                      SH[(2 * t + c) % 4][64 * q:64 * q + 64, 64 * j:64 * j + 64], False, True, inc=(j == 3 and c == 1))
                    m = ac.act(YB.rearrange("p (j q d) -> p q j d", j=4, q=2)[:, q], Bk[b][:, 0:256].rearrange("p (j d) -> p j d", j=4),
                               ACT.Copy, d, use.get("YB"))
                    bank_free[b] = m
                    ym.append(m)
                    yield
                use["U"] = use[("y", t)] = d
                use[("tile", t)] = [d]
                use[("ym", t)] = ym

            def norm_tile(t):
                ym = use[("ym", t)]
                fast = ve if t == 7 else po
                y3 = YB.rearrange("p (h d) -> p h d", h=8)
                s1, s2 = stat(8), stat(8)
                m = ve.red(s1, y3, ALU.add, ym)
                m = ve.ts(s1, s1, 1.0 / 64, ALU.mult, None, None, m)
                m = ve.tt(y3, y3, bc(s1, 64), ALU.subtract, m)
                y2 = Y2.rearrange("p (h d) -> p h d", h=8)
                m = fast.tt(Y2, YB, YB, ALU.mult, m, use.get("Y2"))
                yield
                m = ve.red(s2, y2, ALU.add, m)
                m = rstd(s2, 8, 1.0 / 64, GN_EPS, m)
                yield
                m = ve.tt(y3, y3, bc(s2, 64), ALU.mult, m)
                m = fast.tt(YB, YB, GW, ALU.mult, m, c_gn)
                m = fast.tt(YB, YB, GB, ALU.add, m)
                m2 = ve.tt(y2, VT[:, t, :].rearrange("p (h d) -> p h d", h=8), bc(bon[:, 8 * t:8 * t + 8], 64), ALU.mult,
                           m_vt[t // 2])
                m = fast.tt(YB, YB, Y2, ALU.add, m, m2)
                yield
                b, free = cb2.next()
                mk = pe.mm(Bk[b], XG[0:96, 128 * t:128 * t + 128], UPS[0:96, :], True, True, free, c_g, inc=True)
                m = ve.tt(Y3, YB, Bk[b], ALU.mult, m, mk, use.get("Y3"))
                bank_free[b] = use["YB"] = use["Y2"] = m
                yield
                marks, d = transposed(Y3, 4, MR, t, m, cb2)
                use["Y3"] = d

            MAf = R[:, 8192:12288]
            for t in range(10):
                if t == 8:
                    m_ma = cload(MAf, md, use["feat"], m_mix)
                A_ = prep(t) if t < 8 else iter(())
                B_ = chain_tile(t - 1) if 1 <= t <= 8 else iter(())
                C_ = norm_tile(t - 2) if t >= 2 else iter(())
                live = [A_, C_, B_]
                while live:
                    live = [x for x in live if next(x, "end") != "end"]
            PH = all_wait()
            W.may_grow = True
            for i in range(6):
                if not W.held[i]:
                    W.slotfree[i] = PH
            W.rawfree[2] = PH

            GP = MASK
            m_gp = cload(GP, bass_rows(a["norm_mix_post_2"], 128), *PH)
            MX = R[:, 4096:12288].rearrange("p (t d) -> p t d", t=8)
            MA = MAf.rearrange("p (c s) -> p c s", c=4)
            m_parts = []
            for j in range(4):
                c2 = slice(256 * j, 256 * j + 256)
                for lo, src, got in ((4, MR, None), (0, MA, m_ma)):
                    h_ = AH[:, lo:lo + 4, c2]
                    m = ac.act(h_, src[:, :, c2], ACT.Copy, got)
                    m = ve.tt(AL[:, lo:lo + 4, c2], src[:, :, c2], h_.bitcast(F32), ALU.subtract, m, got)
                m_parts.append(m)
                for _ in range(2):
                    W.pump()
            X2 = [R[:, 1024 * t:1024 * t + 1024] if t < 4 else R[:, 8192 + 1024 * t:9216 + 1024 * t] for t in range(8)]
            xd3 = xd.rearrange("p (t d) -> p t d", t=8)
            grow = C[:, 1152:2176]
            c_grow = cload(grow, bass_rows(a["norm_ffn_pre_2"], 128), *PH)
            m_xl = [cload(X2[t], xd3[:, t, :], m_parts, m_xs) for t in range(8)]
            six_banks()
            m_mx, m_c1, m_x2 = [], [], []

            def mix_first(t):
                Y = MX[:, t, :]
                ss, m = mean_sq(Y, m_mx[t])
                m = ve.stt(Y, Y, ss, GP, ALU.mult, ALU.mult, m, m_gp)
                m = po.tt(X2[t], X2[t], Y, ALU.add, m, m_xl[t])
                m_x2.append(spill(xd3[:, t, :], X2[t], m))
                return m

            def mix_norm(t):
                ss, m = mean_sq(X2[t], xa.marks[0][t])
                return ve.stt(MX[:, t, :], X2[t], ss, grow, ALU.mult, ALU.mult, m, c_grow)

            def mix_second(t):
                d, m = transposed_parts(MX[:, t, :], 8, t, xa.m1[t], allb, over=m_c1[t])
                m_tr.append(d)
                return m
            m_tr = []
            xa = Line((0, mix_first), (1, mix_norm), (3, mix_second))
            for c in range(2):
                us = W.take4()
                for t in range(8):
                    b, free = allb.next()
                    mk = gemm_tok(b, free, 512, t, us, [m_parts[t // 2]], t == 7)
                    bank_free[b] = ac.act(MX[:, t, 512 * c:512 * c + 512], Bk[b], ACT.Copy, mk, m_parts)
                    if c == 1:
                        m_mx.append(bank_free[b])
                        m_c1.append(mk)
                        xa.step()
            xa.step()
            m_gp = cload(GP, bass_rows(a["norm_ffn_post_2"], 128), xa.marks[0])
            FO = R[:, 8192:16384].rearrange("p (t d) -> p t d", t=8)
            ub = Ring([RR[:, 2048 * j:2048 * j + 2048] for j in range(4)])
            pe.wait(xa.m2[0:4])
            for q in (ve, ac, po):
                q.wait(m_x2[0:4], m_tr[0:4])
            rl = Ring([trig, grow[:, 0:512]])
            rl.free[1] = xa.m1[7]
            fm = [[None, None] for _ in range(8)]
            groups = []

            def up(g):
                us, ws = [], [W.take(), W.take()]
                evs = []
                for j in range(2):
                    ui, ubuf, uf = ub.next()
                    um = []

                    def relu2(s_, b, mk, ubuf=ubuf, uf=uf, um=um):
                        ri, rbuf, rf = rl.next()
                        hi = ubuf[:, 512 * s_:512 * s_ + 512]
                        lo = ubuf[:, 1024 + 512 * s_:1536 + 512 * s_]
                        m = ac.act(rbuf, Bk[b], ACT.Relu, mk, rf)
                        m1 = po.tt(rbuf, rbuf, rbuf, ALU.mult, m)
                        m2 = ac.act(hi, rbuf, ACT.Copy, m1, uf)
                        rl.free[ri] = m3 = ve.tt(lo, rbuf, hi.bitcast(F32), ALU.subtract, m2, uf)
                        um.append(m3)
                        return m
                    evs.append(relu2)
                    us.append((ui, ubuf, um))
                for s_ in range(2):
                    for j in range(2):
                        gemm_half(ws[j], 128, s_, evs[j], s_ == 1)
                        if g == 0 and s_ == 0:
                            xa.step()
                    if g == 0 and s_ == 0:
                        eight_banks()
                        pe.wait(xa.m2)
                groups.append(us)

            def down(g, done=None):
                us = groups[g]
                ws = [W.take(), W.take()]
                for t in range(8):
                    for c in range(2):
                        b, free = allb.next()
                        pe.wait(free)
                        for j in range(2):
                            ui, ubuf, um = us[j]
                            pe.wait(um, ws[j][3])
                            uh, ul = ubuf[:, 128 * t:128 * t + 128], ubuf[:, 1024 + 128 * t:1152 + 128 * t]
                            wh, wl = ws[j][1][:, 0, 512 * c:512 * c + 512], ws[j][2][:, 0, 512 * c:512 * c + 512]
                            pe.mm(Bk[b], uh, wh, j == 0, False)
                            pe.mm(Bk[b], uh, wl, False, False)
                            last = t == 7 and c == 1
                            mk = pe.mm(Bk[b], ul, wh, False, j == 1, inc=j == 1 or last)
                            if last:
                                W.done(ws[j], mk)
                                ub.free[ui] = mk
                        dst = FO[:, t, 512 * c:512 * c + 512]
                        if g == 0:
                            fm[t][c] = ve.copy(dst, Bk[b], mk, m_x2, m_tr)
                        else:
                            fm[t][c] = ve.tt(dst, Bk[b], dst, ALU.add, mk, fm[t][c])
                        bank_free[b] = fm[t][c]
                        if t % 2:
                            W.pump()
                    if done and t:
                        done(t - 1)
                if done:
                    done(7)

            X2 = [AF[:, 1024 * t:1024 * t + 1024] for t in range(8)]
            osrc = out.rearrange("b (t p) d -> p (b t) d", p=128)
            m_xl = []

            def finish(t):
                Y = FO[:, t, :]
                ss, m = mean_sq(Y, fm[t])
                m = ve.stt(Y, Y, ss, GP, ALU.mult, ALU.mult, m, m_gp)
                m = (po if t < 6 else ve).tt(X2[t], X2[t], Y, ALU.add, m, m_xl[t])
                odma.go(osrc[:, t, :], X2[t], m)

            for g in range(15):
                up(g)
                if g:
                    down(g - 1)
            up(15)
            m_xl += [cload(X2[t], xd3[:, t, :], pe.last, m_x2) for t in range(8)]
            down(14)
            six_banks()
            down(15, finish)

        plan1()
        plan2()
        block2(block1())
        finish_up(nc, queues)


def bass_rows(row, n):
    return row.to_broadcast([n, row.shape[1]])


def finish_up(nc, L):
    sp, po, pe, ve, ac = L["sp"], L["po"], L["pe"], L["ve"], L["ac"]
    sp.wait(*L["odma"].all())
    sp.wait(*L["cdma"].all())
    sp.wait(*L["wdma"].all())
    with nc.Block() as block:
        block.sync(sp.emit)
        block.gpsimd(po.emit)
        block.scalar(ac.emit)
        block.tensor(pe.emit)
        block.vector(ve.emit)


def kernel(**inputs):
    import concourse.bacc as bacc
    from concourse.bass_utils import run_bass_kernel_spmd

    nc = bacc.Bacc("TRN2", target_bir_lowering=False, num_devices=1)
    arrays = {n: np.ascontiguousarray(v) for n, v in inputs.items() if np.asarray(v).size}
    for n, v in constants().items():
        arrays["c_" + n] = v
    aps = {n: nc.dram_tensor(n, v.shape, mybir.dt.from_np(v.dtype), kind="ExternalInput").ap() for n, v in arrays.items()}
    out = nc.dram_tensor("out", (1, S, D), F32, kind="ExternalOutput").ap()
    program(nc, aps, out)
    r = run_bass_kernel_spmd(nc, [arrays], core_ids=[0])
    return r.results[0]["out"]
```
